# Optimizing a Trainium2 kernel written in Bass

```python
import math
import jax, jax.numpy as jnp
from jax import lax
import numpy as np

D_MODEL = 1024
BATCH = 1
SEQ = 256
DEPTH = 2

N_MIXERS = 3
RET_HEADS = 4
RET_QK_DIM = D_MODEL // RET_HEADS
RET_V_DIM = 2 * D_MODEL // RET_HEADS
RET_CHUNK = 256
S5_WIDTH = D_MODEL
S5_GROUP = 16
S5_GROUPS = S5_WIDTH // S5_GROUP
S5_STATE = 64
S5_CHUNK = 1024
S5_DT_MIN = 1e-3
S5_DT_MAX = 1e-1
MOBA_HEADS = 8
MOBA_HEAD_DIM = D_MODEL // MOBA_HEADS
MOBA_BLOCK = 256
MOBA_TOPK = 3
MOBA_Q_CHUNK = 32
D_FF = 3584
N_EXPERTS = 8
TOP_K = 2
MOE_BLOCK = 256
NORM_EPS = 1e-6
NEG_INF = -1e30

kernel_name = 'hybrid_retention_s5_moba_moe_trunk'

def _layer_counts(depth):
    n_ret = sum(1 for i in range(depth) if i % N_MIXERS == 0)
    n_s5 = sum(1 for i in range(depth) if i % N_MIXERS == 1)
    n_moba = sum(1 for i in range(depth) if i % N_MIXERS == 2)
    n_dense = sum(1 for i in range(depth) if i % 2 == 0)
    n_moe = depth - n_dense
    return n_ret, n_s5, n_moba, n_dense, n_moe

def _rmsnorm(x, gain):
    xf = x.astype(jnp.float32)
    y = xf * lax.rsqrt(jnp.mean(xf * xf, axis=-1, keepdims=True) + NORM_EPS)
    return (y * gain.astype(jnp.float32)).astype(x.dtype)

def _swiglu(h, w_gate, w_up, w_down):
    return (jax.nn.silu(h @ w_gate) * (h @ w_up)) @ w_down

def _retention(h, w_in, gn_gain, w_out):
    B, T, _ = h.shape
    H, dk, dv = RET_HEADS, RET_QK_DIM, RET_V_DIM
    C = math.gcd(T, RET_CHUNK)
    nC = T // C
    proj = h @ w_in
    q, k, v, g = jnp.split(proj, [D_MODEL, 2 * D_MODEL, 4 * D_MODEL], axis=-1)

    def heads(a, d):
        return a.reshape(B, nC, C, H, d).transpose(0, 3, 1, 2, 4).astype(jnp.float32)

    q = heads(q, dk)
    k = heads(k, dk) * (dk ** -0.5)
    v = heads(v, dv)
    log_gamma = jnp.log1p(-jnp.exp2(-5.0 - jnp.arange(H, dtype=jnp.float32)))
    idx = jnp.arange(C, dtype=jnp.float32)
    diff = idx[:, None] - idx[None, :]
    decay = jnp.where(diff >= 0, jnp.exp(log_gamma[:, None, None] * jnp.maximum(diff, 0.0)), 0.0)
    scores = jnp.einsum('bhncd,bhned->bhnce', q, k) * decay[:, None]
    y_intra = jnp.einsum('bhnce,bhnev->bhncv', scores, v)
    q_decay = jnp.exp(log_gamma[:, None] * (idx + 1.0))
    k_decay = jnp.exp(log_gamma[:, None] * (C - 1.0 - idx))
    chunk_decay = jnp.exp(log_gamma * C)

    def step(R, inp):
        qc, kc, vc = inp
        y = jnp.einsum('bhcd,bhdv->bhcv', qc, R) * q_decay[None, :, :, None]
        R = R * chunk_decay[None, :, None, None] + jnp.einsum(
            'bhcd,bhcv->bhdv', kc * k_decay[None, :, :, None], vc)
        return R, y

    R0 = jnp.zeros((B, H, dk, dv), jnp.float32)
    xs = (q.transpose(2, 0, 1, 3, 4), k.transpose(2, 0, 1, 3, 4), v.transpose(2, 0, 1, 3, 4))
    _, y_cross = lax.scan(step, R0, xs)
    y = y_intra + y_cross.transpose(1, 2, 0, 3, 4)
    mu = jnp.mean(y, axis=-1, keepdims=True)
    var = jnp.mean(jnp.square(y - mu), axis=-1, keepdims=True)
    y = (y - mu) * lax.rsqrt(var + NORM_EPS)
    y = y.transpose(0, 2, 3, 1, 4).reshape(B, T, H * dv) * gn_gain.astype(jnp.float32)
    y = y * jax.nn.silu(g.astype(jnp.float32))
    return y.astype(h.dtype) @ w_out

def _s5(h, w_in, a_re, a_im, log_step, b_re, b_im, c_re, c_im, d_skip, w_out):
    B, T, _ = h.shape
    G, P, N = S5_GROUPS, S5_STATE, S5_GROUP
    f32 = jnp.float32
    u = (h @ w_in).astype(f32)
    dt = jnp.exp(log_step.astype(f32))[:, None]
    ar, ai = a_re.astype(f32), a_im.astype(f32)
    mag = jnp.exp(ar * dt)
    abar_re = mag * jnp.cos(ai * dt)
    abar_im = mag * jnp.sin(ai * dt)
    den = ar * ar + ai * ai
    nr = abar_re - 1.0
    ni = abar_im
    f_re = (nr * ar + ni * ai) / den
    f_im = (ni * ar - nr * ai) / den
    br, bi = b_re.astype(f32), b_im.astype(f32)
    bbar_re = f_re[..., None] * br - f_im[..., None] * bi
    bbar_im = f_re[..., None] * bi + f_im[..., None] * br
    cr, ci = c_re.astype(f32), c_im.astype(f32)
    L = math.gcd(T, S5_CHUNK)
    nC = T // L
    u_chunks = u.reshape(B, nC, L, G, N).transpose(1, 2, 0, 3, 4)

    def combine(e1, e2):
        a1r, a1i, b1r, b1i = e1
        a2r, a2i, b2r, b2i = e2
        return (a2r * a1r - a2i * a1i, a2r * a1i + a2i * a1r,
                a2r * b1r - a2i * b1i + b2r, a2r * b1i + a2i * b1r + b2i)

    def step(carry, uc):
        sr, si = carry
        bu_re = jnp.einsum('lbgn,gpn->lbgp', uc, bbar_re)
        bu_im = jnp.einsum('lbgn,gpn->lbgp', uc, bbar_im)
        a_r = jnp.broadcast_to(abar_re[None, None], bu_re.shape)
        a_i = jnp.broadcast_to(abar_im[None, None], bu_re.shape)
        Ar, Ai, Hr, Hi = lax.associative_scan(combine, (a_r, a_i, bu_re, bu_im), axis=0)
        hr = Hr + Ar * sr - Ai * si
        hi = Hi + Ar * si + Ai * sr
        y = jnp.einsum('lbgp,gnp->lbgn', hr, cr) - jnp.einsum('lbgp,gnp->lbgn', hi, ci)
        return (hr[-1], hi[-1]), y

    s0 = (jnp.zeros((B, G, P), f32), jnp.zeros((B, G, P), f32))
    _, y = lax.scan(step, s0, u_chunks)
    y = y.transpose(2, 0, 1, 3, 4).reshape(B, T, S5_WIDTH) + d_skip.astype(f32) * u
    y = jax.nn.gelu(y)
    z = y.astype(h.dtype) @ w_out
    za, zb = jnp.split(z, 2, axis=-1)
    return za * jax.nn.sigmoid(zb)

def _moba(h, w_in, w_out):
    B, T, _ = h.shape
    H, hd, Bk = MOBA_HEADS, MOBA_HEAD_DIM, MOBA_BLOCK
    f32 = jnp.float32
    pad = (-T) % Bk
    Tp = T + pad
    nb = Tp // Bk
    K = max(1, min(MOBA_TOPK, nb - 1))
    q, k, v = jnp.split(h @ w_in, 3, axis=-1)

    def heads(a):
        a = jnp.pad(a, ((0, 0), (0, pad), (0, 0)))
        return a.reshape(B, Tp, H, hd).transpose(0, 2, 1, 3)

    q = heads(q) * (hd ** -0.5)
    k = heads(k)
    v = heads(v)
    k_blk = k.reshape(B, H, nb, Bk, hd)
    v_blk = v.reshape(B, H, nb, Bk, hd)
    k_mean = jnp.mean(k_blk.astype(f32), axis=3)
    slopes = jnp.exp2(-8.0 * (jnp.arange(H, dtype=f32) + 1.0) / H)
    kpos = jnp.arange(Bk)
    blk_ids = jnp.arange(nb)
    bidx = jnp.arange(B)[:, None, None, None]
    hidx = jnp.arange(H)[None, :, None, None]
    Qc = MOBA_Q_CHUNK

    def chunk(ci):
        t0 = ci * Qc
        qc = lax.dynamic_slice_in_dim(q, t0, Qc, axis=2)
        qpos = t0 + jnp.arange(Qc)
        own = t0 // Bk
        gate = jnp.einsum('bhqd,bhnd->bhqn', qc.astype(f32), k_mean)
        gate = jnp.where(blk_ids < own, gate, NEG_INF)
        _, sel = lax.top_k(gate, K)
        sel_valid = jnp.arange(K) < own
        k_sel = k_blk[bidx, hidx, sel]
        v_sel = v_blk[bidx, hidx, sel]
        pos_sel = sel[..., None] * Bk + kpos
        s_sel = jnp.einsum('bhqd,bhqkjd->bhqkj', qc, k_sel).astype(f32)
        s_sel = s_sel - slopes[None, :, None, None, None] * (qpos[:, None, None] - pos_sel).astype(f32)
        s_sel = jnp.where(sel_valid[:, None], s_sel, NEG_INF).reshape(B, H, Qc, K * Bk)
        k_own = lax.dynamic_slice_in_dim(k, own * Bk, Bk, axis=2)
        v_own = lax.dynamic_slice_in_dim(v, own * Bk, Bk, axis=2)
        own_pos = own * Bk + kpos
        dist = (qpos[:, None] - own_pos[None, :]).astype(f32)
        s_own = jnp.einsum('bhqd,bhjd->bhqj', qc, k_own).astype(f32) - slopes[:, None, None] * dist
        s_own = jnp.where(dist >= 0, s_own, NEG_INF)
        p = jax.nn.softmax(jnp.concatenate([s_own, s_sel], axis=-1), axis=-1)
        p_own = p[..., :Bk].astype(v.dtype)
        p_sel = p[..., Bk:].reshape(B, H, Qc, K, Bk).astype(v.dtype)
        return (jnp.einsum('bhqj,bhjd->bhqd', p_own, v_own)
                + jnp.einsum('bhqkj,bhqkjd->bhqd', p_sel, v_sel))

    o = lax.map(chunk, jnp.arange(Tp // Qc))
    o = o.transpose(1, 0, 3, 2, 4).reshape(B, Tp, H * hd)[:, :T]
    return o @ w_out

def _moe(h, router, w_gate, w_up, w_down):
    B, T, D = h.shape
    xf = h.reshape(-1, D)
    N = xf.shape[0]
    logits = (xf @ router).astype(jnp.float32)
    top_logits, top_idx = lax.top_k(logits, TOP_K)
    gates = jax.nn.softmax(top_logits, axis=-1)
    e_flat = top_idx.reshape(-1)
    tok_flat = jnp.arange(N * TOP_K, dtype=jnp.int32) // TOP_K
    g_flat = gates.reshape(-1)
    order = jnp.argsort(e_flat)
    e_sorted = e_flat[order]
    counts = jnp.bincount(e_flat, length=N_EXPERTS)
    padded = ((counts + MOE_BLOCK - 1) // MOE_BLOCK) * MOE_BLOCK
    start = jnp.cumsum(counts) - counts
    pend = jnp.cumsum(padded)
    pstart = pend - padded
    rank = jnp.arange(N * TOP_K, dtype=jnp.int32) - start[e_sorted]
    dest = pstart[e_sorted] + rank
    n_slots = (-(-(N * TOP_K) // MOE_BLOCK)) * MOE_BLOCK + N_EXPERTS * MOE_BLOCK
    n_blocks = n_slots // MOE_BLOCK
    slot_tok = jnp.full((n_slots,), N, jnp.int32).at[dest].set(tok_flat[order])
    slot_gate = jnp.zeros((n_slots,), jnp.float32).at[dest].set(g_flat[order])
    block_e = jnp.minimum(
        jnp.searchsorted(pend, jnp.arange(n_blocks) * MOE_BLOCK, side='right'), N_EXPERTS - 1)
    x_pad = jnp.concatenate([xf, jnp.zeros((1, D), xf.dtype)], axis=0)

    def run_block(args):
        tok, e = args
        xb = x_pad[tok]
        return _swiglu(xb, w_gate[e], w_up[e], w_down[e])

    y = lax.map(run_block, (slot_tok.reshape(n_blocks, MOE_BLOCK), block_e))
    y = y.reshape(n_slots, D) * slot_gate[:, None].astype(y.dtype)
    out = jax.ops.segment_sum(y, slot_tok, num_segments=N + 1)[:N]
    return out.reshape(B, T, D)

def setup_inputs(seed: int = 0) -> dict:
    key = jax.random.key(seed)
    ks = iter(jax.random.split(key, 32))
    f32 = jnp.float32

    def nrm(shape, scale):
        return jax.random.normal(next(ks), shape, f32) * scale

    D, F, E = D_MODEL, D_FF, N_EXPERTS
    G, P, N = S5_GROUPS, S5_STATE, S5_GROUP
    NR, NS, NM, ND, NE = _layer_counts(DEPTH)
    out_scale = (2.0 * DEPTH) ** -0.5
    x = nrm((BATCH, SEQ, D), 1.0)
    norm_mix = 1.0 + nrm((DEPTH, D), 0.02)
    norm_ffn = 1.0 + nrm((DEPTH, D), 0.02)
    norm_final = 1.0 + nrm((D,), 0.02)
    ret_w_in = nrm((NR, D, 6 * D), D ** -0.5)
    ret_gn = 1.0 + nrm((NR, 2 * D), 0.02)
    ret_w_out = nrm((NR, 2 * D, D), (2 * D) ** -0.5 * out_scale)
    s5_w_in = nrm((NS, D, S5_WIDTH), D ** -0.5)
    s5_a_re = -0.5 * jnp.exp(nrm((NS, G, P), 0.05))
    s5_a_im = math.pi * jnp.arange(P, dtype=f32) + nrm((NS, G, P), 0.01)
    s5_log_step = math.log(S5_DT_MIN) + jax.random.uniform(next(ks), (NS, G), f32) * (
        math.log(S5_DT_MAX) - math.log(S5_DT_MIN))
    s5_b_re = nrm((NS, G, P, N), (2 * N) ** -0.5)
    s5_b_im = nrm((NS, G, P, N), (2 * N) ** -0.5)
    s5_c_re = nrm((NS, G, N, P), (2 * P) ** -0.5)
    s5_c_im = nrm((NS, G, N, P), (2 * P) ** -0.5)
    s5_d = nrm((NS, S5_WIDTH), 1.0)
    s5_w_out = nrm((NS, S5_WIDTH, 2 * D), S5_WIDTH ** -0.5 * out_scale)
    moba_w_in = nrm((NM, D, 3 * D), D ** -0.5)
    moba_w_out = nrm((NM, D, D), D ** -0.5 * out_scale)
    ffn_w_gate = nrm((ND, D, F), D ** -0.5)
    ffn_w_up = nrm((ND, D, F), D ** -0.5)
    ffn_w_down = nrm((ND, F, D), F ** -0.5 * out_scale)
    moe_router = nrm((NE, D, E), D ** -0.5)
    moe_w_gate = nrm((NE, E, D, F), D ** -0.5)
    moe_w_up = nrm((NE, E, D, F), D ** -0.5)
    moe_w_down = nrm((NE, E, F, D), F ** -0.5 * out_scale)
    return {'x': x, 'norm_mix': norm_mix, 'norm_ffn': norm_ffn, 'norm_final': norm_final,
            'ret_w_in': ret_w_in, 'ret_gn': ret_gn, 'ret_w_out': ret_w_out,
            's5_w_in': s5_w_in, 's5_a_re': s5_a_re, 's5_a_im': s5_a_im, 's5_log_step': s5_log_step,
            's5_b_re': s5_b_re, 's5_b_im': s5_b_im, 's5_c_re': s5_c_re, 's5_c_im': s5_c_im,
            's5_d': s5_d, 's5_w_out': s5_w_out,
            'moba_w_in': moba_w_in, 'moba_w_out': moba_w_out,
            'ffn_w_gate': ffn_w_gate, 'ffn_w_up': ffn_w_up, 'ffn_w_down': ffn_w_down,
            'moe_router': moe_router, 'moe_w_gate': moe_w_gate, 'moe_w_up': moe_w_up,
            'moe_w_down': moe_w_down}

def reference(x, norm_mix, norm_ffn, norm_final, ret_w_in, ret_gn, ret_w_out,
              s5_w_in, s5_a_re, s5_a_im, s5_log_step, s5_b_re, s5_b_im, s5_c_re, s5_c_im,
              s5_d, s5_w_out, moba_w_in, moba_w_out, ffn_w_gate, ffn_w_up, ffn_w_down,
              moe_router, moe_w_gate, moe_w_up, moe_w_down):
    h = x
    i_ret = i_s5 = i_moba = i_dense = i_moe = 0
    for i in range(DEPTH):
        hn = _rmsnorm(h, norm_mix[i])
        mixer = i % N_MIXERS
        if mixer == 0:
            mix = _retention(hn, ret_w_in[i_ret], ret_gn[i_ret], ret_w_out[i_ret])
            i_ret += 1
        elif mixer == 1:
            mix = _s5(hn, s5_w_in[i_s5], s5_a_re[i_s5], s5_a_im[i_s5], s5_log_step[i_s5],
                      s5_b_re[i_s5], s5_b_im[i_s5], s5_c_re[i_s5], s5_c_im[i_s5],
                      s5_d[i_s5], s5_w_out[i_s5])
            i_s5 += 1
        else:
            mix = _moba(hn, moba_w_in[i_moba], moba_w_out[i_moba])
            i_moba += 1
        h = h + mix.astype(h.dtype)
        hn = _rmsnorm(h, norm_ffn[i])
        if i % 2 == 0:
            ffn = _swiglu(hn, ffn_w_gate[i_dense], ffn_w_up[i_dense], ffn_w_down[i_dense])
            i_dense += 1
        else:
            ffn = _moe(hn, moe_router[i_moe], moe_w_gate[i_moe], moe_w_up[i_moe], moe_w_down[i_moe])
            i_moe += 1
        h = h + ffn.astype(h.dtype)
    return _rmsnorm(h, norm_final)


_drawn_inputs = setup_inputs


def setup_inputs(seed=0):
    import zlib

    import numpy as np

    out = dict(_drawn_inputs(seed))
    spreads = {}
    factors = {'norm_mix': 2.681,
     'norm_final': 9.051,
     'ret_gn': 17.674,
     's5_a_re': 64.0,
     's5_a_im': 29.904,
     's5_log_step': 51.904,
     's5_b_re': 27.92,
     's5_b_im': 29.12,
     's5_c_re': 43.76,
     's5_c_im': 51.472,
     'norm_ffn': 8.0}
    for name, (base, spread) in spreads.items():
        noise = np.random.default_rng([zlib.crc32(name.encode()), seed]).standard_normal(out[name].shape)
        drawn = base * np.exp(spread * noise) if base else spread * noise
        out[name] = __import__('jax').numpy.asarray(drawn.astype(out[name].dtype))
    for name, factor in factors.items():
        out[name] = (out[name] * factor).astype(out[name].dtype)
    return out
```

```python
import math
from contextlib import ExitStack

import numpy as np

import concourse.bass as bass
from concourse import mybir

F32 = mybir.dt.float32
F32R = mybir.dt.float32r
I32 = mybir.dt.int32
ALU = mybir.AluOpType
ACT = mybir.ActivationFunctionType
AX_X = mybir.AxisListType.X

P = 128
D = 1024
SEQ = 256
TT = SEQ // P
KT = D // P
EPS = 1e-6

HEADS = 4
DK = D // HEADS
DV = 2 * D // HEADS

GROUPS, STATES, GROUP_W = 64, 64, 16
PAIRS = GROUPS // 2
S5_BLOCK = 32
S5_BLOCKS = SEQ // S5_BLOCK

FF = 3584
FC = 512
STEPS = FF // FC
FT = FC // P
EXPERTS = 8
SLOTS = P

UNIT = 2048
RAW = 6
SPLIT = 3
FFN_UNITS = 6 * STEPS

RET_U0 = 0
RET_UNITS = 8 * HEADS
FFN_U0 = RET_U0 + RET_UNITS
S5_U0 = FFN_U0 + FFN_UNITS
S5_IN_UNITS, S5_OUT_UNITS = 4, 8
MOE_U0 = S5_U0 + S5_IN_UNITS + S5_OUT_UNITS

C_DECAY = 0
C_IDENT = C_DECAY + HEADS * SEQ
C_IOTA = C_IDENT + P
C_TRI = C_IOTA + P
C_ONES = C_TRI + P
C_EVEN = C_ONES + P
C_ODD = C_EVEN + 1
C_EPS = C_ODD + 1
C_COLS = C_EPS + 2

TWO_PI = 2 * math.pi
PI_1 = 6.28125
PI_2 = float(np.float32(round((TWO_PI - PI_1) * 2 ** 21) / 2 ** 21))
PI_3 = TWO_PI - PI_1 - PI_2
ROUND = 1.5 * 2 ** 23
PI_F32 = 3.1415925


def constants():
    c = np.zeros((P, C_COLS), np.float32)
    key = np.arange(P)[:, None].astype(np.float64)
    query = np.arange(SEQ)[None, :].astype(np.float64)
    for h in range(HEADS):
        log_gamma = np.log1p(-np.exp2(-5.0 - h))
        decay = np.where(query >= key, np.exp(log_gamma * np.maximum(query - key, 0)), 0)
        c[:, C_DECAY + h * SEQ:C_DECAY + (h + 1) * SEQ] = decay * DK ** -0.5
    c[:, C_IDENT:C_IDENT + P] = np.eye(P)
    c[:, C_IOTA:C_IOTA + P] = np.arange(P)[None, :]
    c[:, C_TRI:C_TRI + P] = np.arange(P)[:, None] < np.arange(P)[None, :]
    c[:, C_ONES:C_ONES + P] = 1
    odd = (np.arange(P) // GROUP_W) % 2
    c[:, C_EVEN], c[:, C_ODD] = 1 - odd, odd
    c[:, C_EPS] = EPS
    return c


def ret_first(h):
    return 0 if h == 0 else 8 * h - 2


def ffn_first(s):
    return 0 if s == 0 else 6 * s - 2


def state_at(m):
    return m % 4 * (PAIRS // 4) + m // 4


def trunk(nc, A, consts, out):
    with ExitStack() as ctx:
        def sem(name):
            return ctx.enter_context(nc.semaphore(name))

        base = 16512

        def place(name, shape, dt, offset):
            return nc.alloc_sbuf_tensor_at(name, [P, *shape], dt, offset=base + offset)

        raw = place("weights_raw", [RAW, UNIT], F32, 0)
        w_hi = place("weights_hi", [SPLIT, UNIT], F32R, 49152)
        w_lo = place("weights_lo", [SPLIT, UNIT], F32R, 73728)
        cst = place("constants", [C_COLS], F32, 98304)
        SMALL = 98304 + 6208
        H_OFF = SMALL + 4096
        resid = place("residual", [TT, D], F32, H_OFF)
        hn = place("normed_rows", [TT, D], F32, H_OFF + 8192)
        xt_hi = place("x_transposed_hi", [KT, SEQ], F32R, H_OFF + 16384)
        xt_lo = place("x_transposed_lo", [KT, SEQ], F32R, H_OFF + 24576)
        K_OFF = H_OFF + 32768
        bb_re = place("b_rows_re", [PAIRS, 2 * GROUP_W], F32, K_OFF)
        bb_im = place("b_rows_im", [PAIRS, 2 * GROUP_W], F32, K_OFF + 4096)
        cc_re = place("c_rows_re", [KT, P], F32, K_OFF + 8192)
        cc_im = place("c_rows_im", [KT, P], F32, K_OFF + 12288)
        cos_t = place("cos_table", [PAIRS, S5_BLOCK], F32, K_OFF + 16384)
        sin_t = place("sin_table", [PAIRS, S5_BLOCK], F32, K_OFF + 20480)
        mag_t = place("magnitude_table", [PAIRS, S5_BLOCK], F32, K_OFF + 24576)
        W_OFF = K_OFF + 28672
        ht_hi = [place(f"act_transposed_hi{b}", [TT, FT, P], F32R, W_OFF + 4096 * b) for b in range(2)]
        ht_lo = [place(f"act_transposed_lo{b}", [TT, FT, P], F32R, W_OFF + 8192 + 4096 * b) for b in range(2)]
        gated = place("silu_of_gate", [TT, FC], F32, W_OFF + 16384)
        act_rows = place("act_rows", [TT, FC], F32, W_OFF + 20480)
        qk_t = place("q_and_k_transposed", [2, 2, SEQ], F32, W_OFF + 24576)
        v_rows = place("v_rows", [TT, DV], F32, W_OFF + 28672)
        gain_rows = place("gain_rows", [P], F32, W_OFF + 28672)
        scores = place("scores_transposed", [384], F32, W_OFF + 32768)
        T_OFF = W_OFF + 34304
        tmp1 = place("setup_tmp1", [PAIRS, GROUP_W], F32, T_OFF)
        tmp2 = place("setup_tmp2", [PAIRS, GROUP_W], F32, T_OFF + 2048)
        b_re = place("b_re", [PAIRS, GROUP_W], F32, W_OFF + 4096)
        b_im = place("b_im", [PAIRS, GROUP_W], F32, W_OFF + 4096 + 2048)
        c_re = place("c_re", [KT, STATES], F32, W_OFF + 12288)
        c_im = place("c_im", [KT, STATES], F32, W_OFF + 12288 + 2048)
        log_step = place("log_step", [2], F32, T_OFF + 4096)
        dt = place("dt", [2], F32, T_OFF + 4128)
        par_in = place("params_by_pair", [5, P], F32, T_OFF + 4160)
        a_re = place("a_re", [P], F32, T_OFF)
        a_im = place("a_im", [P], F32, T_OFF + 512)
        p1 = place("param_tmp1", [P], F32, T_OFF + 1024)
        p2 = place("param_tmp2", [P], F32, T_OFF + 1536)
        p3 = place("param_tmp3", [P], F32, T_OFF + 2048)
        p4 = place("param_tmp4", [P], F32, T_OFF + 2560)
        p5 = place("param_tmp5", [P], F32, T_OFF + 3072)
        p6 = place("param_tmp6", [P], F32, T_OFF + 3584)
        u_t = place("u_transposed", [KT, SEQ], F32, H_OFF + 8192)
        y_t = place("y_transposed", [KT, SEQ], F32, H_OFF + 16384)
        bt_re = place("b_transposed_re", [KT, P], F32, W_OFF)
        bt_im = place("b_transposed_im", [KT, P], F32, W_OFF + 4096)
        ct_re = place("c_transposed_re", [KT, P], F32, W_OFF + 8192)
        ct_im = place("c_transposed_im", [KT, P], F32, W_OFF + 12288)
        s_re = place("scan_re", [PAIRS, S5_BLOCK], F32, W_OFF + 16384)
        s_im = place("scan_im", [PAIRS, S5_BLOCK], F32, W_OFF + 20480)
        s_tmp = place("scan_tmp", [PAIRS, S5_BLOCK], F32, W_OFF + 24576)
        st_re = place("state_re", [PAIRS, S5_BLOCK], F32, W_OFF + 28672)
        st_im = place("state_im", [PAIRS, S5_BLOCK], F32, W_OFF + 32768)
        gelu_t = place("gelu_transposed", [KT, SEQ], F32, W_OFF + 16384)
        glu_gate = place("glu_gate", [TT, 512], F32, W_OFF + 24576)
        glu_out = place("glu_out", [TT, 512], F32, W_OFF + 28672)
        gain_row = place("ffn_gain_row", [D], F32, K_OFF)
        hn_t = place("normed_transposed", [KT, SEQ], F32, K_OFF + 4096)
        xg_hi = place("gathered_hi", [KT, SLOTS], F32R, K_OFF + 12288)
        xg_lo = place("gathered_lo", [KT, SLOTS], F32R, K_OFF + 16384)
        y_rows = place("expert_rows", [D], F32, K_OFF + 20480)
        pick = place("pick", [TT, SLOTS], F32, K_OFF + 24576)
        pick_g = place("pick_gated", [TT, SLOTS], F32, K_OFF + 25600)
        put_g = place("put_gated", [TT, P], F32, K_OFF + 26624)
        final_gain = place("final_gain_row", [D], F32, H_OFF + 16384)

        small_at = [SMALL]

        def small(name, shape, dt=F32):
            size = -(-4 * math.prod(shape) // 32) * 32
            small_at[0] += size
            assert small_at[0] <= H_OFF
            return place(name, shape, dt, small_at[0] - size)

        gains = small("gains", [7 * KT])
        g_gn = gains[:, 4 * KT:6 * KT]
        d_skip = gains[:, 6 * KT:7 * KT]
        ssq = small("sum_of_squares", [TT])
        std = small("std", [TT])
        rstd = small("rstd", [TT])
        bn_s = small("bn_stats", [TT, 6])
        bn_a = small("bn_mean_var", [TT, 2])
        hstd = small("head_std", [TT])
        hrstd = small("head_rstd", [TT])
        par = small("params", [5, PAIRS])
        ab_re = small("abar_re", [PAIRS])
        ab_im = small("abar_im", [PAIRS])
        pw_re = small("power_re", [PAIRS])
        pw_im = small("power_im", [PAIRS])
        pw_t = small("power_tmp", [2, PAIRS])
        car = small("carry", [4, PAIRS])
        router = small("router", [KT, EXPERTS])
        logit = small("logits", [TT, EXPERTS])
        top = small("top", [TT, 8])
        r_gt = small("is_above_second", [TT, EXPERTS])
        r_eq = small("is_second", [TT, EXPERTS])
        r_cum = small("count_of_second", [TT, EXPERTS])
        r_n = small("n_above", [TT])
        chosen = small("chosen", [TT, EXPERTS])
        r_exp = small("exp", [TT, EXPERTS])
        neg_top = small("neg_top", [TT])
        gate_w = small("gate_weight", [TT, EXPERTS])
        key = [small(f"slot_key{b}", [TT, EXPERTS + 1]) for b in range(2)]
        most = small("largest_count", [1])
        over = small("over", [1], I32)

        PS = ctx.enter_context(nc.psum_tensor("PS", [P, 8, 512], F32))

        ident = cst[:, C_IDENT:C_IDENT + P]
        iota = cst[:, C_IOTA:C_IOTA + P]
        tri = cst[:, C_TRI:C_TRI + P]
        ones = cst[:, C_ONES:C_ONES + P]
        eps = cst[:, C_EPS:C_EPS + 1]

        def gate_banks(tts):
            return list(range(tts))

        def up_banks(tts):
            return list(range(tts, 2 * tts))

        def out_bank(tt, dh):
            return 4 + 2 * tt + dh

        landed = [sem(f"raw_landed{i}") for i in range(RAW)]
        hi_ready = sem("weights_hi_ready")
        lo_ready = sem("weights_lo_ready")
        used = sem("units_used")
        x_landed = sem("x_landed")
        c_landed = sem("constants_landed")
        g_landed = sem("gains_landed")
        gains_t = sem("gains_transposed")
        gains_ready = sem("gains_ready")
        a_landed = sem("s5_a_landed")
        bc_landed = sem("s5_bc_landed")
        moe_landed = sem("moe_params_landed")
        fin_landed = sem("final_gain_landed")
        resid_ready = sem("residual_ready")
        ssq0_done = sem("ssq0_done")
        ssq1_done = sem("ssq1_done")
        std_done = sem("std_done")
        rstd_done = sem("rstd_done")
        hn0_ready = sem("normed0_ready")
        hn1_ready = sem("normed1_ready")
        xt_done = sem("x_transposed")
        xhi_ready = sem("x_hi_ready")
        xlo_ready = sem("x_lo_ready")
        qk_copied = sem("q_k_copied")
        v_copied = sem("v_copied")
        g_silu = sem("g_silu_done")
        scores_done = sem("scores_done")
        decayed = sem("scores_decayed")
        y_done = sem("retention_y_done")
        bn_done = sem("bn_done")
        hstd_done = sem("head_std_done")
        y_normed = sem("y_normed")
        yt_done = sem("y_transposed_done")
        yt_hi = sem("y_transposed_hi")
        yt_lo = sem("y_transposed_lo")
        silu_done = sem("silu_done")
        mult_done = sem("act_rows_done")
        act_t_done = sem("act_transposed")
        act_hi = sem("act_hi_ready")
        act_lo = sem("act_lo_ready")
        dt_done = sem("dt_done")
        ar_done = sem("a_times_dt_done")
        mag_done = sem("mag_done")
        angle_done = sem("angle_done")
        sin_done = sem("sin_done")
        den_done = sem("den_done")
        rden_done = sem("rden_done")
        par_done = sem("params_done")
        par_t = sem("params_transposed")
        par_ready = sem("params_ready")
        setup_done = sem("s5_setup_done")
        bt_done = sem("b_transposed_done")
        bt_copied = sem("b_copied")
        ct_done = sem("c_transposed_done")
        ct_copied = sem("c_copied")
        u_copied = sem("u_copied")
        du_done = sem("d_times_u_done")
        bu_done = sem("bu_done")
        bu_read = sem("bu_read")
        st_ready = sem("states_ready")
        sy_done = sem("s5_y_done")
        sy_added = sem("s5_y_added")
        gelu_done = sem("gelu_done")
        glu_sig = sem("glu_sigmoid_done")
        glu_read = sem("glu_gate_read")
        hnt_done = sem("normed_transposed_done")
        hnt_copied = sem("normed_transposed_copied")
        logits_done = sem("logits_done")
        top_done = sem("top_done")
        exp_done = sem("exp_done")
        chosen_done = sem("chosen_done")
        rank_done = sem("rank_done")
        keys_done = sem("keys_done")
        pick_ready = sem("pick_ready")
        pick_g_ready = sem("pick_gated_ready")
        gathered = sem("gathered")
        xg_hi_ready = sem("gathered_hi_ready")
        xg_lo_ready = sem("gathered_lo_ready")
        put_t_done = sem("put_transposed")
        put_ready = sem("put_ready")
        y0_copied = sem("expert_rows0_copied")
        y1_copied = sem("expert_rows1_copied")
        scattered = sem("scattered")
        scatter_added = sem("scatter_added")
        out_ready = sem("out_ready")
        stored = sem("output_stored")
        dve_self = sem("vector_self")
        act_self = sem("scalar_self")
        pool_self = sem("gpsimd_self")

        def count(static, e=None, per=0):
            return static if e is None else e * per + static

        def ffn_sources(w_gate, w_up, w_down):
            units = []
            for s in range(STEPS + 1):
                if s < STEPS:
                    for w in (w_gate, w_up):
                        for half in range(2):
                            units.append((4, w[half * 512:half * 512 + 512, s * FC:(s + 1) * FC]))
                if s > 0:
                    for half in range(2):
                        r = (s - 1) * FC + half * 256
                        units.append((2, w_down[r:r + 256, :]))
            return units

        def static_sources():
            w_in, w_out = A["ret_w_in"][0], A["ret_w_out"][0]
            units = []

            def head_out(h):
                return [(2, w_out[h * DV + a:h * DV + a + 256, :]) for a in (0, 256)]
            for h in range(HEADS):
                units.append((8, w_in[:, h * DK:(h + 1) * DK]))
                units.append((8, w_in[:, D + h * DK:D + (h + 1) * DK]))
                for c0 in (2 * D + h * DV, 4 * D + h * DV):
                    units += [(4, w_in[a:a + 512, c0:c0 + DV]) for a in (0, 512)]
                if h:
                    units += head_out(h - 1)
            units += head_out(HEADS - 1)
            units += ffn_sources(A["ffn_w_gate"][0], A["ffn_w_up"][0], A["ffn_w_down"][0])
            s_in, s_out = A["s5_w_in"][0], A["s5_w_out"][0]
            units += [(8, s_in[:, c * 256:(c + 1) * 256]) for c in range(4)]
            for dh in range(2):
                for c0 in (dh * 512, D + dh * 512):
                    units += [(4, s_out[a:a + 512, c0:c0 + 512]) for a in (0, 512)]
            assert len(units) == MOE_U0
            return units

        block = ctx.enter_context(nc.Block())

        @block.sync
        def _(sp):
            sp.dma_start(resid[:, :, :], A["x"][0].rearrange("(t p) d -> p t d", p=P)).then_inc(x_landed, 16)

            def load(n, kt, src, e=None):
                if n >= RAW:
                    sp.wait_ge(lo_ready, count(n - RAW + 1, e, FFN_UNITS))
                sp.dma_start(raw[:, n % RAW, :].rearrange("p (k n) -> p k n", k=kt),
                             src.rearrange("(k p) n -> p k n", p=P)).then_inc(landed[n % RAW], 16)

            for n, (kt, src) in enumerate(static_sources()):
                load(n, kt, src)

            def experts(u0):
                with sp.Fori(0, EXPERTS) as e:
                    for i, (kt, src) in enumerate(ffn_sources(
                            A["moe_w_gate"][0, e], A["moe_w_up"][0, e], A["moe_w_down"][0, e])):
                        load(u0 + i, kt, src, e)

            experts(MOE_U0)
            sp.wait_ge(keys_done, 1)
            flag = sp.value_load(over[0:1, 0:1], min_val=0, max_val=1)
            with sp.If(flag > 0):
                experts(MOE_U0 + EXPERTS * FFN_UNITS)
            sp.wait_ge(out_ready, 1)
            sp.dma_start(out[0].rearrange("(t p) d -> p t d", p=P), hn[:, :, :]).then_inc(stored, 16)
            sp.wait_ge(stored, 16)

        @block.gpsimd
        def _(pool):
            n_self = [0]

            def link(ins):
                n_self[0] += 1
                ins.then_inc(pool_self, 1)
                pool.wait_ge(pool_self, n_self[0])

            def tt(o, a, b, op):
                link(nc.gpsimd.tensor_tensor(o, a, b, op))

            def ts(o, a, x, y, op0, op1):
                link(nc.gpsimd.tensor_scalar(o, a, x, y, op0, op1))

            q = slice(0, PAIRS)
            pool.dma_start(log_step[q, :], A["s5_log_step"][0].rearrange("(m g) -> m g", g=2)).then_inc(a_landed, 16)
            pool.dma_start(a_re[q, :], A["s5_a_re"][0].rearrange("(m g) p -> m (g p)", g=2)).then_inc(a_landed, 16)
            pool.dma_start(a_im[q, :], A["s5_a_im"][0].rearrange("(m g) p -> m (g p)", g=2)).then_inc(a_landed, 16)
            for dst, name in ((b_re, "s5_b_re"), (b_im, "s5_b_im")):
                pool.dma_start(dst[:, :, :], A[name][0].rearrange("(m g) p n -> (g p) m n", g=2)).then_inc(bc_landed, 16)
            for dst, name in ((c_re, "s5_c_re"), (c_im, "s5_c_im")):
                pool.dma_start(dst[:, :, :], A[name][0].rearrange("(t g) n p -> (g n) t p", g=8)).then_inc(bc_landed, 16)

            pool.wait_ge(a_landed, 48)
            pool.wait_ge(dt_done, 1)
            halves = lambda x: x[q, :].rearrange("m (g p) -> m g p", g=2)
            dt_b = dt[q, :].unsqueeze(2).to_broadcast([PAIRS, 2, STATES])
            nc.gpsimd.tensor_tensor(halves(p1), halves(a_re), dt_b, ALU.mult).then_inc(ar_done, 1)
            tt(halves(p2), halves(a_im), dt_b, ALU.mult)
            ts(p3[q, :], p2[q, :], 1 / TWO_PI, ROUND, ALU.mult, ALU.add)
            ts(p3[q, :], p3[q, :], ROUND, None, ALU.subtract, ALU.bypass)
            for part in (PI_1, PI_2, PI_3):
                ts(p4[q, :], p3[q, :], part, None, ALU.mult, ALU.bypass)
                tt(p2[q, :], p2[q, :], p4[q, :], ALU.subtract)
            nc.gpsimd.tensor_scalar(p2[q, :], p2[q, :], PI_F32, -PI_F32, ALU.min, ALU.max).then_inc(angle_done, 1)
            tt(p4[q, :], a_re[q, :], a_re[q, :], ALU.mult)
            tt(p5[q, :], a_im[q, :], a_im[q, :], ALU.mult)
            nc.gpsimd.tensor_tensor(p4[q, :], p4[q, :], p5[q, :], ALU.add).then_inc(den_done, 1)
            pool.wait_ge(sin_done, 2)
            pool.wait_ge(den_done, 1)
            pool.wait_ge(mag_done, 1)
            mag, cos, sin, f_re, f_im = (par_in[q, i, :] for i in range(5))
            tt(p5[q, :], cos, cos, ALU.mult)
            ts(cos, p5[q, :], -2.0, 1.0, ALU.mult, ALU.add)
            tt(p1[q, :], mag, cos, ALU.mult)
            ts(p1[q, :], p1[q, :], 1.0, None, ALU.subtract, ALU.bypass)
            tt(p2[q, :], mag, sin, ALU.mult)
            pool.wait_ge(rden_done, 1)
            tt(p3[q, :], p1[q, :], a_re[q, :], ALU.mult)
            tt(p5[q, :], p2[q, :], a_im[q, :], ALU.mult)
            tt(p3[q, :], p3[q, :], p5[q, :], ALU.add)
            tt(f_re, p3[q, :], p6[q, :], ALU.mult)
            tt(p3[q, :], p2[q, :], a_re[q, :], ALU.mult)
            tt(p5[q, :], p1[q, :], a_im[q, :], ALU.mult)
            tt(p3[q, :], p3[q, :], p5[q, :], ALU.subtract)
            nc.gpsimd.tensor_tensor(f_im, p3[q, :], p6[q, :], ALU.mult).then_inc(par_done, 1)

            pool.wait_ge(par_ready, 1)
            mag, cos, sin, f_re, f_im = (par[:, i, :] for i in range(5))
            tt(ab_re[:, :], mag, cos, ALU.mult)
            tt(ab_im[:, :], mag, sin, ALU.mult)
            link(nc.gpsimd.tensor_copy(mag_t[:, :, :], mag.unsqueeze(2).to_broadcast([P, PAIRS, S5_BLOCK])))
            link(nc.gpsimd.memset(mag_t[:, :, 0:1], 0.0))
            link(nc.gpsimd.memset(cos_t[:, :, 0:1], 1.0))
            link(nc.gpsimd.memset(sin_t[:, :, 0:1], 0.0))
            link(nc.gpsimd.tensor_copy(cos_t[:, :, 1:2], cos.unsqueeze(2)))
            link(nc.gpsimd.tensor_copy(sin_t[:, :, 1:2], sin.unsqueeze(2)))
            link(nc.gpsimd.tensor_copy(pw_re[:, :], cos))
            link(nc.gpsimd.tensor_copy(pw_im[:, :], sin))
            n = 2
            while n < S5_BLOCK:
                tt(pw_t[:, 0, :], pw_re[:, :], pw_re[:, :], ALU.mult)
                tt(pw_t[:, 1, :], pw_im[:, :], pw_im[:, :], ALU.mult)
                tt(pw_im[:, :], pw_im[:, :], pw_re[:, :], ALU.mult)
                ts(pw_im[:, :], pw_im[:, :], 2.0, None, ALU.mult, ALU.bypass)
                tt(pw_re[:, :], pw_t[:, 0, :], pw_t[:, 1, :], ALU.subtract)
                wr = pw_re[:, :].unsqueeze(2).to_broadcast([P, PAIRS, n])
                wi = pw_im[:, :].unsqueeze(2).to_broadcast([P, PAIRS, n])
                t1, t2 = tmp1[:, :, 0:n], tmp2[:, :, 0:n]
                tt(t1, cos_t[:, :, 0:n], wr, ALU.mult)
                tt(t2, sin_t[:, :, 0:n], wi, ALU.mult)
                tt(cos_t[:, :, n:2 * n], t1, t2, ALU.subtract)
                tt(t1, cos_t[:, :, 0:n], wi, ALU.mult)
                tt(t2, sin_t[:, :, 0:n], wr, ALU.mult)
                tt(sin_t[:, :, n:2 * n], t1, t2, ALU.add)
                n *= 2
            pool.wait_ge(bc_landed, 64)
            def by_pair(f):
                return f.rearrange("p (i k) -> p k i", i=4).unsqueeze(3).to_broadcast([P, KT, 4, GROUP_W])

            def quads(x):
                return x[:, :, :].rearrange("p (k i) n -> p k i n", i=4)

            fr, fi = by_pair(f_re), by_pair(f_im)
            for dst, x, y, op in ((bb_re, b_re, b_im, ALU.subtract), (bb_im, b_im, b_re, ALU.add)):
                link(nc.gpsimd.memset(dst[:, :, :], 0.0))
                tt(quads(tmp1), quads(x), fr, ALU.mult)
                tt(quads(tmp2), quads(y), fi, ALU.mult)
                for g in range(2):
                    h = slice(STATES * g, STATES * (g + 1))
                    tt(dst[h, :, GROUP_W * g:GROUP_W * (g + 1)], tmp1[h, :, :], tmp2[h, :, :], op)
            pool.wait_ge(c_landed, 16)
            for dst, src, sign in ((cc_re, c_re, 1.0), (cc_im, c_im, -1.0)):
                for g, col in ((0, C_EVEN), (1, C_ODD)):
                    ts(dst[:, :, STATES * g:STATES * (g + 1)], src[:, :, :], cst[:, col:col + 1], sign, ALU.mult, ALU.mult)
            nc.gpsimd.memset(pw_t[:, :, :], 0.0).then_inc(setup_done, 1)

            pool.dma_start(router[:, :, :], A["moe_router"][0].rearrange("(k p) e -> p k e", p=P)).then_inc(moe_landed, 16)
            pool.wait_ge(bt_done, 1)
            pool.dma_start(gain_row[:, :], A["norm_ffn"][1:2, :].to_broadcast([P, D])).then_inc(moe_landed, 16)
            pool.wait_ge(used, MOE_U0)
            pool.dma_start(final_gain[:, :], A["norm_final"].unsqueeze(0).to_broadcast([P, D])).then_inc(fin_landed, 16)

        @block.scalar
        def _(act):
            n_self = [0]

            def link(ins):
                n_self[0] += 1
                ins.then_inc(act_self, 1)
                act.wait_ge(act_self, n_self[0])

            def copy(o, i):
                return nc.scalar.activation(o, i, ACT.Copy)

            act.dma_start(cst[:, :], consts).then_inc(c_landed, 16)
            act.dma_start(gain_rows[0:16, :], A["norm_mix"].rearrange("l (k p) -> (l k) p", p=P)).then_inc(g_landed, 16)
            act.dma_start(gain_rows[16:32, :], A["norm_ffn"].rearrange("l (k p) -> (l k) p", p=P)).then_inc(g_landed, 16)
            act.dma_start(gain_rows[32:48, :], A["ret_gn"][0].rearrange("(k p) -> k p", p=P)).then_inc(g_landed, 16)
            act.dma_start(gain_rows[48:56, :], A["s5_d"][0].rearrange("(k p) -> k p", p=P)).then_inc(g_landed, 16)

            def split_hi(n, e=None):
                act.wait_ge(landed[n % RAW], count(16 * (n // RAW + 1), e, 16 * (FFN_UNITS // RAW)))
                if n >= SPLIT:
                    act.wait_ge(used, count(n - SPLIT + 1, e, FFN_UNITS))
                copy(w_hi[:, n % SPLIT, :], raw[:, n % RAW, :]).then_inc(hi_ready, 1)

            def norm_rows(i):
                if i == 0:
                    act.wait_ge(x_landed, 16)
                    act.wait_ge(c_landed, 16)
                else:
                    act.wait_ge(resid_ready, i)
                nc.scalar.activation(hn[:, 0, :], resid[:, 0, :], ACT.Square, accum_out=ssq[:, 0:1]).then_inc(ssq0_done, 1)
                act.wait_ge(ssq0_done, i + 1)
                act.wait_ge(ssq1_done, i + 1)
                nc.scalar.activation(std[:, :], ssq[:, :], ACT.Sqrt, scale=1.0 / D, bias=eps).then_inc(std_done, 1)
                if i < 3:
                    act.wait_ge(rstd_done, i + 1)
                    nc.scalar.activation(hn[:, 1, :], resid[:, 1, :], ACT.Copy, scale=rstd[:, 1:2]).then_inc(hn1_ready, 1)

            def norm_split(i):
                gain = (gains[:, 0:KT], gains[:, 2 * KT:3 * KT], gains[:, KT:2 * KT])[i]
                act.wait_ge(gains_ready, 1)
                for bank in range(KT // 2):
                    act.wait_ge(xt_done, KT // 2 * i + bank + 1)
                    for j in range(2):
                        kt = 2 * bank + j
                        ins = nc.scalar.activation(xt_hi[:, kt, :], PS[:, bank, j * SEQ:(j + 1) * SEQ], ACT.Copy,
                                                   scale=gain[:, kt:kt + 1])
                    ins.then_inc(xhi_ready, 1)

            def ffn(u0, s0, tts, e=None, each=None):
                silu_at = {ffn_first(s) + 4: s for s in range(STEPS)}
                evac_at = {7 if s == 0 else 41 if s == STEPS - 1 else 6 * s + 6: s for s in range(STEPS)}
                for i in range(FFN_UNITS):
                    if i in silu_at:
                        s = s0 + silu_at[i]
                        act.wait_ge(used, count(u0 + ffn_first(silu_at[i]) + 2, e, FFN_UNITS))
                        if s:
                            act.wait_ge(mult_done, count(s, e, STEPS))
                        nc.scalar.activation(gated[:, 0:tts, :], PS[:, 0:tts, :], ACT.Silu).then_inc(silu_done, 1)
                    if i in evac_at:
                        s = s0 + evac_at[i]
                        act.wait_ge(act_t_done, count(s + 1, e, STEPS))
                        copy(ht_hi[evac_at[i] % 2][:, 0:tts, :, :],
                             PS[:, tts:2 * tts, :].rearrange("p t (f c) -> p t f c", f=FT)).then_inc(act_hi, 1)
                    if each:
                        each(i)
                    if e is None and i < 3:
                        continue
                    split_hi(u0 + i, e)

            norm_rows(0)
            act.wait_ge(gains_t, 1)
            copy(gains[:, :], PS[:, 7, 0:7 * KT]).then_inc(gains_ready, 1)
            act.wait_ge(a_landed, 48)
            q = slice(0, PAIRS)
            nc.scalar.activation(dt[q, :], log_step[q, :], ACT.Exp).then_inc(dt_done, 1)
            norm_split(0)
            split_hi(0)
            split_hi(1)

            def evac_yt(h):
                act.wait_ge(yt_done, h + 1)
                for ft in range(FT):
                    ins = nc.scalar.activation(ht_hi[0][:, :, ft, :], PS[:, 2:4, ft * P:(ft + 1) * P], ACT.Copy,
                                               scale=g_gn[:, h * FT + ft:h * FT + ft + 1])
                ins.then_inc(yt_hi, 1)

            for h in range(HEADS):
                f0 = ret_first(h)
                last = RET_UNITS if h == HEADS - 1 else ret_first(h + 1)
                for n in range(f0, last):
                    if n == 3:
                        act.wait_ge(ar_done, 1)
                        nc.scalar.activation(par_in[q, 0, :], p1[q, :], ACT.Exp).then_inc(mag_done, 1)
                        act.wait_ge(angle_done, 1)
                        nc.scalar.activation(par_in[q, 1, :], p2[q, :], ACT.Sin, scale=0.5).then_inc(sin_done, 1)
                        nc.scalar.activation(par_in[q, 2, :], p2[q, :], ACT.Sin).then_inc(sin_done, 1)
                    if h and n == f0 + 1:
                        act.wait_ge(bn_done, h)
                        nc.scalar.activation(hstd[:, :], bn_a[:, :, 1], ACT.Sqrt, bias=eps).then_inc(hstd_done, 1)
                    if h and n == f0 + 3:
                        evac_yt(h - 1)
                    if n == f0 + 4:
                        act.wait_ge(used, f0 + 2)
                        copy(qk_t[:, :, :, :], PS[:, 0:2, :].rearrange("p a (b c) -> p a b c", b=2)).then_inc(qk_copied, 1)
                    if h and n == f0:
                        act.wait_ge(used, ret_first(h - 1) + 6)
                        if h > 1:
                            act.wait_ge(y_normed, h - 1)
                        nc.scalar.activation(gated[:, :, :], PS[:, 0:2, :], ACT.Silu).then_inc(g_silu, 1)
                    if h == 1 and n == f0 + 2:
                        act.wait_ge(par_t, 1)
                        copy(par[:, :, :].rearrange("p a (i k) -> p a i k", i=4),
                             PS[:, 4, 0:5 * PAIRS].rearrange("p (a k i) -> p a i k", a=5, i=4)).then_inc(par_ready, 1)
                    if h == HEADS - 1 and n == f0 + 8:
                        act.wait_ge(used, f0 + 6)
                        act.wait_ge(y_normed, h)
                        nc.scalar.activation(gated[:, :, :], PS[:, 0:2, :], ACT.Silu).then_inc(g_silu, 1)
                    if h == HEADS - 1 and n == f0 + 9:
                        act.wait_ge(bn_done, HEADS)
                        nc.scalar.activation(hstd[:, :], bn_a[:, :, 1], ACT.Sqrt, bias=eps).then_inc(hstd_done, 1)
                    if n >= 2:
                        split_hi(n)
            evac_yt(HEADS - 1)

            for i in range(2):
                split_hi(FFN_U0 + i)
            norm_rows(1)
            norm_split(1)
            split_hi(FFN_U0 + 2)
            act.wait_ge(setup_done, 1)
            ffn(FFN_U0, 0, TT)

            for i in range(2):
                split_hi(S5_U0 + i)
            norm_rows(2)
            norm_split(2)
            for tables, done, copied in (((bt_re, bt_im), bt_done, bt_copied), ((ct_re, ct_im), ct_done, ct_copied)):
                act.wait_ge(done, 1)
                for j, t in enumerate(tables):
                    copy(t[:, :, :], PS[:, 4 + 2 * j:6 + 2 * j, :].rearrange("p a (b c) -> p (a b) c", c=P)).then_inc(copied, 1)
            for c in range(S5_IN_UNITS):
                split_hi(S5_U0 + 2 + c)
                act.wait_ge(used, S5_U0 + c + 1)
                copy(u_t[:, 2 * c:2 * c + 2, :], PS[:, c, :].rearrange("p (a b) -> p a b", a=2)).then_inc(u_copied, 1)
            split_hi(S5_U0 + 6)
            act.wait_ge(sy_added, S5_BLOCKS)
            for half in range(2):
                k = slice(4 * half, 4 * half + 4)
                nc.scalar.activation(gelu_t[:, k, :], y_t[:, k, :], ACT.Gelu_apprx_tanh).then_inc(gelu_done, 1)
                act.wait_ge(gelu_done, half + 1)
                copy(xt_hi[:, k, :], gelu_t[:, k, :]).then_inc(xhi_ready, 1)
            for n in range(7, S5_IN_UNITS + S5_OUT_UNITS):
                if n == 11:
                    act.wait_ge(used, S5_U0 + 8)
                    nc.scalar.activation(glu_gate[:, :, :], PS[:, 2:4, :], ACT.Sigmoid).then_inc(glu_sig, 1)
                split_hi(S5_U0 + n)
            act.wait_ge(used, MOE_U0)
            act.wait_ge(glu_read, 1)
            nc.scalar.activation(glu_gate[:, :, :], PS[:, 6:8, :], ACT.Sigmoid).then_inc(glu_sig, 1)

            norm_rows(3)
            act.wait_ge(hnt_done, 1)
            copy(hn_t[:, 0:4, :], PS[:, 0:2, :].rearrange("p a (b c) -> p (a b) c", c=SEQ)).then_inc(hnt_copied, 1)
            act.wait_ge(top_done, 1)
            for t in range(TT):
                nc.scalar.activation(r_exp[:, t, :], logit[:, t, :], ACT.Exp, bias=neg_top[:, t:t + 1]).then_inc(exp_done, 1)

            def gather_hi(g):
                act.wait_ge(gathered, g)
                copy(xg_hi[:, :, :], PS[:, 2:4, :].rearrange("p a (b c) -> p (a b) c", c=SLOTS)).then_inc(xg_hi_ready, 1)

            def experts(p):
                u0 = MOE_U0 + p * EXPERTS * FFN_UNITS
                gather_hi(9 * p + 1)
                with act.Fori(0, EXPERTS) as e:
                    def each(i):
                        if i == 2:
                            act.wait_ge(used, count(u0, e, FFN_UNITS))
                            copy(y_rows[:, 0:512], PS[:, 4, :]).then_inc(y0_copied, 1)
                        if i == 19:
                            act.wait_ge(put_t_done, count(8 * p + 1, e, 1))
                            copy(put_g[:, :, :], PS[:, 6, 0:2 * P].rearrange("p (a b) -> p a b", a=2)).then_inc(put_ready, 1)
                    ffn(u0, STEPS * (1 + EXPERTS * p), 1, e, each)
                    gather_hi(count(9 * p + 2, e, 1))
                act.wait_ge(used, u0 + EXPERTS * FFN_UNITS)
                copy(y_rows[:, 0:512], PS[:, 4, :]).then_inc(y0_copied, 1)

            experts(0)
            act.wait_ge(keys_done, 1)
            flag = act.value_load(over[0:1, 0:1], min_val=0, max_val=1)
            with act.If(flag > 0):
                experts(1)
            norm_rows(4)

        @block.vector
        def _(dve):
            n_self = [0]

            def link(ins):
                n_self[0] += 1
                ins.then_inc(dve_self, 1)
                dve.wait_ge(dve_self, n_self[0])

            def tt(o, a, b, op):
                return nc.vector.tensor_tensor(o, a, b, op)

            def split_lo(n, e=None):
                dve.wait_ge(hi_ready, count(n + 1, e, FFN_UNITS))
                tt(w_lo[:, n % SPLIT, :], raw[:, n % RAW, :], w_hi[:, n % SPLIT, :].bitcast(F32),
                   ALU.subtract).then_inc(lo_ready, 1)

            def norm_rows(i):
                if i == 0:
                    dve.wait_ge(x_landed, 16)
                else:
                    dve.wait_ge(resid_ready, i)
                nc.vector.scalar_tensor_tensor(out=hn[:, 1, :], in0=resid[:, 1, :], scalar=1.0, in1=resid[:, 1, :],
                                               op0=ALU.mult, op1=ALU.mult, accum_out=ssq[:, 1:2]).then_inc(ssq1_done, 1)
                dve.wait_ge(std_done, i + 1)
                nc.vector.reciprocal(rstd[:, :], std[:, :]).then_inc(rstd_done, 1)
                dve.wait_ge(rstd_done, i + 1)
                if i < 3:
                    nc.vector.tensor_scalar(hn[:, 0, :], resid[:, 0, :], rstd[:, 0:1], None, ALU.mult).then_inc(hn0_ready, 1)

            def norm_split(i):
                gain = (gains[:, 0:KT], gains[:, 2 * KT:3 * KT], gains[:, KT:2 * KT])[i]
                dve.wait_ge(gains_ready, 1)
                for bank in range(KT // 2):
                    dve.wait_ge(xhi_ready, KT // 2 * i + bank + 1)
                    for j in range(2):
                        kt = 2 * bank + j
                        ins = nc.vector.scalar_tensor_tensor(
                            out=xt_lo[:, kt, :], in0=PS[:, bank, j * SEQ:(j + 1) * SEQ], scalar=gain[:, kt:kt + 1],
                            in1=xt_hi[:, kt, :].bitcast(F32), op0=ALU.mult, op1=ALU.subtract)
                    ins.then_inc(xlo_ready, 1)

            def ffn(u0, s0, tts, e=None, each=None):
                mult_at = {ffn_first(s) + 6: s for s in range(STEPS)}
                evac_at = {7 if s == 0 else 41 if s == STEPS - 1 else 6 * s + 6: s for s in range(STEPS)}
                for i in range(FFN_UNITS):
                    if i in mult_at:
                        s = s0 + mult_at[i]
                        dve.wait_ge(silu_done, count(s + 1, e, STEPS))
                        dve.wait_ge(used, count(u0 + ffn_first(mult_at[i]) + 4, e, FFN_UNITS))
                        if s:
                            dve.wait_ge(act_t_done, count(s, e, STEPS))
                        tt(act_rows[:, 0:tts, :], gated[:, 0:tts, :], PS[:, tts:2 * tts, :], ALU.mult).then_inc(mult_done, 1)
                    if i in evac_at:
                        s = s0 + evac_at[i]
                        dve.wait_ge(act_hi, count(s + 1, e, STEPS))
                        b = evac_at[i] % 2
                        for t in range(tts):
                            ins = tt(ht_lo[b][:, t, :, :], PS[:, tts + t, :].rearrange("p (f c) -> p f c", f=FT),
                                     ht_hi[b][:, t, :, :].bitcast(F32), ALU.subtract)
                        ins.then_inc(act_lo, 1)
                    if each:
                        each(i)
                    if e is None and i < 3:
                        continue
                    split_lo(u0 + i, e)

            def add_out():
                for t in range(TT):
                    ins = tt(resid[:, t, :], resid[:, t, :], PS[:, 4 + 2 * t:6 + 2 * t, :].rearrange("p a b -> p (a b)"), ALU.add)
                ins.then_inc(resid_ready, 1)

            norm_rows(0)
            norm_split(0)
            split_lo(0)
            split_lo(1)

            def decay(h):
                dve.wait_ge(scores_done, h + 1)
                c = C_DECAY + h * SEQ
                tt(scores[:, 0:SEQ], PS[:, 2, 0:SEQ], cst[:, c:c + SEQ], ALU.mult)
                tt(scores[:, SEQ:SEQ + P], PS[:, 2, SEQ:SEQ + P], cst[:, c:c + P], ALU.mult).then_inc(decayed, 1)

            def group_norm(h):
                dve.wait_ge(y_done, h + 1)
                for t in range(TT):
                    link(nc.vector.bn_stats(bn_s[:, t, :], PS[:, 3 - t, :]))
                for t in range(TT):
                    ins = nc.vector.bn_aggr(bn_a[:, t, :], bn_s[:, t, :])
                ins.then_inc(bn_done, 1)
                dve.wait_ge(hstd_done, h + 1)
                link(nc.vector.reciprocal(hrstd[:, :], hstd[:, :]))
                for t in range(TT):
                    link(nc.vector.tensor_scalar(act_rows[:, t, :], PS[:, 3 - t, :], bn_a[:, t, 0:1], hrstd[:, t:t + 1],
                                                 ALU.subtract, ALU.mult))
                dve.wait_ge(g_silu, h + 1)
                tt(act_rows[:, :, :], act_rows[:, :, :], gated[:, :, :], ALU.mult).then_inc(y_normed, 1)

            def evac_yt(h):
                dve.wait_ge(yt_hi, h + 1)
                for ft in range(FT):
                    ins = nc.vector.scalar_tensor_tensor(
                        out=ht_lo[0][:, :, ft, :], in0=PS[:, 2:4, ft * P:(ft + 1) * P], scalar=g_gn[:, h * FT + ft:h * FT + ft + 1],
                        in1=ht_hi[0][:, :, ft, :].bitcast(F32), op0=ALU.mult, op1=ALU.subtract)
                ins.then_inc(yt_lo, 1)

            for h in range(HEADS):
                f0 = ret_first(h)
                last = RET_UNITS if h == HEADS - 1 else ret_first(h + 1)
                for n in range(f0, last):
                    if n == 3:
                        dve.wait_ge(den_done, 1)
                        nc.vector.reciprocal(p6[0:PAIRS, :], p4[0:PAIRS, :]).then_inc(rden_done, 1)
                    if h and n == f0:
                        decay(h - 1)
                    if h and n == f0 + 1:
                        group_norm(h - 1)
                    if h and n == f0 + 3:
                        evac_yt(h - 1)
                    if n == f0 + 6 and h:
                        dve.wait_ge(used, f0 + 4)
                        nc.vector.tensor_copy(v_rows[:, :, :], PS[:, 2:4, :]).then_inc(v_copied, 1)
                    if h == HEADS - 1 and n == f0 + 8:
                        decay(h)
                    if h == HEADS - 1 and n == f0 + 9:
                        group_norm(h)
                    if n >= 2:
                        split_lo(n)
                if h == 0:
                    dve.wait_ge(used, f0 + 4)
                    nc.vector.tensor_copy(v_rows[:, :, :], PS[:, 2:4, :]).then_inc(v_copied, 1)
            evac_yt(HEADS - 1)

            for i in range(2):
                split_lo(FFN_U0 + i)
            dve.wait_ge(used, FFN_U0)
            add_out()
            norm_rows(1)
            norm_split(1)
            split_lo(FFN_U0 + 2)
            ffn(FFN_U0, 0, TT)

            for i in range(2):
                split_lo(S5_U0 + i)
            dve.wait_ge(used, S5_U0)
            add_out()
            norm_rows(2)
            norm_split(2)
            for c in range(S5_IN_UNITS):
                split_lo(S5_U0 + 2 + c)
                if c == S5_IN_UNITS - 1:
                    split_lo(S5_U0 + 6)
                    dve.wait_ge(u_copied, S5_IN_UNITS)
                    for k in range(KT):
                        ins = nc.vector.tensor_scalar(y_t[:, k, :], u_t[:, k, :], d_skip[:, k:k + 1], None, ALU.mult)
                    ins.then_inc(du_done, 1)

            def flat(t):
                return t[:, :, :].rearrange("p m s -> p (m s)")

            def add_y(b):
                dve.wait_ge(sy_done, b + 1)
                s = slice(b * S5_BLOCK, (b + 1) * S5_BLOCK)
                tt(y_t[:, :, s], y_t[:, :, s], PS[:, 4 + b % 2, 0:KT * S5_BLOCK].rearrange("p (k s) -> p k s", k=KT),
                   ALU.add).then_inc(sy_added, 1)

            dve.wait_ge(du_done, 1)
            dve.wait_ge(setup_done, 1)
            def quarters(t):
                return t[:, :, :].rearrange("p (i k) s -> p i (k s)", i=4)

            bu_re, bu_im = PS[:, 0:4, 0:256], PS[:, 0:4, 256:512]
            cos, sin, re, im, tmp, x_re, x_im = (quarters(t) for t in (cos_t, sin_t, s_re, s_im, s_tmp, st_re, st_im))
            for b in range(S5_BLOCKS):
                dve.wait_ge(bu_done, b + 1)
                tt(re, bu_re, cos, ALU.mult)
                link(tt(im, bu_im, sin, ALU.mult))
                link(tt(re, re, im, ALU.add))
                tt(im, bu_im, cos, ALU.mult)
                tt(tmp, bu_re, sin, ALU.mult).then_inc(bu_read, 1)
                dve.wait_ge(bu_read, b + 1)
                link(tt(im, im, tmp, ALU.subtract))
                if b:
                    lr, li = st_re[:, :, S5_BLOCK - 1], st_im[:, :, S5_BLOCK - 1]
                    tt(car[:, 0, :], ab_re[:, :], lr, ALU.mult)
                    tt(car[:, 1, :], ab_im[:, :], li, ALU.mult)
                    tt(car[:, 2, :], ab_re[:, :], li, ALU.mult)
                    link(tt(car[:, 3, :], ab_im[:, :], lr, ALU.mult))
                    tt(car[:, 0, :], car[:, 0, :], car[:, 1, :], ALU.subtract)
                    link(tt(car[:, 2, :], car[:, 2, :], car[:, 3, :], ALU.add))
                    tt(s_re[:, :, 0], s_re[:, :, 0], car[:, 0, :], ALU.add)
                    link(tt(s_im[:, :, 0], s_im[:, :, 0], car[:, 2, :], ALU.add))
                nc.vector.tensor_tensor_scan(flat(s_re), flat(mag_t), flat(s_re), 0.0, ALU.mult, ALU.add)
                link(nc.vector.tensor_tensor_scan(flat(s_im), flat(mag_t), flat(s_im), 0.0, ALU.mult, ALU.add))
                if b:
                    add_y(b - 1)
                tt(x_re, re, cos, ALU.mult)
                link(tt(tmp, im, sin, ALU.mult))
                link(tt(x_re, x_re, tmp, ALU.subtract))
                tt(x_im, im, cos, ALU.mult)
                link(tt(tmp, re, sin, ALU.mult))
                tt(x_im, x_im, tmp, ALU.add).then_inc(st_ready, 1)
                dve.wait_ge(st_ready, b + 1)
            add_y(S5_BLOCKS - 1)
            for half in range(2):
                k = slice(4 * half, 4 * half + 4)
                dve.wait_ge(xhi_ready, 3 * (KT // 2) + half + 1)
                tt(xt_lo[:, k, :], gelu_t[:, k, :], xt_hi[:, k, :].bitcast(F32), ALU.subtract).then_inc(xlo_ready, 1)

            def glu(dh):
                dve.wait_ge(glu_sig, dh + 1)
                link(tt(glu_out[:, :, :], glu_gate[:, :, :], PS[:, 4 * dh:4 * dh + 2, :], ALU.mult))
                return tt(resid[:, :, dh * 512:dh * 512 + 512], resid[:, :, dh * 512:dh * 512 + 512],
                          glu_out[:, :, :], ALU.add)

            for n in range(7, S5_IN_UNITS + S5_OUT_UNITS):
                if n == 11:
                    glu(0).then_inc(glu_read, 1)
                split_lo(S5_U0 + n)
            dve.wait_ge(glu_read, 1)
            glu(1).then_inc(resid_ready, 1)

            norm_rows(3)
            dve.wait_ge(moe_landed, 32)
            dve.wait_ge(ssq0_done, 4)
            for t, ready in enumerate((hn0_ready, hn1_ready)):
                nc.vector.scalar_tensor_tensor(out=hn[:, t, :], in0=resid[:, t, :], scalar=rstd[:, t:t + 1], in1=gain_row[:, :],
                                               op0=ALU.mult, op1=ALU.mult).then_inc(ready, 1)
            dve.wait_ge(hnt_done, 2)
            nc.vector.tensor_copy(hn_t[:, 4:8, :], PS[:, 2:4, :].rearrange("p a (b c) -> p (a b) c", c=SEQ)).then_inc(hnt_copied, 1)
            dve.wait_ge(logits_done, 1)
            link(nc.vector.tensor_copy(logit[:, :, :], PS[:, 6, 0:TT * EXPERTS].rearrange("p (t e) -> p t e", t=TT)))
            for t in range(TT):
                link(nc.vector.max(top[:, t, :], logit[:, t, :]))
            nc.vector.tensor_scalar(neg_top[:, :], top[:, :, 0], -1.0, None, ALU.mult).then_inc(top_done, 1)
            for t in range(TT):
                second = top[:, t, 1:2]
                nc.vector.tensor_scalar(r_gt[:, t, :], logit[:, t, :], second, None, ALU.is_gt)
                link(nc.vector.tensor_scalar(r_eq[:, t, :], logit[:, t, :], second, None, ALU.is_equal))
                nc.vector.tensor_tensor_scan(r_cum[:, t, :], ones[:, 0:EXPERTS], r_eq[:, t, :], 0.0, ALU.mult, ALU.add)
            link(nc.vector.tensor_reduce(r_n[:, :], r_gt[:, :, :], AX_X, ALU.add))
            link(nc.vector.tensor_scalar(r_n[:, :], r_n[:, :], -1.0, 2.0, ALU.mult, ALU.add))
            for t in range(TT):
                link(nc.vector.tensor_scalar(r_cum[:, t, :], r_cum[:, t, :], r_n[:, t:t + 1], None, ALU.is_le))
            link(tt(r_eq[:, :, :], r_eq[:, :, :], r_cum[:, :, :], ALU.mult))
            tt(chosen[:, :, :], r_gt[:, :, :], r_eq[:, :, :], ALU.add).then_inc(chosen_done, 1)
            dve.wait_ge(chosen_done, 1)
            dve.wait_ge(exp_done, TT)
            link(tt(r_exp[:, :, :], r_exp[:, :, :], chosen[:, :, :], ALU.mult))
            link(nc.vector.tensor_reduce(r_n[:, :], r_exp[:, :, :], AX_X, ALU.add))
            link(nc.vector.reciprocal(r_n[:, :], r_n[:, :]))
            for t in range(TT):
                link(nc.vector.tensor_scalar(gate_w[:, t, :], r_exp[:, t, :], r_n[:, t:t + 1], None, ALU.mult))
            dve.wait_ge(rank_done, 1)
            link(nc.vector.tensor_scalar(r_cum[:, :, :], PS[:, 6, 32:32 + TT * EXPERTS].rearrange("p (t e) -> p t e", t=TT),
                                         1.0, None, ALU.add))
            for b in range(2):
                link(nc.vector.memset(key[b][:, :, :], -1.0))
            link(tt(r_cum[:, :, :], r_cum[:, :, :], chosen[:, :, :], ALU.mult))
            link(nc.vector.tensor_scalar(key[0][:, :, 0:EXPERTS], r_cum[:, :, :], 1.0, None, ALU.subtract))
            link(nc.vector.tensor_scalar(key[1][:, :, 0:EXPERTS], r_cum[:, :, :], 1.0 + SLOTS, None, ALU.subtract))
            link(nc.vector.tensor_reduce(most[:, :], PS[:, 6, 64:64 + EXPERTS], AX_X, ALU.max))
            link(nc.vector.tensor_scalar(most[:, :], most[:, :], float(SLOTS), None, ALU.is_gt))
            nc.vector.tensor_copy(over[:, :], most[:, :]).then_inc(keys_done, 1)
            dve.wait_ge(keys_done, 1)
            link(nc.vector.memset(PS[:, 4, :], 0.0))
            link(nc.vector.memset(PS[:, 5, :], 0.0))

            def make_pick(b, col):
                for t in range(TT):
                    ins = nc.vector.tensor_scalar(pick[:, t, :], iota, key[b][:, t, col], None, ALU.is_equal)
                ins.then_inc(pick_ready, 1)

            def gather_lo(g):
                dve.wait_ge(xg_hi_ready, g)
                tt(xg_lo[:, :, :], PS[:, 2:4, :].rearrange("p a (b c) -> p (a b) c", c=SLOTS), xg_hi[:, :, :].bitcast(F32),
                   ALU.subtract).then_inc(xg_lo_ready, 1)

            def add_scattered(n):
                dve.wait_ge(scattered, n)
                tt(resid[:, 0, :], resid[:, 0, :], PS[:, 2:4, :].rearrange("p a b -> p (a b)"), ALU.add)
                tt(resid[:, 1, :], resid[:, 1, :], PS[:, 6:8, :].rearrange("p a b -> p (a b)"), ALU.add).then_inc(scatter_added, 1)

            def experts(p):
                u0 = MOE_U0 + p * EXPERTS * FFN_UNITS
                nc.vector.memset(put_g[:, :, :], 0.0).then_inc(put_ready, 1)
                make_pick(p, slice(0, 1))
                gather_lo(9 * p + 1)
                with dve.Fori(0, EXPERTS) as e:
                    def each(i):
                        if i == 2:
                            dve.wait_ge(used, count(u0, e, FFN_UNITS))
                            nc.vector.tensor_copy(y_rows[:, 512:1024], PS[:, 5, :]).then_inc(y1_copied, 1)
                            make_pick(p, bass.ds(e + 1, 1))
                        if i == 8:
                            add_scattered(count(9 * p + 1, e, 1))
                        if i == 10:
                            for t in range(TT):
                                ins = nc.vector.tensor_scalar(pick_g[:, t, :], iota, key[p][:, t, bass.ds(e, 1)],
                                                              gate_w[:, t, bass.ds(e, 1)], ALU.is_equal, ALU.mult)
                            ins.then_inc(pick_g_ready, 1)
                    ffn(u0, STEPS * (1 + EXPERTS * p), 1, e, each)
                    gather_lo(count(9 * p + 2, e, 1))
                dve.wait_ge(used, u0 + EXPERTS * FFN_UNITS)
                nc.vector.tensor_copy(y_rows[:, 512:1024], PS[:, 5, :]).then_inc(y1_copied, 1)
                add_scattered(9 * p + 9)
                dve.wait_ge(scatter_added, 9 * p + 9)

            experts(0)
            flag = dve.value_load(over[0:1, 0:1], min_val=0, max_val=1)
            with dve.If(flag > 0):
                experts(1)
            nc.vector.memset(ssq[:, :], 0.0).then_inc(resid_ready, 1)
            norm_rows(4)
            dve.wait_ge(ssq0_done, 5)
            dve.wait_ge(fin_landed, 16)
            for t in range(TT):
                ins = nc.vector.scalar_tensor_tensor(out=hn[:, t, :], in0=resid[:, t, :], scalar=rstd[:, t:t + 1],
                                                     in1=final_gain[:, :], op0=ALU.mult, op1=ALU.mult)
            ins.then_inc(out_ready, 1)

        @block.tensor
        def _(pe):
            def mm(o, l, r, start, stop):
                return nc.tensor.matmul(o, l, r, start=start, stop=stop)

            def split_ready(n, e=None):
                pe.wait_ge(lo_ready, count(n + 1, e, FFN_UNITS))

            def product3(o, l_hi, l_lo, r_hi, r_lo, start, stop):
                mm(o, l_hi, r_hi, start, False)
                mm(o, l_hi, r_lo, False, False)
                return mm(o, l_lo, r_hi, False, stop)

            def rows_unit(n, half, banks, x_hi, x_lo, e=None):
                split_ready(n, e)
                hi = w_hi[:, n % SPLIT, :].rearrange("p (k n) -> p k n", k=4)
                lo = w_lo[:, n % SPLIT, :].rearrange("p (k n) -> p k n", k=4)
                for k in range(4):
                    kt = 4 * half + k
                    for t, bank in enumerate(banks):
                        cols = slice(t * P, (t + 1) * P)
                        ins = product3(PS[:, bank, :], x_hi[:, kt, cols], x_lo[:, kt, cols], hi[:, k, :], lo[:, k, :],
                                       kt == 0, kt == KT - 1)
                ins.then_inc(used, 1)

            def cols_unit(n, bank):
                split_ready(n)
                hi = w_hi[:, n % SPLIT, :].rearrange("p (k n) -> p k n", k=KT)
                lo = w_lo[:, n % SPLIT, :].rearrange("p (k n) -> p k n", k=KT)
                for j in range(2):
                    o = PS[:, bank, j * SEQ:(j + 1) * SEQ]
                    for kt in range(KT):
                        c = slice(j * P, (j + 1) * P)
                        mm(o, hi[:, kt, c], xt_hi[:, kt, :], kt == 0, False)
                        mm(o, hi[:, kt, c], xt_lo[:, kt, :], False, False)
                        ins = mm(o, lo[:, kt, c], xt_hi[:, kt, :], False, kt == KT - 1)
                ins.then_inc(used, 1)

            def out_unit(n, half, tts, a_hi, a_lo, first, last, e=None):
                split_ready(n, e)
                hi = w_hi[:, n % SPLIT, :].rearrange("p (k n) -> p k n", k=2)
                lo = w_lo[:, n % SPLIT, :].rearrange("p (k n) -> p k n", k=2)
                for k in range(2):
                    ft = 2 * half + k
                    for t in range(tts):
                        for dh in range(2):
                            c = slice(dh * 512, dh * 512 + 512)
                            ins = product3(PS[:, out_bank(t, dh), :], a_hi[:, t, ft, :], a_lo[:, t, ft, :],
                                           hi[:, k, c], lo[:, k, c], first and ft == 0, last and ft == FT - 1)
                ins.then_inc(used, 1)

            def transposes(i):
                pe.wait_ge(hn0_ready, i + 1)
                pe.wait_ge(hn1_ready, i + 1)
                for kt in range(KT):
                    for t in range(TT):
                        c = kt % 2 * SEQ + t * P
                        ins = nc.tensor.transpose(PS[:, kt // 2, c:c + P], hn[:, t, kt * P:(kt + 1) * P], ident)
                    yield kt, ins

            def norm(i):
                for kt, ins in transposes(i):
                    if kt % 2:
                        ins.then_inc(xt_done, 1)
                pe.wait_ge(xlo_ready, KT // 2 * (i + 1))

            def turn_rows(banks):
                for t, bank in enumerate(banks):
                    for ft in range(FT):
                        ins = nc.tensor.transpose(PS[:, bank, ft * P:(ft + 1) * P],
                                                  act_rows[:, t, ft * P:(ft + 1) * P], ident)
                return ins

            def ffn(u0, s0, tts, x_hi, x_lo, e=None, after_up0=None, each=None, before_last=None):
                def turn(s):
                    pe.wait_ge(mult_done, count(s0 + s + 1, e, STEPS))
                    turn_rows(up_banks(tts)).then_inc(act_t_done, 1)

                def down(s, half, i):
                    if half == 0:
                        pe.wait_ge(act_lo, count(s0 + s + 1, e, STEPS))
                    out_unit(u0 + i, half, tts, ht_hi[s % 2], ht_lo[s % 2], s == 0, s == STEPS - 1, e)

                for s in range(STEPS):
                    f0 = ffn_first(s)
                    if s0 + s:
                        pe.wait_ge(silu_done, count(s0 + s, e, STEPS))
                    for half in range(2):
                        rows_unit(u0 + f0 + half, half, gate_banks(tts), x_hi, x_lo, e)
                    if s0 + s:
                        pe.wait_ge(act_lo, count(s0 + s, e, STEPS))
                    for half in range(2):
                        rows_unit(u0 + f0 + 2 + half, half, up_banks(tts), x_hi, x_lo, e)
                    if s == 0:
                        if after_up0:
                            after_up0()
                        turn(0)
                        continue
                    down(s - 1, 0, f0 + 4)
                    turn(s)
                    if each:
                        each(s)
                    down(s - 1, 1, f0 + 5)
                if before_last:
                    before_last()
                down(STEPS - 1, 0, FFN_UNITS - 2)
                down(STEPS - 1, 1, FFN_UNITS - 1)

            pe.wait_ge(c_landed, 16)
            pe.wait_ge(g_landed, 64)
            nc.tensor.transpose(PS[:, 7, 0:7 * KT], gain_rows[0:7 * KT, :],
                                cst[0:7 * KT, C_IDENT:C_IDENT + 7 * KT]).then_inc(gains_t, 1)
            norm(0)

            def turn_y(h):
                pe.wait_ge(y_normed, h + 1)
                turn_rows([2, 3]).then_inc(yt_done, 1)

            def head_out(h, half, n):
                if half == 0:
                    pe.wait_ge(yt_lo, h + 1)
                    pe.wait_ge(par_ready, 1)
                out_unit(n, half, TT, ht_hi[0], ht_lo[0], h == 0, h == HEADS - 1)

            for h in range(HEADS):
                f0 = ret_first(h)
                if h:
                    pe.wait_ge(g_silu, h)
                cols_unit(f0, 0)
                if h:
                    turn_y(h - 1)
                cols_unit(f0 + 1, 1)
                if h:
                    pe.wait_ge(yt_lo, h)
                for half in range(2):
                    rows_unit(f0 + 2 + half, half, (2, 3), xt_hi, xt_lo)
                pe.wait_ge(qk_copied, h + 1)
                for half in range(2):
                    rows_unit(f0 + 4 + half, half, (0, 1), xt_hi, xt_lo)
                pe.wait_ge(v_copied, h + 1)
                for dt_i in range(2):
                    mm(PS[:, 2, 0:SEQ], qk_t[:, 1, dt_i, 0:P], qk_t[:, 0, dt_i, :], dt_i == 0, dt_i == 1)
                for dt_i in range(2):
                    ins = mm(PS[:, 2, SEQ:SEQ + P], qk_t[:, 1, dt_i, P:SEQ], qk_t[:, 0, dt_i, P:SEQ], dt_i == 0, dt_i == 1)
                ins.then_inc(scores_done, 1)
                if h:
                    head_out(h - 1, 0, f0 + 6)
                pe.wait_ge(decayed, h + 1)
                mm(PS[:, 3, :], scores[:, 0:P], v_rows[:, 0, :], True, True)
                mm(PS[:, 2, :], scores[:, P:SEQ], v_rows[:, 0, :], True, False)
                mm(PS[:, 2, :], scores[:, SEQ:SEQ + P], v_rows[:, 1, :], False, True).then_inc(y_done, 1)
                if h:
                    head_out(h - 1, 1, f0 + 7)
                if h == 0:
                    pe.wait_ge(par_done, 1)
                    for i in range(5):
                        ins = nc.tensor.transpose(PS[:, 4, i * PAIRS:(i + 1) * PAIRS], par_in[0:PAIRS, i, :],
                                                  cst[0:PAIRS, C_IDENT:C_IDENT + PAIRS])
                    ins.then_inc(par_t, 1)
            turn_y(HEADS - 1)
            for half in range(2):
                head_out(HEADS - 1, half, RET_UNITS - 2 + half)

            norm(1)
            ffn(FFN_U0, 0, TT, xt_hi, xt_lo)

            norm(2)
            pe.wait_ge(setup_done, 1)
            for j, (src, m) in enumerate(((bb_re, 4), (bb_im, 4))):
                for k in range(KT):
                    ins = nc.tensor.transpose(PS[:, 4 + 2 * j + k // 4, k % 4 * P:(k % 4 + 1) * P],
                                              src[:, m * k:m * k + m, :].rearrange("p a b -> p (a b)"), ident)
            ins.then_inc(bt_done, 1)
            pe.wait_ge(bt_copied, 2)
            for j, src in enumerate((cc_re, cc_im)):
                for k in range(KT):
                    ins = nc.tensor.transpose(PS[:, 4 + 2 * j + k // 4, k % 4 * P:(k % 4 + 1) * P], src[:, k, :], ident)
            ins.then_inc(ct_done, 1)
            for c in range(S5_IN_UNITS):
                cols_unit(S5_U0 + c, c)
            pe.wait_ge(u_copied, S5_IN_UNITS)
            pe.wait_ge(ct_copied, 2)

            def rows32(m):
                return slice(32 * (m % 4), 32 * (m % 4) + 32)

            def s5_in(b):
                for j, w in enumerate((bt_re, bt_im)):
                    for m in range(PAIRS):
                        r = rows32(m)
                        c = 256 * j + m // 4 * S5_BLOCK
                        ins = mm(PS[:, m % 4, c:c + S5_BLOCK],
                                 w[r, m // 4, :], u_t[r, m // 4, b * S5_BLOCK:(b + 1) * S5_BLOCK], True, True)
                ins.then_inc(bu_done, 1)

            s5_in(0)
            for b in range(S5_BLOCKS):
                if b + 1 < S5_BLOCKS:
                    pe.wait_ge(bu_read, b + 1)
                    s5_in(b + 1)
                pe.wait_ge(st_ready, b + 1)
                if b >= 2:
                    pe.wait_ge(sy_added, b - 1)
                for m in range(PAIRS):
                    r = rows32(m)
                    o = PS[r, 4 + b % 2, m // 4 * S5_BLOCK:(m // 4 + 1) * S5_BLOCK]
                    mm(o, ct_re[:, m // 4, r], st_re[:, state_at(m), :], True, False)
                    ins = mm(o, ct_im[:, m // 4, r], st_im[:, state_at(m), :], False, True)
                ins.then_inc(sy_done, 1)
            pe.wait_ge(xlo_ready, 3 * (KT // 2) + 2)
            n = S5_U0 + S5_IN_UNITS
            for dh in range(2):
                for part in range(2):
                    for half in range(2):
                        rows_unit(n, half, (4 * dh + 2 * part, 4 * dh + 2 * part + 1), xt_hi, xt_lo)
                        n += 1

            for kt, ins in transposes(3):
                if kt % 4 == 3:
                    ins.then_inc(hnt_done, 1)
            pe.wait_ge(hnt_copied, 2)
            pe.wait_ge(moe_landed, 32)
            for t in range(TT):
                for kt in range(KT):
                    ins = mm(PS[:, 6, t * EXPERTS:(t + 1) * EXPERTS], hn_t[:, kt, t * P:(t + 1) * P], router[:, kt, :],
                             kt == 0, kt == KT - 1)
            ins.then_inc(logits_done, 1)
            pe.wait_ge(chosen_done, 1)
            mm(PS[:, 6, 32:32 + EXPERTS], tri, chosen[:, 0, :], True, True)
            mm(PS[:, 6, 40:40 + EXPERTS], ones, chosen[:, 0, :], True, False)
            mm(PS[:, 6, 40:40 + EXPERTS], tri, chosen[:, 1, :], False, True)
            mm(PS[:, 6, 64:64 + EXPERTS], ones, chosen[:, 0, :], True, False)
            mm(PS[:, 6, 64:64 + EXPERTS], ones, chosen[:, 1, :], False, True).then_inc(rank_done, 1)

            def gather(n):
                pe.wait_ge(pick_ready, n)
                for kt in range(KT):
                    for t in range(TT):
                        ins = mm(PS[:, 2 + kt // 4, kt % 4 * P:(kt % 4 + 1) * P], hn[:, t, kt * P:(kt + 1) * P],
                                 pick[:, t, :], t == 0, t == TT - 1)
                ins.then_inc(gathered, 1)

            def scatter(n):
                pe.wait_ge(y0_copied, n)
                pe.wait_ge(y1_copied, n)
                pe.wait_ge(put_ready, n)
                for t in range(TT):
                    for dh in range(2):
                        ins = mm(PS[:, 2 + 4 * t + dh, :], put_g[:, t, :], y_rows[:, dh * 512:dh * 512 + 512], True, True)
                ins.then_inc(scattered, 1)

            def experts(p):
                u0 = MOE_U0 + p * EXPERTS * FFN_UNITS
                gather(9 * p + 1)
                with pe.Fori(0, EXPERTS) as e:
                    pe.wait_ge(xg_lo_ready, count(9 * p + 1, e, 1))

                    def after_up0():
                        scatter(count(9 * p + 1, e, 1))

                    def each(s):
                        if s == 2:
                            pe.wait_ge(pick_g_ready, count(8 * p + 1, e, 1))
                            pe.wait_ge(scatter_added, count(9 * p + 1, e, 1))
                            for t in range(TT):
                                ins = nc.tensor.transpose(PS[:, 6, t * P:(t + 1) * P], pick_g[:, t, :], ident)
                            ins.then_inc(put_t_done, 1)

                    def before_last():
                        gather(count(9 * p + 2, e, 1))

                    ffn(u0, STEPS * (1 + EXPERTS * p), 1, xg_hi, xg_lo, e, after_up0, each, before_last)
                pe.wait_ge(xg_lo_ready, 9 * p + 9)
                scatter(9 * p + 9)
                pe.wait_ge(scatter_added, 9 * p + 9)

            experts(0)
            pe.wait_ge(keys_done, 1)
            flag = pe.value_load(over[0:1, 0:1], min_val=0, max_val=1)
            with pe.If(flag > 0):
                experts(1)


_INS = ["x", "norm_mix", "norm_ffn", "norm_final", "ret_w_in", "ret_gn", "ret_w_out", "s5_w_in", "s5_a_re", "s5_a_im",
        "s5_log_step", "s5_b_re", "s5_b_im", "s5_c_re", "s5_c_im", "s5_d", "s5_w_out", "ffn_w_gate", "ffn_w_up",
        "ffn_w_down", "moe_router", "moe_w_gate", "moe_w_up", "moe_w_down"]


def kernel(**inputs):
    import concourse.bacc as bacc
    from concourse.bass_utils import run_bass_kernel_spmd

    nc = bacc.Bacc("TRN2", target_bir_lowering=False, num_devices=1)
    arrays, aps = {}, {}
    for name in _INS:
        a = np.ascontiguousarray(inputs[name])
        arrays[f"in_{name}"] = a
        aps[name] = nc.dram_tensor(f"in_{name}", a.shape, F32, kind="ExternalInput").ap()
    arrays["in_constants"] = constants()
    consts = nc.dram_tensor("in_constants", (P, C_COLS), F32, kind="ExternalInput").ap()
    out = nc.dram_tensor("out", (1, SEQ, D), F32, kind="ExternalOutput").ap()
    trunk(nc, aps, consts, out)
    r = run_bass_kernel_spmd(nc, [arrays], core_ids=[0])
    return r.results[0]["out"]
```

```python
import math
from contextlib import ExitStack

import numpy as np

import concourse.bass as bass
from concourse import mybir

F32 = mybir.dt.float32
F32R = mybir.dt.float32r
I32 = mybir.dt.int32
ALU = mybir.AluOpType
ACT = mybir.ActivationFunctionType
AX_X = mybir.AxisListType.X

P = 128
D = 1024
SEQ = 256
TT = SEQ // P
KT = D // P
EPS = 1e-6

HEADS = 4
DK = D // HEADS
DV = 2 * D // HEADS

GROUPS, STATES, GROUP_W = 64, 64, 16
PAIRS = GROUPS // 2
STEP = 2
FRAME = 64
FRAMES = SEQ // STEP // FRAME
QUARTERS = 4
QPAIRS = PAIRS // QUARTERS

FF = 3584
FC = 512
STEPS = FF // FC
FT = FC // P
EXPERTS = 8
SLOTS = P

UNIT = 2048
RAW = 6
SPLIT = 3
FFN_UNITS = 6 * STEPS

RET_U0 = 0
RET_UNITS = 8 * HEADS
FFN_U0 = RET_U0 + RET_UNITS
S5_U0 = FFN_U0 + FFN_UNITS
S5_IN_UNITS, S5_OUT_UNITS = 4, 8
MOE_U0 = S5_U0 + S5_IN_UNITS + S5_OUT_UNITS

C_DECAY = 0
C_IDENT = C_DECAY + HEADS * SEQ
C_IOTA = C_IDENT + P
C_TRI = C_IOTA + P
C_ONES = C_TRI + P
C_EVEN = C_ONES + P
C_ODD = C_EVEN + 1
C_EPS = C_ODD + 1
C_COLS = C_EPS + 2

TWO_PI = 2 * math.pi
PI_1 = 6.28125
PI_2 = float(np.float32(round((TWO_PI - PI_1) * 2 ** 21) / 2 ** 21))
PI_3 = TWO_PI - PI_1 - PI_2
ROUND = 1.5 * 2 ** 23
PI_F32 = 3.1415925


def constants():
    c = np.zeros((P, C_COLS), np.float32)
    key = np.arange(P)[:, None].astype(np.float64)
    query = np.arange(SEQ)[None, :].astype(np.float64)
    for h in range(HEADS):
        log_gamma = np.log1p(-np.exp2(-5.0 - h))
        decay = np.where(query >= key, np.exp(log_gamma * np.maximum(query - key, 0)), 0)
        c[:, C_DECAY + h * SEQ:C_DECAY + (h + 1) * SEQ] = decay * DK ** -0.5
    c[:, C_IDENT:C_IDENT + P] = np.eye(P)
    c[:, C_IOTA:C_IOTA + P] = np.arange(P)[None, :]
    c[:, C_TRI:C_TRI + P] = np.arange(P)[:, None] < np.arange(P)[None, :]
    c[:, C_ONES:C_ONES + P] = 1
    odd = (np.arange(P) // GROUP_W) % 2
    c[:, C_EVEN], c[:, C_ODD] = 1 - odd, odd
    c[:, C_EPS] = EPS
    return c


def ret_first(h):
    return 0 if h == 0 else 8 * h - 2


def ffn_first(s):
    return 0 if s == 0 else 6 * s - 2


def slot_of(m):
    return m % 4 * 2 + m // 4 % 2


def trunk(nc, A, consts, out):
    with ExitStack() as ctx:
        def sem(name):
            return ctx.enter_context(nc.semaphore(name))

        base = 16512

        def place(name, shape, dt, offset):
            return nc.alloc_sbuf_tensor_at(name, [P, *shape], dt, offset=base + offset)

        raw = place("weights_raw", [RAW, UNIT], F32, 0)
        w_hi = place("weights_hi", [SPLIT, UNIT], F32R, 49152)
        w_lo = place("weights_lo", [SPLIT, UNIT], F32R, 73728)
        cst = place("constants", [C_COLS], F32, 98304)
        SMALL = 98304 + 6208
        H_OFF = SMALL + 5120
        resid = place("residual", [TT, D], F32, H_OFF)
        hn = place("normed_rows", [TT, D], F32, H_OFF + 8192)
        xt_hi = place("x_transposed_hi", [KT, SEQ], F32R, H_OFF + 16384)
        xt_lo = place("x_transposed_lo", [KT, SEQ], F32R, H_OFF + 24576)
        K_OFF = H_OFF + 32768
        cos_t = place("cos_table", [QUARTERS, QPAIRS * FRAME], F32, K_OFF)
        sin_t = place("sin_table", [QUARTERS, QPAIRS * FRAME], F32, K_OFF + 8192)
        bb = [[place("b_rows_re", [PAIRS, 2 * GROUP_W], F32, K_OFF + 16384),
               place("b_rows_im", [PAIRS, 2 * GROUP_W], F32, K_OFF + 20480)],
              [place("ab_rows_re", [PAIRS, 2 * GROUP_W], F32, K_OFF + 24576),
               place("ab_rows_im", [PAIRS, 2 * GROUP_W], F32, 98304 + 4 * C_DECAY)]]
        W_OFF = K_OFF + 28672
        ht_hi = [place(f"act_transposed_hi{b}", [TT, FT, P], F32R, W_OFF + 4096 * b) for b in range(2)]
        ht_lo = [place(f"act_transposed_lo{b}", [TT, FT, P], F32R, W_OFF + 8192 + 4096 * b) for b in range(2)]
        gated = place("silu_of_gate", [TT, FC], F32, W_OFF + 16384)
        act_rows = place("act_rows", [TT, FC], F32, W_OFF + 20480)
        qk_t = place("q_and_k_transposed", [2, 2, SEQ], F32, W_OFF + 24576)
        v_rows = place("v_rows", [TT, DV], F32, W_OFF + 28672)
        gain_rows = place("gain_rows", [P], F32, W_OFF + 28672)
        scores = place("scores_transposed", [384], F32, W_OFF + 32768)
        T_OFF = W_OFF + 34304
        tmp1 = place("setup_tmp1", [PAIRS, GROUP_W], F32, T_OFF)
        tmp2 = place("setup_tmp2", [PAIRS, GROUP_W], F32, T_OFF + 2048)
        b_re = place("b_re", [PAIRS, GROUP_W], F32, W_OFF + 4096)
        b_im = place("b_im", [PAIRS, GROUP_W], F32, W_OFF + 4096 + 2048)
        log_step = place("log_step", [2], F32, T_OFF + 4096)
        dt = place("dt", [2], F32, T_OFF + 4128)
        par_in = place("params_by_pair", [5, P], F32, T_OFF + 4160)
        a_re = place("a_re", [P], F32, T_OFF)
        a_im = place("a_im", [P], F32, T_OFF + 512)
        p1 = place("param_tmp1", [P], F32, T_OFF + 1024)
        p2 = place("param_tmp2", [P], F32, T_OFF + 1536)
        p3 = place("param_tmp3", [P], F32, T_OFF + 2048)
        p4 = place("param_tmp4", [P], F32, T_OFF + 2560)
        p5 = place("param_tmp5", [P], F32, T_OFF + 3072)
        p6 = place("param_tmp6", [P], F32, T_OFF + 3584)
        u_t = place("u_transposed", [KT, SEQ], F32, H_OFF + 8192)
        y_t = place("y_transposed", [KT, SEQ], F32, H_OFF + 16384)
        bt = [[place(f"b{i}_transposed_{part}", [KT, P], F32, W_OFF + 8192 * i + 4096 * j)
               for j, part in enumerate(("re", "im"))] for i in range(STEP)]
        ct = [[place(f"c{i}_transposed_{part}", [KT, P], F32, W_OFF + 16384 + 8192 * i + 4096 * j)
               for j, part in enumerate(("re", "im"))] for i in range(STEP)]
        cc = [place(f"c_rows_{part}", [KT, P], F32, W_OFF + 24576 + 4096 * j) for j, part in enumerate(("re", "im"))]
        c_in = [place(f"c_{part}", [KT, STATES], F32, T_OFF + 2048 * j) for j, part in enumerate(("re", "im"))]
        gelu_t = place("gelu_transposed", [KT, SEQ], F32, W_OFF + 32768)
        direct = place("direct_transposed", [KT, P], F32, 98304 + 4 * C_DECAY)
        scan = place("scan", [2, FRAMES, QPAIRS * FRAME], F32, 49152)
        scan_tmp = place("scan_tmp", [FRAMES, QPAIRS * FRAME], F32, 73728)
        mag_t = place("magnitude_table", [QUARTERS, QPAIRS * FRAME], F32, 49152 + 8192)
        states = [place("states0", [2, FRAMES, QPAIRS * FRAME], F32, 49152 + 16384),
                  place("states1", [2, FRAMES, QPAIRS * FRAME], F32, 73728 + 16384)]
        glu_gate = place("glu_gate", [TT, 512], F32, W_OFF + 24576)
        glu_out = place("glu_out", [TT, 512], F32, W_OFF + 28672)
        gain_row = place("ffn_gain_row", [D], F32, K_OFF)
        hn_t = place("normed_transposed", [KT, SEQ], F32, K_OFF + 4096)
        xg_hi = place("gathered_hi", [KT, SLOTS], F32R, K_OFF + 12288)
        xg_lo = place("gathered_lo", [KT, SLOTS], F32R, K_OFF + 16384)
        y_rows = place("expert_rows", [D], F32, K_OFF + 20480)
        pick = place("pick", [TT, SLOTS], F32, K_OFF + 24576)
        pick_g = place("pick_gated", [TT, SLOTS], F32, K_OFF + 25600)
        put_g = place("put_gated", [TT, P], F32, K_OFF + 26624)
        final_gain = place("final_gain_row", [D], F32, H_OFF + 16384)

        small_at = [SMALL]

        def small(name, shape, dt=F32):
            size = -(-4 * math.prod(shape) // 32) * 32
            small_at[0] += size
            assert small_at[0] <= H_OFF
            return place(name, shape, dt, small_at[0] - size)

        gains = small("gains", [7 * KT])
        g_gn = gains[:, 4 * KT:6 * KT]
        d_skip = gains[:, 6 * KT:7 * KT]
        ssq = small("sum_of_squares", [TT])
        std = small("std", [TT])
        rstd = small("rstd", [TT])
        bn_s = small("bn_stats", [TT, 6])
        bn_a = small("bn_mean_var", [TT, 2])
        hstd = small("head_std", [TT])
        hrstd = small("head_rstd", [TT])
        par = small("params", [5, PAIRS])
        ab_re = small("abar_re", [PAIRS])
        ab_im = small("abar_im", [PAIRS])
        af_re = small("abar_f_re", [PAIRS])
        af_im = small("abar_f_im", [PAIRS])
        nat = small("two_steps", [3, PAIRS])
        mag2 = small("magnitude", [PAIRS])
        pw_re = small("power_re", [PAIRS])
        pw_im = small("power_im", [PAIRS])
        pw_t = small("power_tmp", [2, PAIRS])
        turn_re = small("frame_turn_re", [PAIRS])
        turn_im = small("frame_turn_im", [PAIRS])
        car = small("carry", [2, 2, QPAIRS])
        router = small("router", [KT, EXPERTS])
        logit = small("logits", [TT, EXPERTS])
        top = small("top", [TT, 8])
        r_gt = small("is_above_second", [TT, EXPERTS])
        r_eq = small("is_second", [TT, EXPERTS])
        r_cum = small("count_of_second", [TT, EXPERTS])
        r_n = small("n_above", [TT])
        chosen = small("chosen", [TT, EXPERTS])
        r_exp = small("exp", [TT, EXPERTS])
        neg_top = small("neg_top", [TT])
        gate_w = small("gate_weight", [TT, EXPERTS])
        key = [small(f"slot_key{b}", [TT, EXPERTS + 1]) for b in range(2)]
        most = small("largest_count", [1])
        over = small("over", [1], I32)

        PS = ctx.enter_context(nc.psum_tensor("PS", [P, 8, 512], F32))

        ident = cst[:, C_IDENT:C_IDENT + P]
        iota = cst[:, C_IOTA:C_IOTA + P]
        tri = cst[:, C_TRI:C_TRI + P]
        ones = cst[:, C_ONES:C_ONES + P]
        eps = cst[:, C_EPS:C_EPS + 1]

        def gate_banks(tts):
            return list(range(tts))

        def up_banks(tts):
            return list(range(tts, 2 * tts))

        def out_bank(tt, dh):
            return 4 + 2 * tt + dh

        landed = [sem(f"raw_landed{i}") for i in range(RAW)]
        hi_ready = sem("weights_hi_ready")
        lo_ready = sem("weights_lo_ready")
        used = sem("units_used")
        x_landed = sem("x_landed")
        c_landed = sem("constants_landed")
        g_landed = sem("gains_landed")
        gains_t = sem("gains_transposed")
        gains_ready = sem("gains_ready")
        a_landed = sem("s5_a_landed")
        bc_landed = sem("s5_b_landed")
        cin_landed = sem("s5_c_landed")
        moe_landed = sem("moe_params_landed")
        fin_landed = sem("final_gain_landed")
        resid_ready = sem("residual_ready")
        ssq0_done = sem("ssq0_done")
        ssq1_done = sem("ssq1_done")
        std_done = sem("std_done")
        rstd_done = sem("rstd_done")
        hn0_ready = sem("normed0_ready")
        hn1_ready = sem("normed1_ready")
        xt_done = sem("x_transposed")
        xhi_ready = sem("x_hi_ready")
        xlo_ready = sem("x_lo_ready")
        qk_copied = sem("q_k_copied")
        v_copied = sem("v_copied")
        g_silu = sem("g_silu_done")
        scores_done = sem("scores_done")
        decayed = sem("scores_decayed")
        y_done = sem("retention_y_done")
        bn_done = sem("bn_done")
        hstd_done = sem("head_std_done")
        y_normed = sem("y_normed")
        yt_done = sem("y_transposed_done")
        yt_hi = sem("y_transposed_hi")
        yt_lo = sem("y_transposed_lo")
        silu_done = sem("silu_done")
        mult_done = sem("act_rows_done")
        act_t_done = sem("act_transposed")
        act_hi = sem("act_hi_ready")
        act_lo = sem("act_lo_ready")
        dt_done = sem("dt_done")
        ar_done = sem("a_times_dt_done")
        mag_done = sem("mag_done")
        angle_done = sem("angle_done")
        sin_done = sem("sin_done")
        den_done = sem("den_done")
        rden_done = sem("rden_done")
        par_done = sem("params_done")
        par_t = sem("params_transposed")
        par_ready = sem("params_ready")
        setup_done = sem("s5_setup_done")
        bt_done = sem("b_transposed_done")
        bt_copied = sem("b_copied")
        ct_done = sem("c_transposed_done")
        ct_copied = sem("c_copied")
        u_copied = sem("u_copied")
        bu_done = sem("bu_done")
        bu_read = sem("bu_read")
        c_padded = sem("c_rows_padded")
        ct1_ready = sem("c_times_abar_ready")
        mag_ready = sem("magnitude_table_ready")
        zero_ready = sem("direct_zeroed")
        direct_done = sem("direct_done")
        direct_ready = sem("direct_ready")
        st_re_ready = sem("states_re_ready")
        st_im_ready = sem("states_im_ready")
        sy_done = sem("s5_y_done")
        sy_added = sem("s5_y_added")
        gelu_done = sem("gelu_done")
        glu_sig = sem("glu_sigmoid_done")
        glu_read = sem("glu_gate_read")
        hnt_done = sem("normed_transposed_done")
        hnt_copied = sem("normed_transposed_copied")
        logits_done = sem("logits_done")
        top_done = sem("top_done")
        exp_done = sem("exp_done")
        chosen_done = sem("chosen_done")
        rank_done = sem("rank_done")
        keys_done = sem("keys_done")
        pick_ready = sem("pick_ready")
        pick_g_ready = sem("pick_gated_ready")
        gathered = sem("gathered")
        xg_hi_ready = sem("gathered_hi_ready")
        xg_lo_ready = sem("gathered_lo_ready")
        put_t_done = sem("put_transposed")
        put_ready = sem("put_ready")
        y0_copied = sem("expert_rows0_copied")
        y1_copied = sem("expert_rows1_copied")
        scattered = sem("scattered")
        scatter_added = sem("scatter_added")
        out_ready = sem("out_ready")
        stored = sem("output_stored")
        dve_self = sem("vector_self")
        act_self = sem("scalar_self")
        pool_self = sem("gpsimd_self")

        def count(static, e=None, per=0):
            return static if e is None else e * per + static

        def ffn_sources(w_gate, w_up, w_down):
            units = []
            for s in range(STEPS + 1):
                if s < STEPS:
                    for w in (w_gate, w_up):
                        for half in range(2):
                            units.append((4, w[half * 512:half * 512 + 512, s * FC:(s + 1) * FC]))
                if s > 0:
                    for half in range(2):
                        r = (s - 1) * FC + half * 256
                        units.append((2, w_down[r:r + 256, :]))
            return units

        def static_sources():
            w_in, w_out = A["ret_w_in"][0], A["ret_w_out"][0]
            units = []

            def head_out(h):
                return [(2, w_out[h * DV + a:h * DV + a + 256, :]) for a in (0, 256)]
            for h in range(HEADS):
                units.append((8, w_in[:, h * DK:(h + 1) * DK]))
                units.append((8, w_in[:, D + h * DK:D + (h + 1) * DK]))
                for c0 in (2 * D + h * DV, 4 * D + h * DV):
                    units += [(4, w_in[a:a + 512, c0:c0 + DV]) for a in (0, 512)]
                if h:
                    units += head_out(h - 1)
            units += head_out(HEADS - 1)
            units += ffn_sources(A["ffn_w_gate"][0], A["ffn_w_up"][0], A["ffn_w_down"][0])
            s_in, s_out = A["s5_w_in"][0], A["s5_w_out"][0]
            units += [(8, s_in[:, c * 256:(c + 1) * 256]) for c in range(4)]
            for dh in range(2):
                for c0 in (dh * 512, D + dh * 512):
                    units += [(4, s_out[a:a + 512, c0:c0 + 512]) for a in (0, 512)]
            assert len(units) == MOE_U0
            return units

        block = ctx.enter_context(nc.Block())

        @block.sync
        def _(sp):
            sp.dma_start(resid[:, :, :], A["x"][0].rearrange("(t p) d -> p t d", p=P)).then_inc(x_landed, 16)

            def load(n, kt, src, e=None):
                if n >= RAW:
                    sp.wait_ge(lo_ready, count(n - RAW + 1, e, FFN_UNITS))
                sp.dma_start(raw[:, n % RAW, :].rearrange("p (k n) -> p k n", k=kt),
                             src.rearrange("(k p) n -> p k n", p=P)).then_inc(landed[n % RAW], 16)

            for n, (kt, src) in enumerate(static_sources()):
                load(n, kt, src)

            def experts(u0):
                with sp.Fori(0, EXPERTS) as e:
                    for i, (kt, src) in enumerate(ffn_sources(
                            A["moe_w_gate"][0, e], A["moe_w_up"][0, e], A["moe_w_down"][0, e])):
                        load(u0 + i, kt, src, e)

            experts(MOE_U0)
            sp.wait_ge(keys_done, 1)
            flag = sp.value_load(over[0:1, 0:1], min_val=0, max_val=1)
            with sp.If(flag > 0):
                experts(MOE_U0 + EXPERTS * FFN_UNITS)
            sp.wait_ge(out_ready, 1)
            sp.dma_start(out[0].rearrange("(t p) d -> p t d", p=P), hn[:, :, :]).then_inc(stored, 16)
            sp.wait_ge(stored, 16)

        @block.gpsimd
        def _(pool):
            n_self = [0]

            def link(ins):
                n_self[0] += 1
                ins.then_inc(pool_self, 1)
                pool.wait_ge(pool_self, n_self[0])

            def tt(o, a, b, op):
                link(nc.gpsimd.tensor_tensor(o, a, b, op))

            def ts(o, a, x, y, op0, op1):
                link(nc.gpsimd.tensor_scalar(o, a, x, y, op0, op1))

            q = slice(0, PAIRS)
            pool.dma_start(log_step[q, :], A["s5_log_step"][0].rearrange("(m g) -> m g", g=2)).then_inc(a_landed, 16)
            pool.dma_start(a_re[q, :], A["s5_a_re"][0].rearrange("(m g) p -> m (g p)", g=2)).then_inc(a_landed, 16)
            pool.dma_start(a_im[q, :], A["s5_a_im"][0].rearrange("(m g) p -> m (g p)", g=2)).then_inc(a_landed, 16)
            for dst, name in ((b_re, "s5_b_re"), (b_im, "s5_b_im")):
                pool.dma_start(dst[:, :, :], A[name][0].rearrange("(m g) p n -> (g p) m n", g=2)).then_inc(bc_landed, 16)

            pool.wait_ge(a_landed, 48)
            pool.wait_ge(dt_done, 1)
            halves = lambda x: x[q, :].rearrange("m (g p) -> m g p", g=2)
            dt_b = dt[q, :].unsqueeze(2).to_broadcast([PAIRS, 2, STATES])
            nc.gpsimd.tensor_tensor(halves(p1), halves(a_re), dt_b, ALU.mult).then_inc(ar_done, 1)
            tt(halves(p2), halves(a_im), dt_b, ALU.mult)
            ts(p3[q, :], p2[q, :], 1 / TWO_PI, ROUND, ALU.mult, ALU.add)
            ts(p3[q, :], p3[q, :], ROUND, None, ALU.subtract, ALU.bypass)
            for part in (PI_1, PI_2, PI_3):
                ts(p4[q, :], p3[q, :], part, None, ALU.mult, ALU.bypass)
                tt(p2[q, :], p2[q, :], p4[q, :], ALU.subtract)
            nc.gpsimd.tensor_scalar(p2[q, :], p2[q, :], PI_F32, -PI_F32, ALU.min, ALU.max).then_inc(angle_done, 1)
            tt(p4[q, :], a_re[q, :], a_re[q, :], ALU.mult)
            tt(p5[q, :], a_im[q, :], a_im[q, :], ALU.mult)
            nc.gpsimd.tensor_tensor(p4[q, :], p4[q, :], p5[q, :], ALU.add).then_inc(den_done, 1)
            pool.wait_ge(sin_done, 2)
            pool.wait_ge(den_done, 1)
            pool.wait_ge(mag_done, 1)
            mag, cos, sin, f_re, f_im = (par_in[q, i, :] for i in range(5))
            tt(p5[q, :], cos, cos, ALU.mult)
            ts(cos, p5[q, :], -2.0, 1.0, ALU.mult, ALU.add)
            tt(p1[q, :], mag, cos, ALU.mult)
            ts(p1[q, :], p1[q, :], 1.0, None, ALU.subtract, ALU.bypass)
            tt(p2[q, :], mag, sin, ALU.mult)
            pool.wait_ge(rden_done, 1)
            tt(p3[q, :], p1[q, :], a_re[q, :], ALU.mult)
            tt(p5[q, :], p2[q, :], a_im[q, :], ALU.mult)
            tt(p3[q, :], p3[q, :], p5[q, :], ALU.add)
            tt(f_re, p3[q, :], p6[q, :], ALU.mult)
            tt(p3[q, :], p2[q, :], a_re[q, :], ALU.mult)
            tt(p5[q, :], p1[q, :], a_im[q, :], ALU.mult)
            tt(p3[q, :], p3[q, :], p5[q, :], ALU.subtract)
            nc.gpsimd.tensor_tensor(f_im, p3[q, :], p6[q, :], ALU.mult).then_inc(par_done, 1)

            pool.wait_ge(par_ready, 1)
            mag, cos, sin, f_re, f_im = (par[:, i, :] for i in range(5))
            tt(ab_re[:, :], mag, cos, ALU.mult)
            tt(ab_im[:, :], mag, sin, ALU.mult)
            tt(nat[:, 0, :], mag, mag, ALU.mult)
            tt(pw_t[:, 0, :], cos, cos, ALU.mult)
            tt(pw_t[:, 1, :], sin, sin, ALU.mult)
            tt(nat[:, 1, :], pw_t[:, 0, :], pw_t[:, 1, :], ALU.subtract)
            tt(pw_t[:, 0, :], cos, sin, ALU.mult)
            ts(nat[:, 2, :], pw_t[:, 0, :], 2.0, None, ALU.mult, ALU.bypass)
            for i, dst in enumerate((mag2, pw_re, pw_im)):
                for qt in range(QUARTERS):
                    c = slice(qt * QPAIRS, (qt + 1) * QPAIRS)
                    link(nc.gpsimd.tensor_copy(dst[:, c].rearrange("p (i k) -> p i k", i=4),
                                               nat[:, i, c].rearrange("p (k i) -> p i k", i=4)))
            cos_s, sin_s = (t[:, :, :].rearrange("p q (m s) -> p (q m) s", s=FRAME) for t in (cos_t, sin_t))

            def square():
                tt(pw_t[:, 0, :], pw_re[:, :], pw_re[:, :], ALU.mult)
                tt(pw_t[:, 1, :], pw_im[:, :], pw_im[:, :], ALU.mult)
                tt(pw_im[:, :], pw_im[:, :], pw_re[:, :], ALU.mult)
                ts(pw_im[:, :], pw_im[:, :], 2.0, None, ALU.mult, ALU.bypass)
                tt(pw_re[:, :], pw_t[:, 0, :], pw_t[:, 1, :], ALU.subtract)

            link(nc.gpsimd.memset(cos_s[:, :, 0:1], 1.0))
            link(nc.gpsimd.memset(sin_s[:, :, 0:1], 0.0))
            link(nc.gpsimd.tensor_copy(cos_s[:, :, 1:2], pw_re[:, :].unsqueeze(2)))
            link(nc.gpsimd.tensor_copy(sin_s[:, :, 1:2], pw_im[:, :].unsqueeze(2)))
            n = 2
            while n < FRAME:
                square()
                for k0 in range(0, n, GROUP_W):
                    k1 = min(n, k0 + GROUP_W)
                    wr = pw_re[:, :].unsqueeze(2).to_broadcast([P, PAIRS, k1 - k0])
                    wi = pw_im[:, :].unsqueeze(2).to_broadcast([P, PAIRS, k1 - k0])
                    t1, t2 = tmp1[:, :, 0:k1 - k0], tmp2[:, :, 0:k1 - k0]
                    tt(t1, cos_s[:, :, k0:k1], wr, ALU.mult)
                    tt(t2, sin_s[:, :, k0:k1], wi, ALU.mult)
                    tt(cos_s[:, :, n + k0:n + k1], t1, t2, ALU.subtract)
                    tt(t1, cos_s[:, :, k0:k1], wi, ALU.mult)
                    tt(t2, sin_s[:, :, k0:k1], wr, ALU.mult)
                    tt(sin_s[:, :, n + k0:n + k1], t1, t2, ALU.add)
                n *= 2
            square()
            tt(turn_re[:, :], pw_re[:, :], mag2[:, :], ALU.mult)
            tt(turn_im[:, :], pw_im[:, :], mag2[:, :], ALU.mult)
            tt(pw_t[:, 0, :], ab_re[:, :], f_re, ALU.mult)
            tt(pw_t[:, 1, :], ab_im[:, :], f_im, ALU.mult)
            tt(af_re[:, :], pw_t[:, 0, :], pw_t[:, 1, :], ALU.subtract)
            tt(pw_t[:, 0, :], ab_re[:, :], f_im, ALU.mult)
            tt(pw_t[:, 1, :], ab_im[:, :], f_re, ALU.mult)
            tt(af_im[:, :], pw_t[:, 0, :], pw_t[:, 1, :], ALU.add)
            pool.wait_ge(bc_landed, 32)
            for i, (fr, fi) in enumerate(((f_re, f_im), (af_re[:, :], af_im[:, :]))):
                fr, fi = (f.unsqueeze(2).to_broadcast([P, PAIRS, GROUP_W]) for f in (fr, fi))
                for dst, x, y, op in ((bb[i][0], b_re, b_im, ALU.subtract), (bb[i][1], b_im, b_re, ALU.add)):
                    tt(tmp1[:, :, :], x[:, :, :], fr, ALU.mult)
                    tt(tmp2[:, :, :], y[:, :, :], fi, ALU.mult)
                    if dst is bb[1][1]:
                        pool.wait_ge(decayed, HEADS)
                    link(nc.gpsimd.memset(dst[:, :, :], 0.0))
                    for g in range(2):
                        h = slice(STATES * g, STATES * (g + 1))
                        ins = nc.gpsimd.tensor_tensor(dst[h, :, GROUP_W * g:GROUP_W * (g + 1)], tmp1[h, :, :], tmp2[h, :, :], op)
                        if dst is bb[1][1] and g == 1:
                            ins.then_inc(setup_done, 1)
                        else:
                            link(ins)
            pool.dma_start(router[:, :, :], A["moe_router"][0].rearrange("(k p) e -> p k e", p=P)).then_inc(moe_landed, 16)

            pool.wait_ge(setup_done, 1)
            pool.wait_ge(used, S5_U0)
            for dst, name in zip(c_in, ("s5_c_re", "s5_c_im")):
                pool.dma_start(dst[:, :, :], A[name][0].rearrange("(t g) n p -> (g n) t p", g=8)).then_inc(cin_landed, 16)
            pool.wait_ge(cin_landed, 32)
            for dst, src, sign in ((cc[0], c_in[0], 1.0), (cc[1], c_in[1], -1.0)):
                for g, col in ((0, C_EVEN), (1, C_ODD)):
                    nc.gpsimd.tensor_scalar(dst[:, :, STATES * g:STATES * (g + 1)], src[:, :, :], cst[:, col:col + 1], sign,
                                            ALU.mult, ALU.mult).then_inc(c_padded, 1)
            pool.wait_ge(bt_done, 2)
            nc.gpsimd.memset(direct[:, :, :], 0.0).then_inc(zero_ready, 1)
            pool.wait_ge(c_padded, 4)
            pool.wait_ge(ct_copied, 2)
            for half in range(2):
                k = slice(half * KT // 2, (half + 1) * KT // 2)
                m = slice(half * PAIRS // 2, (half + 1) * PAIRS // 2)
                ar, ai = (a[:, m].unsqueeze(2).to_broadcast([P, PAIRS // 2, 32]) for a in (ab_re, ab_im))

                def pairs(t):
                    return t[:, k, :].rearrange("p k (i n) -> p (k i) n", i=4)
                t1, t2 = (t[:, :, :].rearrange("p m n -> p (m n)").rearrange("p (m n) -> p m n", n=32) for t in (tmp1, tmp2))
                for dst, x, y, op in ((ct[1][0], ct[0][0], ct[0][1], ALU.add), (ct[1][1], ct[0][1], ct[0][0], ALU.subtract)):
                    tt(t1, pairs(x), ar, ALU.mult)
                    tt(t2, pairs(y), ai, ALU.mult)
                    nc.gpsimd.tensor_tensor(pairs(dst), t1, t2, op).then_inc(ct1_ready, 1)
                    pool.wait_ge(ct1_ready, 2 * half + (1 if dst is ct[1][0] else 2))
            pool.wait_ge(used, S5_U0 + S5_IN_UNITS)
            mag_s = mag_t[:, :, :].rearrange("p q (m s) -> p (q m) s", s=FRAME)
            link(nc.gpsimd.tensor_copy(mag_s, mag2[:, :].unsqueeze(2).to_broadcast([P, PAIRS, FRAME])))
            nc.gpsimd.memset(mag_s[:, :, 0:1], 0.0).then_inc(mag_ready, 1)

            pool.wait_ge(st_im_ready, QUARTERS)
            pool.dma_start(gain_row[:, :], A["norm_ffn"][1:2, :].to_broadcast([P, D])).then_inc(moe_landed, 16)
            pool.wait_ge(used, MOE_U0)
            pool.dma_start(final_gain[:, :], A["norm_final"].unsqueeze(0).to_broadcast([P, D])).then_inc(fin_landed, 16)

        @block.scalar
        def _(act):
            n_self = [0]

            def link(ins):
                n_self[0] += 1
                ins.then_inc(act_self, 1)
                act.wait_ge(act_self, n_self[0])

            def copy(o, i):
                return nc.scalar.activation(o, i, ACT.Copy)

            act.dma_start(cst[:, :], consts).then_inc(c_landed, 16)
            act.dma_start(gain_rows[0:16, :], A["norm_mix"].rearrange("l (k p) -> (l k) p", p=P)).then_inc(g_landed, 16)
            act.dma_start(gain_rows[16:32, :], A["norm_ffn"].rearrange("l (k p) -> (l k) p", p=P)).then_inc(g_landed, 16)
            act.dma_start(gain_rows[32:48, :], A["ret_gn"][0].rearrange("(k p) -> k p", p=P)).then_inc(g_landed, 16)
            act.dma_start(gain_rows[48:56, :], A["s5_d"][0].rearrange("(k p) -> k p", p=P)).then_inc(g_landed, 16)

            def split_hi(n, e=None):
                act.wait_ge(landed[n % RAW], count(16 * (n // RAW + 1), e, 16 * (FFN_UNITS // RAW)))
                if n >= SPLIT:
                    act.wait_ge(used, count(n - SPLIT + 1, e, FFN_UNITS))
                copy(w_hi[:, n % SPLIT, :], raw[:, n % RAW, :]).then_inc(hi_ready, 1)

            def norm_rows(i):
                if i == 0:
                    act.wait_ge(x_landed, 16)
                    act.wait_ge(c_landed, 16)
                else:
                    act.wait_ge(resid_ready, i)
                nc.scalar.activation(hn[:, 0, :], resid[:, 0, :], ACT.Square, accum_out=ssq[:, 0:1]).then_inc(ssq0_done, 1)
                act.wait_ge(ssq0_done, i + 1)
                act.wait_ge(ssq1_done, i + 1)
                nc.scalar.activation(std[:, :], ssq[:, :], ACT.Sqrt, scale=1.0 / D, bias=eps).then_inc(std_done, 1)
                if i < 3:
                    act.wait_ge(rstd_done, i + 1)
                    nc.scalar.activation(hn[:, 1, :], resid[:, 1, :], ACT.Copy, scale=rstd[:, 1:2]).then_inc(hn1_ready, 1)

            def norm_split(i):
                gain = (gains[:, 0:KT], gains[:, 2 * KT:3 * KT], gains[:, KT:2 * KT])[i]
                act.wait_ge(gains_ready, 1)
                for bank in range(KT // 2):
                    act.wait_ge(xt_done, KT // 2 * i + bank + 1)
                    for j in range(2):
                        kt = 2 * bank + j
                        ins = nc.scalar.activation(xt_hi[:, kt, :], PS[:, bank, j * SEQ:(j + 1) * SEQ], ACT.Copy,
                                                   scale=gain[:, kt:kt + 1])
                    ins.then_inc(xhi_ready, 1)

            def ffn(u0, s0, tts, e=None, each=None):
                silu_at = {ffn_first(s) + 4: s for s in range(STEPS)}
                evac_at = {7 if s == 0 else 41 if s == STEPS - 1 else 6 * s + 6: s for s in range(STEPS)}
                for i in range(FFN_UNITS):
                    if i in silu_at:
                        s = s0 + silu_at[i]
                        act.wait_ge(used, count(u0 + ffn_first(silu_at[i]) + 2, e, FFN_UNITS))
                        if s:
                            act.wait_ge(mult_done, count(s, e, STEPS))
                        nc.scalar.activation(gated[:, 0:tts, :], PS[:, 0:tts, :], ACT.Silu).then_inc(silu_done, 1)
                    if i in evac_at:
                        s = s0 + evac_at[i]
                        act.wait_ge(act_t_done, count(s + 1, e, STEPS))
                        copy(ht_hi[evac_at[i] % 2][:, 0:tts, :, :],
                             PS[:, tts:2 * tts, :].rearrange("p t (f c) -> p t f c", f=FT)).then_inc(act_hi, 1)
                    if each:
                        each(i)
                    if e is None and i < 3:
                        continue
                    split_hi(u0 + i, e)

            norm_rows(0)
            act.wait_ge(gains_t, 1)
            copy(gains[:, :], PS[:, 7, 0:7 * KT]).then_inc(gains_ready, 1)
            act.wait_ge(a_landed, 48)
            q = slice(0, PAIRS)
            nc.scalar.activation(dt[q, :], log_step[q, :], ACT.Exp).then_inc(dt_done, 1)
            norm_split(0)
            split_hi(0)
            split_hi(1)

            def evac_yt(h):
                act.wait_ge(yt_done, h + 1)
                for ft in range(FT):
                    ins = nc.scalar.activation(ht_hi[0][:, :, ft, :], PS[:, 2:4, ft * P:(ft + 1) * P], ACT.Copy,
                                               scale=g_gn[:, h * FT + ft:h * FT + ft + 1])
                ins.then_inc(yt_hi, 1)

            for h in range(HEADS):
                f0 = ret_first(h)
                last = RET_UNITS if h == HEADS - 1 else ret_first(h + 1)
                for n in range(f0, last):
                    if n == 3:
                        act.wait_ge(ar_done, 1)
                        nc.scalar.activation(par_in[q, 0, :], p1[q, :], ACT.Exp).then_inc(mag_done, 1)
                        act.wait_ge(angle_done, 1)
                        nc.scalar.activation(par_in[q, 1, :], p2[q, :], ACT.Sin, scale=0.5).then_inc(sin_done, 1)
                        nc.scalar.activation(par_in[q, 2, :], p2[q, :], ACT.Sin).then_inc(sin_done, 1)
                    if h and n == f0 + 1:
                        act.wait_ge(bn_done, h)
                        nc.scalar.activation(hstd[:, :], bn_a[:, :, 1], ACT.Sqrt, bias=eps).then_inc(hstd_done, 1)
                    if h and n == f0 + 3:
                        evac_yt(h - 1)
                    if n == f0 + 4:
                        act.wait_ge(used, f0 + 2)
                        copy(qk_t[:, :, :, :], PS[:, 0:2, :].rearrange("p a (b c) -> p a b c", b=2)).then_inc(qk_copied, 1)
                    if h and n == f0:
                        act.wait_ge(used, ret_first(h - 1) + 6)
                        if h > 1:
                            act.wait_ge(y_normed, h - 1)
                        nc.scalar.activation(gated[:, :, :], PS[:, 0:2, :], ACT.Silu).then_inc(g_silu, 1)
                    if h == 1 and n == f0 + 2:
                        act.wait_ge(par_t, 1)
                        copy(par[:, :, :], PS[:, 4, 0:5 * PAIRS].rearrange("p (a m) -> p a m", a=5)).then_inc(par_ready, 1)
                    if h == HEADS - 1 and n == f0 + 8:
                        act.wait_ge(used, f0 + 6)
                        act.wait_ge(y_normed, h)
                        nc.scalar.activation(gated[:, :, :], PS[:, 0:2, :], ACT.Silu).then_inc(g_silu, 1)
                    if h == HEADS - 1 and n == f0 + 9:
                        act.wait_ge(bn_done, HEADS)
                        nc.scalar.activation(hstd[:, :], bn_a[:, :, 1], ACT.Sqrt, bias=eps).then_inc(hstd_done, 1)
                    if n >= 2:
                        split_hi(n)
            evac_yt(HEADS - 1)

            for i in range(2):
                split_hi(FFN_U0 + i)
            norm_rows(1)
            norm_split(1)
            split_hi(FFN_U0 + 2)
            act.wait_ge(setup_done, 1)
            ffn(FFN_U0, 0, TT)

            for i in range(2):
                split_hi(S5_U0 + i)
            norm_rows(2)
            norm_split(2)
            def evac_turned(tables, copied):
                for j, t in enumerate(tables):
                    copy(t[:, :, :], PS[:, 4 + 2 * j:6 + 2 * j, :].rearrange("p a (b c) -> p (a b) c", c=P)).then_inc(copied, 1)

            for i in range(STEP):
                act.wait_ge(bt_done, i + 1)
                evac_turned(bt[i], bt_copied)
            def copy_u(c):
                act.wait_ge(used, S5_U0 + c + 1)
                copy(u_t[:, 2 * c:2 * c + 2, :], PS[:, c, :].rearrange("p (a b) -> p a b", a=2)).then_inc(u_copied, 1)

            split_hi(S5_U0 + 2)
            copy_u(0)
            split_hi(S5_U0 + 3)
            act.wait_ge(ct_done, 1)
            evac_turned(ct[0], ct_copied)
            for c in range(1, S5_IN_UNITS):
                copy_u(c)
            act.wait_ge(zero_ready, 1)
            act.wait_ge(direct_done, 1)
            for i in range(4):
                r = slice(32 * i, 32 * i + 32)
                copy(direct[r, :, r], PS[r, 7, 0:KT * 32].rearrange("p (k n) -> p k n", k=KT)).then_inc(direct_ready, 1)
            for q in range(QUARTERS):
                if q == QUARTERS - 1:
                    act.wait_ge(st_im_ready, QUARTERS)
                    split_hi(S5_U0 + 4)
                    split_hi(S5_U0 + 5)
                k = slice(2 * q, 2 * q + 2)
                act.wait_ge(sy_added, q + 1)
                nc.scalar.activation(gelu_t[:, k, :], y_t[:, k, :], ACT.Gelu_apprx_tanh).then_inc(gelu_done, 1)
                act.wait_ge(gelu_done, q + 1)
                copy(xt_hi[:, k, :], gelu_t[:, k, :]).then_inc(xhi_ready, 1)
            act.wait_ge(sy_done, QUARTERS)
            split_hi(S5_U0 + 6)
            for n in range(7, S5_IN_UNITS + S5_OUT_UNITS):
                if n == 11:
                    act.wait_ge(used, S5_U0 + 8)
                    nc.scalar.activation(glu_gate[:, :, :], PS[:, 2:4, :], ACT.Sigmoid).then_inc(glu_sig, 1)
                split_hi(S5_U0 + n)
            act.wait_ge(used, MOE_U0)
            act.wait_ge(glu_read, 1)
            nc.scalar.activation(glu_gate[:, :, :], PS[:, 6:8, :], ACT.Sigmoid).then_inc(glu_sig, 1)

            norm_rows(3)
            act.wait_ge(hnt_done, 1)
            copy(hn_t[:, 0:4, :], PS[:, 0:2, :].rearrange("p a (b c) -> p (a b) c", c=SEQ)).then_inc(hnt_copied, 1)
            act.wait_ge(top_done, 1)
            for t in range(TT):
                nc.scalar.activation(r_exp[:, t, :], logit[:, t, :], ACT.Exp, bias=neg_top[:, t:t + 1]).then_inc(exp_done, 1)

            def gather_hi(g):
                act.wait_ge(gathered, g)
                copy(xg_hi[:, :, :], PS[:, 2:4, :].rearrange("p a (b c) -> p (a b) c", c=SLOTS)).then_inc(xg_hi_ready, 1)

            def experts(p):
                u0 = MOE_U0 + p * EXPERTS * FFN_UNITS
                gather_hi(9 * p + 1)
                with act.Fori(0, EXPERTS) as e:
                    def each(i):
                        if i == 2:
                            act.wait_ge(used, count(u0, e, FFN_UNITS))
                            copy(y_rows[:, 0:512], PS[:, 4, :]).then_inc(y0_copied, 1)
                        if i == 19:
                            act.wait_ge(put_t_done, count(8 * p + 1, e, 1))
                            copy(put_g[:, :, :], PS[:, 6, 0:2 * P].rearrange("p (a b) -> p a b", a=2)).then_inc(put_ready, 1)
                    ffn(u0, STEPS * (1 + EXPERTS * p), 1, e, each)
                    gather_hi(count(9 * p + 2, e, 1))
                act.wait_ge(used, u0 + EXPERTS * FFN_UNITS)
                copy(y_rows[:, 0:512], PS[:, 4, :]).then_inc(y0_copied, 1)

            experts(0)
            act.wait_ge(keys_done, 1)
            flag = act.value_load(over[0:1, 0:1], min_val=0, max_val=1)
            with act.If(flag > 0):
                experts(1)
            norm_rows(4)

        @block.vector
        def _(dve):
            n_self = [0]

            def link(ins):
                n_self[0] += 1
                ins.then_inc(dve_self, 1)
                dve.wait_ge(dve_self, n_self[0])

            def tt(o, a, b, op):
                return nc.vector.tensor_tensor(o, a, b, op)

            def split_lo(n, e=None):
                dve.wait_ge(hi_ready, count(n + 1, e, FFN_UNITS))
                tt(w_lo[:, n % SPLIT, :], raw[:, n % RAW, :], w_hi[:, n % SPLIT, :].bitcast(F32),
                   ALU.subtract).then_inc(lo_ready, 1)

            def norm_rows(i):
                if i == 0:
                    dve.wait_ge(x_landed, 16)
                else:
                    dve.wait_ge(resid_ready, i)
                nc.vector.scalar_tensor_tensor(out=hn[:, 1, :], in0=resid[:, 1, :], scalar=1.0, in1=resid[:, 1, :],
                                               op0=ALU.mult, op1=ALU.mult, accum_out=ssq[:, 1:2]).then_inc(ssq1_done, 1)
                dve.wait_ge(std_done, i + 1)
                nc.vector.reciprocal(rstd[:, :], std[:, :]).then_inc(rstd_done, 1)
                dve.wait_ge(rstd_done, i + 1)
                if i < 3:
                    nc.vector.tensor_scalar(hn[:, 0, :], resid[:, 0, :], rstd[:, 0:1], None, ALU.mult).then_inc(hn0_ready, 1)

            def norm_split(i):
                gain = (gains[:, 0:KT], gains[:, 2 * KT:3 * KT], gains[:, KT:2 * KT])[i]
                dve.wait_ge(gains_ready, 1)
                for bank in range(KT // 2):
                    dve.wait_ge(xhi_ready, KT // 2 * i + bank + 1)
                    for j in range(2):
                        kt = 2 * bank + j
                        ins = nc.vector.scalar_tensor_tensor(
                            out=xt_lo[:, kt, :], in0=PS[:, bank, j * SEQ:(j + 1) * SEQ], scalar=gain[:, kt:kt + 1],
                            in1=xt_hi[:, kt, :].bitcast(F32), op0=ALU.mult, op1=ALU.subtract)
                    ins.then_inc(xlo_ready, 1)

            def ffn(u0, s0, tts, e=None, each=None):
                mult_at = {ffn_first(s) + 6: s for s in range(STEPS)}
                evac_at = {7 if s == 0 else 41 if s == STEPS - 1 else 6 * s + 6: s for s in range(STEPS)}
                for i in range(FFN_UNITS):
                    if i in mult_at:
                        s = s0 + mult_at[i]
                        dve.wait_ge(silu_done, count(s + 1, e, STEPS))
                        dve.wait_ge(used, count(u0 + ffn_first(mult_at[i]) + 4, e, FFN_UNITS))
                        if s:
                            dve.wait_ge(act_t_done, count(s, e, STEPS))
                        tt(act_rows[:, 0:tts, :], gated[:, 0:tts, :], PS[:, tts:2 * tts, :], ALU.mult).then_inc(mult_done, 1)
                    if i in evac_at:
                        s = s0 + evac_at[i]
                        dve.wait_ge(act_hi, count(s + 1, e, STEPS))
                        b = evac_at[i] % 2
                        for t in range(tts):
                            ins = tt(ht_lo[b][:, t, :, :], PS[:, tts + t, :].rearrange("p (f c) -> p f c", f=FT),
                                     ht_hi[b][:, t, :, :].bitcast(F32), ALU.subtract)
                        ins.then_inc(act_lo, 1)
                    if each:
                        each(i)
                    if e is None and i < 3:
                        continue
                    split_lo(u0 + i, e)

            def add_out():
                for t in range(TT):
                    ins = tt(resid[:, t, :], resid[:, t, :], PS[:, 4 + 2 * t:6 + 2 * t, :].rearrange("p a b -> p (a b)"), ALU.add)
                ins.then_inc(resid_ready, 1)

            norm_rows(0)
            norm_split(0)
            split_lo(0)
            split_lo(1)

            def decay(h):
                dve.wait_ge(scores_done, h + 1)
                c = C_DECAY + h * SEQ
                tt(scores[:, 0:SEQ], PS[:, 2, 0:SEQ], cst[:, c:c + SEQ], ALU.mult)
                tt(scores[:, SEQ:SEQ + P], PS[:, 2, SEQ:SEQ + P], cst[:, c:c + P], ALU.mult).then_inc(decayed, 1)

            def group_norm(h):
                dve.wait_ge(y_done, h + 1)
                for t in range(TT):
                    link(nc.vector.bn_stats(bn_s[:, t, :], PS[:, 3 - t, :]))
                for t in range(TT):
                    ins = nc.vector.bn_aggr(bn_a[:, t, :], bn_s[:, t, :])
                ins.then_inc(bn_done, 1)
                dve.wait_ge(hstd_done, h + 1)
                link(nc.vector.reciprocal(hrstd[:, :], hstd[:, :]))
                for t in range(TT):
                    link(nc.vector.tensor_scalar(act_rows[:, t, :], PS[:, 3 - t, :], bn_a[:, t, 0:1], hrstd[:, t:t + 1],
                                                 ALU.subtract, ALU.mult))
                dve.wait_ge(g_silu, h + 1)
                tt(act_rows[:, :, :], act_rows[:, :, :], gated[:, :, :], ALU.mult).then_inc(y_normed, 1)

            def evac_yt(h):
                dve.wait_ge(yt_hi, h + 1)
                for ft in range(FT):
                    ins = nc.vector.scalar_tensor_tensor(
                        out=ht_lo[0][:, :, ft, :], in0=PS[:, 2:4, ft * P:(ft + 1) * P], scalar=g_gn[:, h * FT + ft:h * FT + ft + 1],
                        in1=ht_hi[0][:, :, ft, :].bitcast(F32), op0=ALU.mult, op1=ALU.subtract)
                ins.then_inc(yt_lo, 1)

            for h in range(HEADS):
                f0 = ret_first(h)
                last = RET_UNITS if h == HEADS - 1 else ret_first(h + 1)
                for n in range(f0, last):
                    if n == 3:
                        dve.wait_ge(den_done, 1)
                        nc.vector.reciprocal(p6[0:PAIRS, :], p4[0:PAIRS, :]).then_inc(rden_done, 1)
                    if h and n == f0:
                        decay(h - 1)
                    if h and n == f0 + 1:
                        group_norm(h - 1)
                    if h and n == f0 + 3:
                        evac_yt(h - 1)
                    if n == f0 + 6 and h:
                        dve.wait_ge(used, f0 + 4)
                        nc.vector.tensor_copy(v_rows[:, :, :], PS[:, 2:4, :]).then_inc(v_copied, 1)
                    if h == HEADS - 1 and n == f0 + 8:
                        decay(h)
                    if h == HEADS - 1 and n == f0 + 9:
                        group_norm(h)
                    if n >= 2:
                        split_lo(n)
                if h == 0:
                    dve.wait_ge(used, f0 + 4)
                    nc.vector.tensor_copy(v_rows[:, :, :], PS[:, 2:4, :]).then_inc(v_copied, 1)
            evac_yt(HEADS - 1)

            for i in range(2):
                split_lo(FFN_U0 + i)
            dve.wait_ge(used, FFN_U0)
            add_out()
            norm_rows(1)
            norm_split(1)
            split_lo(FFN_U0 + 2)
            ffn(FFN_U0, 0, TT)

            for i in range(2):
                split_lo(S5_U0 + i)
            dve.wait_ge(used, S5_U0)
            add_out()
            norm_rows(2)
            norm_split(2)
            for i in range(2, 4):
                split_lo(S5_U0 + i)

            def add_y(q):
                dve.wait_ge(sy_done, q + 1)
                for j in range(2):
                    k = 2 * q + j
                    ins = nc.vector.scalar_tensor_tensor(out=y_t[:, k, :], in0=u_t[:, k, :], scalar=d_skip[:, k:k + 1],
                                                         in1=PS[:, 4 + q, j * SEQ:(j + 1) * SEQ], op0=ALU.mult, op1=ALU.add)
                ins.then_inc(sy_added, 1)

            def gelu_lo(q):
                k = slice(2 * q, 2 * q + 2)
                dve.wait_ge(xhi_ready, 3 * (KT // 2) + q + 1)
                tt(xt_lo[:, k, :], gelu_t[:, k, :], xt_hi[:, k, :].bitcast(F32), ALU.subtract).then_inc(xlo_ready, 1)

            def by_row_tile(t):
                return t.rearrange("p h (i x) -> p h i x", i=4)

            def table(t, q):
                return t[:, q, :].rearrange("p (i x) -> p i x", i=4).unsqueeze(1).to_broadcast([P, FRAMES, 4, 2 * FRAME])

            re, im, tmp = by_row_tile(scan[:, 0]), by_row_tile(scan[:, 1]), by_row_tile(scan_tmp[:, :, :])
            bu_re, bu_im = (PS[:, 0:4, j * 256:(j + 1) * 256].rearrange("p i (h x) -> p h i x", h=FRAMES) for j in range(2))
            dve.wait_ge(u_copied, S5_IN_UNITS)
            for q in range(QUARTERS):
                cos, sin = table(cos_t, q), table(sin_t, q)
                dve.wait_ge(bu_done, q + 1)
                tt(re, bu_re, cos, ALU.mult)
                link(tt(im, bu_im, sin, ALU.mult))
                link(tt(re, re, im, ALU.add))
                tt(im, bu_im, cos, ALU.mult)
                tt(tmp, bu_re, sin, ALU.mult).then_inc(bu_read, 1)
                dve.wait_ge(bu_read, q + 1)
                link(tt(im, im, tmp, ALU.subtract))
                if q == 0:
                    dve.wait_ge(mag_ready, 1)
                for f in range(FRAMES):
                    first = scan[:, :, f, :].rearrange("p j (m s) -> p j m s", s=FRAME)[:, :, :, 0]
                    if f:
                        last = scan[:, :, f - 1, :].rearrange("p j (m s) -> p j m s", s=FRAME)[:, :, :, FRAME - 1]
                        for j, turn in enumerate((turn_re, turn_im)):
                            ins = tt(car[:, j], last, turn[:, q * QPAIRS:(q + 1) * QPAIRS].unsqueeze(1).to_broadcast(
                                [P, 2, QPAIRS]), ALU.mult)
                        link(ins)
                        link(tt(first, first, car[:, 0], ALU.add))
                        tt(first[:, 0], first[:, 0], car[:, 1, 1], ALU.subtract)
                        link(tt(first[:, 1], first[:, 1], car[:, 1, 0], ALU.add))
                    for j in range(2):
                        ins = nc.vector.tensor_tensor_scan(scan[:, j, f, :], mag_t[:, q, :], scan[:, j, f, :], 0.0,
                                                           ALU.mult, ALU.add)
                    link(ins)
                if q >= 2:
                    dve.wait_ge(sy_done, q - 1)
                x_re, x_im = (by_row_tile(states[q % 2][:, j]) for j in range(2))
                tt(x_re, re, cos, ALU.mult)
                link(tt(tmp, im, sin, ALU.mult))
                tt(x_re, x_re, tmp, ALU.subtract).then_inc(st_re_ready, 1)
                tt(x_im, im, cos, ALU.mult)
                dve.wait_ge(st_re_ready, q + 1)
                link(tt(tmp, re, sin, ALU.mult))
                tt(x_im, x_im, tmp, ALU.add).then_inc(st_im_ready, 1)
                if q:
                    add_y(q - 1)
            gelu_lo(0)
            gelu_lo(1)
            dve.wait_ge(st_im_ready, QUARTERS)
            split_lo(S5_U0 + 4)
            split_lo(S5_U0 + 5)
            add_y(QUARTERS - 1)
            gelu_lo(2)
            gelu_lo(3)
            split_lo(S5_U0 + 6)

            def glu(dh):
                dve.wait_ge(glu_sig, dh + 1)
                link(tt(glu_out[:, :, :], glu_gate[:, :, :], PS[:, 4 * dh:4 * dh + 2, :], ALU.mult))
                return tt(resid[:, :, dh * 512:dh * 512 + 512], resid[:, :, dh * 512:dh * 512 + 512],
                          glu_out[:, :, :], ALU.add)

            for n in range(7, S5_IN_UNITS + S5_OUT_UNITS):
                if n == 11:
                    glu(0).then_inc(glu_read, 1)
                split_lo(S5_U0 + n)
            dve.wait_ge(glu_read, 1)
            glu(1).then_inc(resid_ready, 1)

            norm_rows(3)
            dve.wait_ge(moe_landed, 32)
            dve.wait_ge(ssq0_done, 4)
            for t, ready in enumerate((hn0_ready, hn1_ready)):
                nc.vector.scalar_tensor_tensor(out=hn[:, t, :], in0=resid[:, t, :], scalar=rstd[:, t:t + 1], in1=gain_row[:, :],
                                               op0=ALU.mult, op1=ALU.mult).then_inc(ready, 1)
            dve.wait_ge(hnt_done, 2)
            nc.vector.tensor_copy(hn_t[:, 4:8, :], PS[:, 2:4, :].rearrange("p a (b c) -> p (a b) c", c=SEQ)).then_inc(hnt_copied, 1)
            dve.wait_ge(logits_done, 1)
            link(nc.vector.tensor_copy(logit[:, :, :], PS[:, 6, 0:TT * EXPERTS].rearrange("p (t e) -> p t e", t=TT)))
            for t in range(TT):
                link(nc.vector.max(top[:, t, :], logit[:, t, :]))
            nc.vector.tensor_scalar(neg_top[:, :], top[:, :, 0], -1.0, None, ALU.mult).then_inc(top_done, 1)
            for t in range(TT):
                second = top[:, t, 1:2]
                nc.vector.tensor_scalar(r_gt[:, t, :], logit[:, t, :], second, None, ALU.is_gt)
                link(nc.vector.tensor_scalar(r_eq[:, t, :], logit[:, t, :], second, None, ALU.is_equal))
                nc.vector.tensor_tensor_scan(r_cum[:, t, :], ones[:, 0:EXPERTS], r_eq[:, t, :], 0.0, ALU.mult, ALU.add)
            link(nc.vector.tensor_reduce(r_n[:, :], r_gt[:, :, :], AX_X, ALU.add))
            link(nc.vector.tensor_scalar(r_n[:, :], r_n[:, :], -1.0, 2.0, ALU.mult, ALU.add))
            for t in range(TT):
                link(nc.vector.tensor_scalar(r_cum[:, t, :], r_cum[:, t, :], r_n[:, t:t + 1], None, ALU.is_le))
            link(tt(r_eq[:, :, :], r_eq[:, :, :], r_cum[:, :, :], ALU.mult))
            tt(chosen[:, :, :], r_gt[:, :, :], r_eq[:, :, :], ALU.add).then_inc(chosen_done, 1)
            dve.wait_ge(chosen_done, 1)
            dve.wait_ge(exp_done, TT)
            link(tt(r_exp[:, :, :], r_exp[:, :, :], chosen[:, :, :], ALU.mult))
            link(nc.vector.tensor_reduce(r_n[:, :], r_exp[:, :, :], AX_X, ALU.add))
            link(nc.vector.reciprocal(r_n[:, :], r_n[:, :]))
            for t in range(TT):
                link(nc.vector.tensor_scalar(gate_w[:, t, :], r_exp[:, t, :], r_n[:, t:t + 1], None, ALU.mult))
            dve.wait_ge(rank_done, 1)
            link(nc.vector.tensor_scalar(r_cum[:, :, :], PS[:, 6, 32:32 + TT * EXPERTS].rearrange("p (t e) -> p t e", t=TT),
                                         1.0, None, ALU.add))
            for b in range(2):
                link(nc.vector.memset(key[b][:, :, :], -1.0))
            link(tt(r_cum[:, :, :], r_cum[:, :, :], chosen[:, :, :], ALU.mult))
            link(nc.vector.tensor_scalar(key[0][:, :, 0:EXPERTS], r_cum[:, :, :], 1.0, None, ALU.subtract))
            link(nc.vector.tensor_scalar(key[1][:, :, 0:EXPERTS], r_cum[:, :, :], 1.0 + SLOTS, None, ALU.subtract))
            link(nc.vector.tensor_reduce(most[:, :], PS[:, 6, 64:64 + EXPERTS], AX_X, ALU.max))
            link(nc.vector.tensor_scalar(most[:, :], most[:, :], float(SLOTS), None, ALU.is_gt))
            nc.vector.tensor_copy(over[:, :], most[:, :]).then_inc(keys_done, 1)
            dve.wait_ge(keys_done, 1)
            link(nc.vector.memset(PS[:, 4, :], 0.0))
            link(nc.vector.memset(PS[:, 5, :], 0.0))

            def make_pick(b, col):
                for t in range(TT):
                    ins = nc.vector.tensor_scalar(pick[:, t, :], iota, key[b][:, t, col], None, ALU.is_equal)
                ins.then_inc(pick_ready, 1)

            def gather_lo(g):
                dve.wait_ge(xg_hi_ready, g)
                tt(xg_lo[:, :, :], PS[:, 2:4, :].rearrange("p a (b c) -> p (a b) c", c=SLOTS), xg_hi[:, :, :].bitcast(F32),
                   ALU.subtract).then_inc(xg_lo_ready, 1)

            def add_scattered(n):
                dve.wait_ge(scattered, n)
                tt(resid[:, 0, :], resid[:, 0, :], PS[:, 2:4, :].rearrange("p a b -> p (a b)"), ALU.add)
                tt(resid[:, 1, :], resid[:, 1, :], PS[:, 6:8, :].rearrange("p a b -> p (a b)"), ALU.add).then_inc(scatter_added, 1)

            def experts(p):
                u0 = MOE_U0 + p * EXPERTS * FFN_UNITS
                nc.vector.memset(put_g[:, :, :], 0.0).then_inc(put_ready, 1)
                make_pick(p, slice(0, 1))
                gather_lo(9 * p + 1)
                with dve.Fori(0, EXPERTS) as e:
                    def each(i):
                        if i == 2:
                            dve.wait_ge(used, count(u0, e, FFN_UNITS))
                            nc.vector.tensor_copy(y_rows[:, 512:1024], PS[:, 5, :]).then_inc(y1_copied, 1)
                            make_pick(p, bass.ds(e + 1, 1))
                        if i == 8:
                            add_scattered(count(9 * p + 1, e, 1))
                        if i == 10:
                            for t in range(TT):
                                ins = nc.vector.tensor_scalar(pick_g[:, t, :], iota, key[p][:, t, bass.ds(e, 1)],
                                                              gate_w[:, t, bass.ds(e, 1)], ALU.is_equal, ALU.mult)
                            ins.then_inc(pick_g_ready, 1)
                    ffn(u0, STEPS * (1 + EXPERTS * p), 1, e, each)
                    gather_lo(count(9 * p + 2, e, 1))
                dve.wait_ge(used, u0 + EXPERTS * FFN_UNITS)
                nc.vector.tensor_copy(y_rows[:, 512:1024], PS[:, 5, :]).then_inc(y1_copied, 1)
                add_scattered(9 * p + 9)
                dve.wait_ge(scatter_added, 9 * p + 9)

            experts(0)
            flag = dve.value_load(over[0:1, 0:1], min_val=0, max_val=1)
            with dve.If(flag > 0):
                experts(1)
            nc.vector.memset(ssq[:, :], 0.0).then_inc(resid_ready, 1)
            norm_rows(4)
            dve.wait_ge(ssq0_done, 5)
            dve.wait_ge(fin_landed, 16)
            for t in range(TT):
                ins = nc.vector.scalar_tensor_tensor(out=hn[:, t, :], in0=resid[:, t, :], scalar=rstd[:, t:t + 1],
                                                     in1=final_gain[:, :], op0=ALU.mult, op1=ALU.mult)
            ins.then_inc(out_ready, 1)

        @block.tensor
        def _(pe):
            def mm(o, l, r, start, stop):
                return nc.tensor.matmul(o, l, r, start=start, stop=stop)

            def split_ready(n, e=None):
                pe.wait_ge(lo_ready, count(n + 1, e, FFN_UNITS))

            def product3(o, l_hi, l_lo, r_hi, r_lo, start, stop):
                mm(o, l_hi, r_hi, start, False)
                mm(o, l_hi, r_lo, False, False)
                return mm(o, l_lo, r_hi, False, stop)

            def rows_unit(n, half, banks, x_hi, x_lo, e=None):
                split_ready(n, e)
                hi = w_hi[:, n % SPLIT, :].rearrange("p (k n) -> p k n", k=4)
                lo = w_lo[:, n % SPLIT, :].rearrange("p (k n) -> p k n", k=4)
                for k in range(4):
                    kt = 4 * half + k
                    for t, bank in enumerate(banks):
                        cols = slice(t * P, (t + 1) * P)
                        ins = product3(PS[:, bank, :], x_hi[:, kt, cols], x_lo[:, kt, cols], hi[:, k, :], lo[:, k, :],
                                       kt == 0, kt == KT - 1)
                ins.then_inc(used, 1)

            def cols_unit(n, bank):
                split_ready(n)
                hi = w_hi[:, n % SPLIT, :].rearrange("p (k n) -> p k n", k=KT)
                lo = w_lo[:, n % SPLIT, :].rearrange("p (k n) -> p k n", k=KT)
                for j in range(2):
                    o = PS[:, bank, j * SEQ:(j + 1) * SEQ]
                    for kt in range(KT):
                        c = slice(j * P, (j + 1) * P)
                        mm(o, hi[:, kt, c], xt_hi[:, kt, :], kt == 0, False)
                        mm(o, hi[:, kt, c], xt_lo[:, kt, :], False, False)
                        ins = mm(o, lo[:, kt, c], xt_hi[:, kt, :], False, kt == KT - 1)
                ins.then_inc(used, 1)

            def out_unit(n, half, tts, a_hi, a_lo, first, last, e=None):
                split_ready(n, e)
                hi = w_hi[:, n % SPLIT, :].rearrange("p (k n) -> p k n", k=2)
                lo = w_lo[:, n % SPLIT, :].rearrange("p (k n) -> p k n", k=2)
                for k in range(2):
                    ft = 2 * half + k
                    for t in range(tts):
                        for dh in range(2):
                            c = slice(dh * 512, dh * 512 + 512)
                            ins = product3(PS[:, out_bank(t, dh), :], a_hi[:, t, ft, :], a_lo[:, t, ft, :],
                                           hi[:, k, c], lo[:, k, c], first and ft == 0, last and ft == FT - 1)
                ins.then_inc(used, 1)

            def transposes(i):
                pe.wait_ge(hn0_ready, i + 1)
                pe.wait_ge(hn1_ready, i + 1)
                for kt in range(KT):
                    for t in range(TT):
                        c = kt % 2 * SEQ + t * P
                        ins = nc.tensor.transpose(PS[:, kt // 2, c:c + P], hn[:, t, kt * P:(kt + 1) * P], ident)
                    yield kt, ins

            def norm(i):
                for kt, ins in transposes(i):
                    if kt % 2:
                        ins.then_inc(xt_done, 1)
                pe.wait_ge(xlo_ready, KT // 2 * (i + 1))

            def turn_rows(banks):
                for t, bank in enumerate(banks):
                    for ft in range(FT):
                        ins = nc.tensor.transpose(PS[:, bank, ft * P:(ft + 1) * P],
                                                  act_rows[:, t, ft * P:(ft + 1) * P], ident)
                return ins

            def ffn(u0, s0, tts, x_hi, x_lo, e=None, after_up0=None, each=None, before_last=None):
                def turn(s):
                    pe.wait_ge(mult_done, count(s0 + s + 1, e, STEPS))
                    turn_rows(up_banks(tts)).then_inc(act_t_done, 1)

                def down(s, half, i):
                    if half == 0:
                        pe.wait_ge(act_lo, count(s0 + s + 1, e, STEPS))
                    out_unit(u0 + i, half, tts, ht_hi[s % 2], ht_lo[s % 2], s == 0, s == STEPS - 1, e)

                for s in range(STEPS):
                    f0 = ffn_first(s)
                    if s0 + s:
                        pe.wait_ge(silu_done, count(s0 + s, e, STEPS))
                    for half in range(2):
                        rows_unit(u0 + f0 + half, half, gate_banks(tts), x_hi, x_lo, e)
                    if s0 + s:
                        pe.wait_ge(act_lo, count(s0 + s, e, STEPS))
                    for half in range(2):
                        rows_unit(u0 + f0 + 2 + half, half, up_banks(tts), x_hi, x_lo, e)
                    if s == 0:
                        if after_up0:
                            after_up0()
                        turn(0)
                        continue
                    down(s - 1, 0, f0 + 4)
                    turn(s)
                    if each:
                        each(s)
                    down(s - 1, 1, f0 + 5)
                if before_last:
                    before_last()
                down(STEPS - 1, 0, FFN_UNITS - 2)
                down(STEPS - 1, 1, FFN_UNITS - 1)

            pe.wait_ge(c_landed, 16)
            pe.wait_ge(g_landed, 64)
            nc.tensor.transpose(PS[:, 7, 0:7 * KT], gain_rows[0:7 * KT, :],
                                cst[0:7 * KT, C_IDENT:C_IDENT + 7 * KT]).then_inc(gains_t, 1)
            norm(0)

            def turn_y(h):
                pe.wait_ge(y_normed, h + 1)
                turn_rows([2, 3]).then_inc(yt_done, 1)

            def head_out(h, half, n):
                if half == 0:
                    pe.wait_ge(yt_lo, h + 1)
                    pe.wait_ge(par_ready, 1)
                out_unit(n, half, TT, ht_hi[0], ht_lo[0], h == 0, h == HEADS - 1)

            for h in range(HEADS):
                f0 = ret_first(h)
                if h:
                    pe.wait_ge(g_silu, h)
                cols_unit(f0, 0)
                if h:
                    turn_y(h - 1)
                cols_unit(f0 + 1, 1)
                if h:
                    pe.wait_ge(yt_lo, h)
                for half in range(2):
                    rows_unit(f0 + 2 + half, half, (2, 3), xt_hi, xt_lo)
                pe.wait_ge(qk_copied, h + 1)
                for half in range(2):
                    rows_unit(f0 + 4 + half, half, (0, 1), xt_hi, xt_lo)
                pe.wait_ge(v_copied, h + 1)
                for dt_i in range(2):
                    mm(PS[:, 2, 0:SEQ], qk_t[:, 1, dt_i, 0:P], qk_t[:, 0, dt_i, :], dt_i == 0, dt_i == 1)
                for dt_i in range(2):
                    ins = mm(PS[:, 2, SEQ:SEQ + P], qk_t[:, 1, dt_i, P:SEQ], qk_t[:, 0, dt_i, P:SEQ], dt_i == 0, dt_i == 1)
                ins.then_inc(scores_done, 1)
                if h:
                    head_out(h - 1, 0, f0 + 6)
                pe.wait_ge(decayed, h + 1)
                mm(PS[:, 3, :], scores[:, 0:P], v_rows[:, 0, :], True, True)
                mm(PS[:, 2, :], scores[:, P:SEQ], v_rows[:, 0, :], True, False)
                mm(PS[:, 2, :], scores[:, SEQ:SEQ + P], v_rows[:, 1, :], False, True).then_inc(y_done, 1)
                if h:
                    head_out(h - 1, 1, f0 + 7)
                if h == 0:
                    pe.wait_ge(par_done, 1)
                    for i in range(5):
                        ins = nc.tensor.transpose(PS[:, 4, i * PAIRS:(i + 1) * PAIRS], par_in[0:PAIRS, i, :],
                                                  cst[0:PAIRS, C_IDENT:C_IDENT + PAIRS])
                    ins.then_inc(par_t, 1)
            turn_y(HEADS - 1)
            for half in range(2):
                head_out(HEADS - 1, half, RET_UNITS - 2 + half)

            norm(1)
            ffn(FFN_U0, 0, TT, xt_hi, xt_lo)

            norm(2)
            pe.wait_ge(setup_done, 1)
            def turn_b(i):
                for j, src in enumerate(bb[i]):
                    for k in range(KT):
                        ins = nc.tensor.transpose(PS[:, 4 + 2 * j + k // 4, k % 4 * P:(k % 4 + 1) * P],
                                                  src[:, 4 * k:4 * k + 4, :].rearrange("p a b -> p (a b)"), ident)
                ins.then_inc(bt_done, 1)

            turn_b(0)
            cols_unit(S5_U0, 0)
            pe.wait_ge(bt_copied, 2)
            turn_b(1)
            cols_unit(S5_U0 + 1, 1)
            pe.wait_ge(bt_copied, 4)
            pe.wait_ge(c_padded, 4)
            for j, src in enumerate(cc):
                for k in range(KT):
                    ins = nc.tensor.transpose(PS[:, 4 + 2 * j + k // 4, k % 4 * P:(k % 4 + 1) * P], src[:, k, :], ident)
            ins.then_inc(ct_done, 1)
            cols_unit(S5_U0 + 2, 2)
            cols_unit(S5_U0 + 3, 3)
            pe.wait_ge(u_copied, S5_IN_UNITS)

            def rows32(m):
                return slice(32 * (m % 4), 32 * (m % 4) + 32)

            def s5_in(q):
                for j in range(2):
                    for m in range(q * QPAIRS, (q + 1) * QPAIRS):
                        r, k, x = rows32(m), m // 4, m // 4 % 2 * FRAME
                        o = PS[:, m % 4, 256 * j:256 * j + 256].rearrange("p (h x) -> p h x", h=FRAMES)[:, :, x:x + FRAME]
                        even = u_t[r, k, :].rearrange("p (h s two) -> p two h s", h=FRAMES, two=STEP)[:, 0]
                        mm(o, bt[0][j][r, k, :], even, True, False)
                        mm(o[:, 0, 1:FRAME], bt[1][j][r, k, :], u_t[r, k, 1:2 * FRAME - 1:2], False, False)
                        ins = mm(o[:, 1, :], bt[1][j][r, k, :], u_t[r, k, 2 * FRAME - 1:SEQ - 1:2], False, True)
                ins.then_inc(bu_done, 1)

            s5_in(0)
            pe.wait_ge(ct_copied, 2)
            for m in range(PAIRS):
                r = rows32(m)
                o = PS[r, 7, m // 4 * 32:m // 4 * 32 + 32]
                mm(o, bb[0][0][:, m, :], ct[0][0][:, m // 4, r], True, False)
                ins = mm(o, bb[0][1][:, m, :], ct[0][1][:, m // 4, r], False, True)
            ins.then_inc(direct_done, 1)
            for q in range(QUARTERS):
                if q + 1 < QUARTERS:
                    pe.wait_ge(bu_read, q + 1)
                    s5_in(q + 1)
                if q == 0:
                    pe.wait_ge(direct_ready, 4)
                    pe.wait_ge(ct1_ready, 4)
                y = PS[:, 4 + q, :].rearrange("p (k s two) -> p k two s", k=2, two=STEP)
                pe.wait_ge(st_re_ready, q + 1)
                pe.wait_ge(st_im_ready, q + 1)
                for m in range(q * QPAIRS, (q + 1) * QPAIRS):
                    r, k = rows32(m), m // 4
                    for i in range(STEP):
                        o = y[r, k % 2, i, :]
                        if i:
                            mm(o, direct[:, k, r], u_t[:, k, 1::2], True, False)
                        for j in range(2):
                            x = states[q % 2][:, j, :, slot_of(m) * FRAME:(slot_of(m) + 1) * FRAME]
                            ins = mm(o.rearrange("p (h s) -> p h s", h=FRAMES), ct[i][j][:, k, r], x, i == 0 and j == 0, j == 1)
                ins.then_inc(sy_done, 1)
            n = S5_U0 + S5_IN_UNITS
            for dh in range(2):
                for part in range(2):
                    for half in range(2):
                        pe.wait_ge(xlo_ready, 3 * (KT // 2) + 2 * half + 2)
                        rows_unit(n, half, (4 * dh + 2 * part, 4 * dh + 2 * part + 1), xt_hi, xt_lo)
                        n += 1

            for kt, ins in transposes(3):
                if kt % 4 == 3:
                    ins.then_inc(hnt_done, 1)
            pe.wait_ge(hnt_copied, 2)
            pe.wait_ge(moe_landed, 32)
            for t in range(TT):
                for kt in range(KT):
                    ins = mm(PS[:, 6, t * EXPERTS:(t + 1) * EXPERTS], hn_t[:, kt, t * P:(t + 1) * P], router[:, kt, :],
                             kt == 0, kt == KT - 1)
            ins.then_inc(logits_done, 1)
            pe.wait_ge(chosen_done, 1)
            mm(PS[:, 6, 32:32 + EXPERTS], tri, chosen[:, 0, :], True, True)
            mm(PS[:, 6, 40:40 + EXPERTS], ones, chosen[:, 0, :], True, False)
            mm(PS[:, 6, 40:40 + EXPERTS], tri, chosen[:, 1, :], False, True)
            mm(PS[:, 6, 64:64 + EXPERTS], ones, chosen[:, 0, :], True, False)
            mm(PS[:, 6, 64:64 + EXPERTS], ones, chosen[:, 1, :], False, True).then_inc(rank_done, 1)

            def gather(n):
                pe.wait_ge(pick_ready, n)
                for kt in range(KT):
                    for t in range(TT):
                        ins = mm(PS[:, 2 + kt // 4, kt % 4 * P:(kt % 4 + 1) * P], hn[:, t, kt * P:(kt + 1) * P],
                                 pick[:, t, :], t == 0, t == TT - 1)
                ins.then_inc(gathered, 1)

            def scatter(n):
                pe.wait_ge(y0_copied, n)
                pe.wait_ge(y1_copied, n)
                pe.wait_ge(put_ready, n)
                for t in range(TT):
                    for dh in range(2):
                        ins = mm(PS[:, 2 + 4 * t + dh, :], put_g[:, t, :], y_rows[:, dh * 512:dh * 512 + 512], True, True)
                ins.then_inc(scattered, 1)

            def experts(p):
                u0 = MOE_U0 + p * EXPERTS * FFN_UNITS
                gather(9 * p + 1)
                with pe.Fori(0, EXPERTS) as e:
                    pe.wait_ge(xg_lo_ready, count(9 * p + 1, e, 1))

                    def after_up0():
                        scatter(count(9 * p + 1, e, 1))

                    def each(s):
                        if s == 2:
                            pe.wait_ge(pick_g_ready, count(8 * p + 1, e, 1))
                            pe.wait_ge(scatter_added, count(9 * p + 1, e, 1))
                            for t in range(TT):
                                ins = nc.tensor.transpose(PS[:, 6, t * P:(t + 1) * P], pick_g[:, t, :], ident)
                            ins.then_inc(put_t_done, 1)

                    def before_last():
                        gather(count(9 * p + 2, e, 1))

                    ffn(u0, STEPS * (1 + EXPERTS * p), 1, xg_hi, xg_lo, e, after_up0, each, before_last)
                pe.wait_ge(xg_lo_ready, 9 * p + 9)
                scatter(9 * p + 9)
                pe.wait_ge(scatter_added, 9 * p + 9)

            experts(0)
            pe.wait_ge(keys_done, 1)
            flag = pe.value_load(over[0:1, 0:1], min_val=0, max_val=1)
            with pe.If(flag > 0):
                experts(1)


_INS = ["x", "norm_mix", "norm_ffn", "norm_final", "ret_w_in", "ret_gn", "ret_w_out", "s5_w_in", "s5_a_re", "s5_a_im",
        "s5_log_step", "s5_b_re", "s5_b_im", "s5_c_re", "s5_c_im", "s5_d", "s5_w_out", "ffn_w_gate", "ffn_w_up",
        "ffn_w_down", "moe_router", "moe_w_gate", "moe_w_up", "moe_w_down"]


def kernel(**inputs):
    import concourse.bacc as bacc
    from concourse.bass_utils import run_bass_kernel_spmd

    nc = bacc.Bacc("TRN2", target_bir_lowering=False, num_devices=1)
    arrays, aps = {}, {}
    for name in _INS:
        a = np.ascontiguousarray(inputs[name])
        arrays[f"in_{name}"] = a
        aps[name] = nc.dram_tensor(f"in_{name}", a.shape, F32, kind="ExternalInput").ap()
    arrays["in_constants"] = constants()
    consts = nc.dram_tensor("in_constants", (P, C_COLS), F32, kind="ExternalInput").ap()
    out = nc.dram_tensor("out", (1, SEQ, D), F32, kind="ExternalOutput").ap()
    trunk(nc, aps, consts, out)
    r = run_bass_kernel_spmd(nc, [arrays], core_ids=[0])
    return r.results[0]["out"]
```

```python
import math
from contextlib import ExitStack

import numpy as np

import concourse.bass as bass
from concourse import mybir

F32 = mybir.dt.float32
F32R = mybir.dt.float32r
I32 = mybir.dt.int32
ALU = mybir.AluOpType
ACT = mybir.ActivationFunctionType
AX_X = mybir.AxisListType.X

P = 128
D = 1024
SEQ = 256
TT = SEQ // P
KT = D // P
EPS = 1e-6

HEADS = 4
DK = D // HEADS
DV = 2 * D // HEADS

GROUPS, STATES, GROUP_W = 64, 64, 16
PAIRS = GROUPS // 2
STEP = 2
FRAME = 64
FRAMES = SEQ // STEP // FRAME
QUARTERS = 4
QPAIRS = PAIRS // QUARTERS
QKT = KT // QUARTERS
KEPT = FRAME * FRAMES

FF = 3584
FC = 512
STEPS = FF // FC
FT = FC // P
EXPERTS = 8
SLOTS = P

UNIT = 2048
RAW = 6
SPLIT = 3
AHEAD = 3
FFN_UNITS = 6 * STEPS

RET_U0 = 0
RET_UNITS = 8 * HEADS
FFN_U0 = RET_U0 + RET_UNITS
S5_U0 = FFN_U0 + FFN_UNITS
S5_IN_UNITS, S5_OUT_UNITS = 4, 8
U_BANK = (0, 1, 3, 4)
MOE_U0 = S5_U0 + S5_IN_UNITS + S5_OUT_UNITS

SPARE = 4
SPARE_U0 = MOE_U0 + RAW + AHEAD

C_IDENT = 0
C_EVEN = C_IDENT + P
C_ODD = C_EVEN + 1
C_EPS = C_ODD + 1
C_ZERO = C_EPS + 1
C_FIRST = C_IDENT + P + 8
C_DECAY = C_FIRST
C_IOTA = C_DECAY + HEADS * SEQ
C_TRI = C_IOTA + P
C_ONES = C_TRI + P
C_COLS = C_ONES + P

TWO_PI = 2 * math.pi
PI_1 = 6.28125
PI_2 = float(np.float32(round((TWO_PI - PI_1) * 2 ** 21) / 2 ** 21))
PI_3 = TWO_PI - PI_1 - PI_2
ROUND = 1.5 * 2 ** 23
PI_F32 = 3.1415925


def constants():
    c = np.zeros((P, C_COLS), np.float32)
    key = np.arange(P)[:, None].astype(np.float64)
    query = np.arange(SEQ)[None, :].astype(np.float64)
    for h in range(HEADS):
        log_gamma = np.log1p(-np.exp2(-5.0 - h))
        decay = np.where(query >= key, np.exp(log_gamma * np.maximum(query - key, 0)), 0)
        c[:, C_DECAY + h * SEQ:C_DECAY + (h + 1) * SEQ] = decay * DK ** -0.5
    c[:, C_IDENT:C_IDENT + P] = np.eye(P)
    c[:, C_IOTA:C_IOTA + P] = np.arange(P)[None, :]
    c[:, C_TRI:C_TRI + P] = np.arange(P)[:, None] < np.arange(P)[None, :]
    c[:, C_ONES:C_ONES + P] = 1
    odd = (np.arange(P) // GROUP_W) % 2
    c[:, C_EVEN], c[:, C_ODD] = 1 - odd, odd
    c[:, C_EPS] = EPS
    return c


def ret_first(h):
    return 0 if h == 0 else 8 * h - 2


def ffn_first(s):
    return 0 if s == 0 else 6 * s - 2


def is_first(e):
    return e is None or isinstance(e, int) and e == 0


def is_spare(n, e):
    return is_first(e) and SPARE_U0 <= n < SPARE_U0 + SPARE


def ring_number(n, e):
    return n if is_first(e) and n < SPARE_U0 else n - SPARE


def trunk(nc, A, consts, out):
    with ExitStack() as ctx:
        def sem(name):
            return ctx.enter_context(nc.semaphore(name))

        base = 16512

        def place(name, shape, dt, offset):
            return nc.alloc_sbuf_tensor_at(name, [P, *shape], dt, offset=base + offset)

        raw = place("weights_raw", [RAW, UNIT], F32, 0)
        w_hi = place("weights_hi", [SPLIT, UNIT], F32R, 49152)
        w_lo = place("weights_lo", [SPLIT, UNIT], F32R, 73728)
        cst = place("constants", [C_COLS], F32, 98304)
        SMALL = 98304 + 4 * C_COLS
        H_OFF = SMALL + 5120
        resid = place("residual", [TT, D], F32, H_OFF)
        hn = place("normed_rows", [TT, D], F32, H_OFF + 8192)
        xt_hi = place("x_transposed_hi", [KT, SEQ], F32R, H_OFF + 16384)
        xt_lo = place("x_transposed_lo", [KT, SEQ], F32R, H_OFF + 24576)
        K_OFF = H_OFF + 32768
        cos_t = place("cos_table", [QUARTERS, QPAIRS * FRAME], F32, K_OFF)
        sin_t = place("sin_table", [QUARTERS, QPAIRS * FRAME], F32, K_OFF + 8192)
        bb = [[place("b_rows_re", [PAIRS, 2 * GROUP_W], F32, K_OFF + 16384),
               place("b_rows_im", [PAIRS, 2 * GROUP_W], F32, K_OFF + 20480)],
              [place("ab_rows_re", [PAIRS, 2 * GROUP_W], F32, K_OFF + 24576),
               place("ab_rows_im", [PAIRS, 2 * GROUP_W], F32, 98304 + 4 * C_DECAY)]]
        W_OFF = K_OFF + 28672
        ht_hi = [place(f"act_transposed_hi{b}", [TT, FT, P], F32R, W_OFF + 4096 * b) for b in range(2)]
        ht_lo = [place(f"act_transposed_lo{b}", [TT, FT, P], F32R, W_OFF + 8192 + 4096 * b) for b in range(2)]
        gated = place("silu_of_gate", [TT, FC], F32, W_OFF + 16384)
        act_rows = place("act_rows", [TT, FC], F32, W_OFF + 20480)
        qk_t = place("q_and_k_transposed", [2, 2, SEQ], F32, W_OFF + 24576)
        v_rows = place("v_rows", [TT, DV], F32, W_OFF + 28672)
        gain_rows = place("gain_rows", [P], F32, W_OFF + 28672)
        scores = place("scores_transposed", [384], F32, W_OFF + 32768)
        T_OFF = W_OFF + 34304
        tmp1 = place("setup_tmp1", [PAIRS, GROUP_W], F32, T_OFF)
        tmp2 = place("setup_tmp2", [PAIRS, GROUP_W], F32, T_OFF + 2048)
        b_re = place("b_re", [PAIRS, GROUP_W], F32, W_OFF + 4096)
        b_im = place("b_im", [PAIRS, GROUP_W], F32, W_OFF + 4096 + 2048)
        log_step = place("log_step", [2], F32, T_OFF + 4096)
        dt = place("dt", [2], F32, T_OFF + 4128)
        par_in = place("params_by_pair", [5, P], F32, T_OFF + 4160)
        a_re = place("a_re", [P], F32, T_OFF)
        a_im = place("a_im", [P], F32, T_OFF + 512)
        p1 = place("param_tmp1", [P], F32, T_OFF + 1024)
        p2 = place("param_tmp2", [P], F32, T_OFF + 1536)
        p3 = place("param_tmp3", [P], F32, T_OFF + 2048)
        p4 = place("param_tmp4", [P], F32, T_OFF + 2560)
        p5 = place("param_tmp5", [P], F32, T_OFF + 3072)
        p6 = place("param_tmp6", [P], F32, T_OFF + 3584)
        u_t = place("u_transposed", [KT, SEQ], F32, H_OFF + 8192)
        y_t = place("y_transposed", [KT, SEQ], F32, H_OFF + 16384)
        bt = [[place(f"b{i}_transposed_{part}", [KT, P], F32, W_OFF + 8192 * i + 4096 * j)
               for j, part in enumerate(("re", "im"))] for i in range(STEP)]
        ct = [[place(f"c{i}_transposed_{part}", [KT, P], F32, W_OFF + 16384 + 8192 * i + 4096 * j)
               for j, part in enumerate(("re", "im"))] for i in range(STEP)]
        cc = [place(f"c_rows_{part}", [KT, P], F32, W_OFF + 24576 + 4096 * j) for j, part in enumerate(("re", "im"))]
        c_in = [place(f"c_{part}", [KT, STATES], F32, T_OFF + 2048 * j) for j, part in enumerate(("re", "im"))]
        gelu_t = place("gelu_transposed", [KT, SEQ], F32, W_OFF + 32768)
        direct = place("direct_transposed", [KT, P], F32, 98304 + 4 * C_DECAY)
        spread = place("u_spread", [QKT, STEP, 4, KEPT], F32, 49152)
        scan = place("scan", [2, FRAMES, QPAIRS * FRAME], F32, 73728)
        scan_tmp = place("scan_tmp", [FRAMES, QPAIRS * FRAME], F32, K_OFF + 24576)
        turned = place("turned", [FRAMES, QPAIRS * FRAME], F32, 73728 + 16384)
        mag_t = place("magnitude_table", [QUARTERS, QPAIRS, FRAME], F32, 49152 + 8192)
        states = [place("states0", [2, FRAMES, QPAIRS * FRAME], F32, 73728 + 8192),
                  place("states1", [2, FRAMES, QPAIRS * FRAME], F32, 49152 + 16384)]
        glu_gate = place("glu_gate", [TT, 512], F32, W_OFF + 24576)
        glu_out = place("glu_out", [TT, 512], F32, W_OFF + 28672)
        spare = [place(f"weights_spare{i}", [UNIT], F32, offset)
                 for i, offset in enumerate((W_OFF + 24576, W_OFF + 32768, H_OFF + 16384, H_OFF + 24576))]
        gain_row = place("ffn_gain_row", [D], F32, K_OFF)
        hn_t = place("normed_transposed", [KT, SEQ], F32, K_OFF + 4096)
        xg_hi = place("gathered_hi", [KT, SLOTS], F32R, K_OFF + 12288)
        xg_lo = place("gathered_lo", [KT, SLOTS], F32R, K_OFF + 16384)
        y_rows = place("expert_rows", [D], F32, K_OFF + 20480)
        hn_hi = place("normed_rows_hi", [TT, D], F32R, K_OFF)
        hn_lo = place("normed_rows_lo", [TT, D], F32R, H_OFF + 8192)
        pick = place("pick", [TT, SLOTS], F32R, K_OFF + 24576)
        pick_g = place("pick_gated", [TT, SLOTS], F32, K_OFF + 25600)
        put_g = place("put_gated", [TT, P], F32, K_OFF + 26624)
        final_gain = place("final_gain_row", [D], F32, H_OFF + 16384)

        small_at = [SMALL]

        def small(name, shape, dt=F32):
            size = -(-4 * math.prod(shape) // 32) * 32
            small_at[0] += size
            assert small_at[0] <= H_OFF
            return place(name, shape, dt, small_at[0] - size)

        gains = small("gains", [7 * KT])
        g_gn = gains[:, 4 * KT:6 * KT]
        d_skip = gains[:, 6 * KT:7 * KT]
        ssq = small("sum_of_squares", [TT])
        std = small("std", [TT])
        rstd = small("rstd", [TT])
        bn_s = small("bn_stats", [TT, 6])
        bn_a = small("bn_mean_var", [TT, 2])
        hstd = small("head_std", [TT])
        hrstd = small("head_rstd", [TT])
        par = small("params", [5, PAIRS])
        ab_re = small("abar_re", [PAIRS])
        ab_im = small("abar_im", [PAIRS])
        af_re = small("abar_f_re", [PAIRS])
        af_im = small("abar_f_im", [PAIRS])
        mag2 = small("magnitude", [PAIRS])
        pw_re = small("power_re", [PAIRS])
        pw_im = small("power_im", [PAIRS])
        pw_t = small("power_tmp", [2, PAIRS])
        turn_re = small("frame_turn_re", [PAIRS])
        turn_im = small("frame_turn_im", [PAIRS])
        car = small("carry", [2, 2, QPAIRS])
        router = small("router", [KT, EXPERTS])
        logit = small("logits", [TT, EXPERTS])
        top = small("top", [TT, 8])
        r_gt = small("is_above_second", [TT, EXPERTS])
        r_eq = small("is_second", [TT, EXPERTS])
        r_cum = small("count_of_second", [TT, EXPERTS])
        r_n = small("n_above", [TT])
        chosen = small("chosen", [TT, EXPERTS])
        r_exp = small("exp", [TT, EXPERTS])
        neg_top = small("neg_top", [TT])
        gate_w = small("gate_weight", [TT, EXPERTS])
        key = [small(f"slot_key{b}", [TT, EXPERTS + 1]) for b in range(2)]
        unused = small("unused", [2])
        most = small("largest_count", [1])
        over = small("over", [1], I32)

        PS = ctx.enter_context(nc.psum_tensor("PS", [P, 8, 512], F32))

        ident = cst[:, C_IDENT:C_IDENT + P]
        iota = cst[:, C_IOTA:C_IOTA + P]
        tri = cst[:, C_TRI:C_TRI + P]
        ones = cst[:, C_ONES:C_ONES + P]
        eps = cst[:, C_EPS:C_EPS + 1]

        def gate_banks(tts):
            return list(range(tts))

        def up_banks(tts):
            return list(range(tts, 2 * tts))

        def out_bank(tt, dh):
            return 4 + 2 * tt + dh

        landed = [sem(f"raw_landed{i}") for i in range(RAW)]
        spare_landed = [sem(f"spare_landed{i}") for i in range(SPARE)]
        hi_ready = sem("weights_hi_ready")
        lo_ready = sem("weights_lo_ready")
        used = sem("units_used")
        x_landed = [sem(f"x_landed{t}") for t in range(TT)]
        c_landed = sem("first_constants_landed")
        c2_landed = sem("constants_landed")
        g_landed = sem("gains_landed")
        unused_set = sem("unused_set")
        gains_t = sem("gains_transposed")
        gains_ready = sem("gains_ready")
        a_landed = sem("s5_a_landed")
        bc_landed = sem("s5_b_landed")
        cin_landed = sem("s5_c_landed")
        moe_landed = sem("moe_params_landed")
        fin_landed = sem("final_gain_landed")
        resid_ready = sem("residual_ready")
        ssq0_done = sem("ssq0_done")
        ssq1_done = sem("ssq1_done")
        std_done = sem("std_done")
        rstd_done = sem("rstd_done")
        hn0_ready = sem("normed0_ready")
        hn1_ready = sem("normed1_ready")
        xt_done = sem("x_transposed")
        xhi_ready = sem("x_hi_ready")
        xlo_ready = sem("x_lo_ready")
        qk_copied = sem("q_k_copied")
        v_copied = sem("v_copied")
        g_silu = sem("g_silu_done")
        scores_done = sem("scores_done")
        decayed = sem("scores_decayed")
        y_done = sem("retention_y_done")
        bn_done = sem("bn_done")
        hstd_done = sem("head_std_done")
        y_normed = sem("y_normed")
        yt_done = sem("y_transposed_done")
        yt_hi = sem("y_transposed_hi")
        yt_lo = sem("y_transposed_lo")
        silu_done = sem("silu_done")
        mult_done = sem("act_rows_done")
        act_t_done = sem("act_transposed")
        act_hi = sem("act_hi_ready")
        act_lo = sem("act_lo_ready")
        dt_done = sem("dt_done")
        ar_done = sem("a_times_dt_done")
        mag_done = sem("mag_done")
        angle_done = sem("angle_done")
        sin_done = sem("sin_done")
        den_done = sem("den_done")
        rden_done = sem("rden_done")
        par_done = sem("params_done")
        par_t = sem("params_transposed")
        par_ready = sem("params_ready")
        setup_done = sem("s5_setup_done")
        bt_done = sem("b_transposed_done")
        bt_copied = sem("b_copied")
        ct_done = sem("c_transposed_done")
        ct_copied = sem("c_copied")
        u_copied = sem("u_copied")
        bu_done = sem("bu_done")
        bu_read = sem("bu_read")
        c_padded = sem("c_rows_padded")
        ct1_ready = sem("c_times_abar_ready")
        mag_ready = sem("magnitude_table_ready")
        spread_zero = sem("u_spread_zeroed")
        spread_ready = sem("u_spread_ready")
        zero_ready = sem("direct_zeroed")
        direct_done = sem("direct_done")
        direct_ready = sem("direct_ready")
        scans_done = sem("scans_done")
        turned_ready = sem("turned_ready")
        im_part_ready = sem("states_im_part_ready")
        st_re_ready = sem("states_re_ready")
        st_im_ready = sem("states_im_ready")
        sy_done = sem("s5_y_done")
        sy_added = sem("s5_y_added")
        gelu_done = sem("gelu_done")
        glu_sig = sem("glu_sigmoid_done")
        glu_read = sem("glu_gate_read")
        hnt_done = sem("normed_transposed_done")
        hnt_copied = sem("normed_transposed_copied")
        logits_done = sem("logits_done")
        hn_hi_ready = sem("normed_rows_hi_ready")
        hn_lo_ready = sem("normed_rows_lo_ready")
        top_done = sem("top_done")
        exp_done = sem("exp_done")
        chosen_done = sem("chosen_done")
        rank_done = sem("rank_done")
        keys_done = sem("keys_done")
        pick_ready = sem("pick_ready")
        pick_g_ready = sem("pick_gated_ready")
        gathered = sem("gathered")
        xg_hi_ready = sem("gathered_hi_ready")
        xg_lo_ready = sem("gathered_lo_ready")
        put_t_done = sem("put_transposed")
        put_ready = sem("put_ready")
        y0_copied = sem("expert_rows0_copied")
        y1_copied = sem("expert_rows1_copied")
        scattered = sem("scattered")
        scatter_added = sem("scatter_added")
        out_ready = sem("out_ready")
        stored = sem("output_stored")
        dve_self = sem("vector_self")
        act_self = sem("scalar_self")
        pool_self = sem("gpsimd_self")

        def count(static, e=None, per=0):
            return static if e is None else e * per + static

        def ffn_sources(w_gate, w_up, w_down):
            units = []
            for s in range(STEPS + 1):
                if s < STEPS:
                    for w in (w_gate, w_up):
                        for half in range(2):
                            units.append((4, w[half * 512:half * 512 + 512, s * FC:(s + 1) * FC]))
                if s > 0:
                    for half in range(2):
                        r = (s - 1) * FC + half * 256
                        units.append((2, w_down[r:r + 256, :]))
            return units

        def static_sources():
            w_in, w_out = A["ret_w_in"][0], A["ret_w_out"][0]
            units = []

            def head_out(h):
                return [(2, w_out[h * DV + a:h * DV + a + 256, :]) for a in (0, 256)]
            for h in range(HEADS):
                units.append((8, w_in[:, h * DK:(h + 1) * DK]))
                units.append((8, w_in[:, D + h * DK:D + (h + 1) * DK]))
                for c0 in (2 * D + h * DV, 4 * D + h * DV):
                    units += [(4, w_in[a:a + 512, c0:c0 + DV]) for a in (0, 512)]
                if h:
                    units += head_out(h - 1)
            units += head_out(HEADS - 1)
            units += ffn_sources(A["ffn_w_gate"][0], A["ffn_w_up"][0], A["ffn_w_down"][0])
            s_in, s_out = A["s5_w_in"][0], A["s5_w_out"][0]
            units += [(8, s_in[:, c * 256:(c + 1) * 256]) for c in range(4)]
            for dh in range(2):
                for c0 in (dh * 512, D + dh * 512):
                    units += [(4, s_out[a:a + 512, c0:c0 + 512]) for a in (0, 512)]
            assert len(units) == MOE_U0
            return units

        def raw_unit(n, e=None):
            return spare[n - SPARE_U0][:, :] if is_spare(n, e) else raw[:, ring_number(n, e) % RAW, :]

        block = ctx.enter_context(nc.Block())

        @block.sync
        def _(sp):
            for t in range(TT):
                sp.dma_start(resid[:, t, :], A["x"][0, t * P:(t + 1) * P, :]).then_inc(x_landed[t], 16)

            sp.dma_start(gain_rows[0:16, :], A["norm_mix"].rearrange("l (k p) -> (l k) p", p=P)).then_inc(g_landed, 16)
            sp.dma_start(gain_rows[16:32, :], A["norm_ffn"].rearrange("l (k p) -> (l k) p", p=P)).then_inc(g_landed, 16)
            sp.dma_start(gain_rows[32:48, :], A["ret_gn"][0].rearrange("(k p) -> k p", p=P)).then_inc(g_landed, 16)
            sp.dma_start(gain_rows[48:56, :], A["s5_d"][0].rearrange("(k p) -> k p", p=P)).then_inc(g_landed, 16)

            def load(n, kt, src, e=None):
                if is_spare(n, e):
                    signal = spare_landed[n - SPARE_U0]
                    if n == SPARE_U0:
                        sp.wait_ge(resid_ready, 3)
                        sp.wait_ge(used, MOE_U0)
                else:
                    signal = landed[ring_number(n, e) % RAW]
                    if n >= RAW:
                        last = n - RAW
                        if is_first(e) and SPARE_U0 <= n and last - SPARE < SPARE_U0:
                            last -= SPARE
                        sp.wait_ge(lo_ready, count(last + 1, e, FFN_UNITS))
                sp.dma_start(raw_unit(n, e).rearrange("p (k n) -> p k n", k=kt),
                             src.rearrange("(k p) n -> p k n", p=P)).then_inc(signal, 16)

            for n, (kt, src) in enumerate(static_sources()):
                load(n, kt, src)

            def experts(u0):
                def expert(e):
                    for i, (kt, src) in enumerate(ffn_sources(
                            A["moe_w_gate"][0, e], A["moe_w_up"][0, e], A["moe_w_down"][0, e])):
                        load(u0 + i, kt, src, e)

                expert(0)
                with sp.Fori(1, EXPERTS) as e:
                    expert(e)

            experts(MOE_U0)
            sp.wait_ge(keys_done, 1)
            flag = sp.value_load(over[0:1, 0:1], min_val=0, max_val=1)
            with sp.If(flag > 0):
                experts(MOE_U0 + EXPERTS * FFN_UNITS)
            for t in range(TT):
                sp.wait_ge(out_ready, t + 1)
                sp.dma_start(out[0, t * P:(t + 1) * P, :], hn[:, t, :]).then_inc(stored, 16)
            sp.wait_ge(stored, 16 * TT)

        @block.gpsimd
        def _(pool):
            n_self = [0]

            def link(ins):
                n_self[0] += 1
                ins.then_inc(pool_self, 1)
                pool.wait_ge(pool_self, n_self[0])

            def tt(o, a, b, op):
                link(nc.gpsimd.tensor_tensor(o, a, b, op))

            def ts(o, a, x, y, op0, op1):
                link(nc.gpsimd.tensor_scalar(o, a, x, y, op0, op1))

            q = slice(0, PAIRS)
            pool.dma_start(log_step[q, :], A["s5_log_step"][0].rearrange("(m g) -> m g", g=2)).then_inc(a_landed, 16)
            pool.dma_start(a_re[q, :], A["s5_a_re"][0].rearrange("(m g) p -> m (g p)", g=2)).then_inc(a_landed, 16)
            pool.dma_start(a_im[q, :], A["s5_a_im"][0].rearrange("(m g) p -> m (g p)", g=2)).then_inc(a_landed, 16)
            for dst, name in ((b_re, "s5_b_re"), (b_im, "s5_b_im")):
                pool.dma_start(dst[:, :, :], A[name][0].rearrange("(m g) p n -> (g p) m n", g=2)).then_inc(bc_landed, 16)

            pool.wait_ge(a_landed, 48)
            pool.wait_ge(dt_done, 1)
            halves = lambda x: x[q, :].rearrange("m (g p) -> m g p", g=2)
            dt_b = dt[q, :].unsqueeze(2).to_broadcast([PAIRS, 2, STATES])
            nc.gpsimd.tensor_tensor(halves(p1), halves(a_re), dt_b, ALU.mult).then_inc(ar_done, 1)
            tt(halves(p2), halves(a_im), dt_b, ALU.mult)
            ts(p3[q, :], p2[q, :], 1 / TWO_PI, ROUND, ALU.mult, ALU.add)
            ts(p3[q, :], p3[q, :], ROUND, None, ALU.subtract, ALU.bypass)
            for part in (PI_1, PI_2, PI_3):
                ts(p4[q, :], p3[q, :], part, None, ALU.mult, ALU.bypass)
                tt(p2[q, :], p2[q, :], p4[q, :], ALU.subtract)
            nc.gpsimd.tensor_scalar(p2[q, :], p2[q, :], PI_F32, -PI_F32, ALU.min, ALU.max).then_inc(angle_done, 1)
            tt(p4[q, :], a_re[q, :], a_re[q, :], ALU.mult)
            tt(p5[q, :], a_im[q, :], a_im[q, :], ALU.mult)
            nc.gpsimd.tensor_tensor(p4[q, :], p4[q, :], p5[q, :], ALU.add).then_inc(den_done, 1)
            pool.wait_ge(sin_done, 2)
            pool.wait_ge(den_done, 1)
            pool.wait_ge(mag_done, 1)
            mag, cos, sin, f_re, f_im = (par_in[q, i, :] for i in range(5))
            tt(p5[q, :], cos, cos, ALU.mult)
            ts(cos, p5[q, :], -2.0, 1.0, ALU.mult, ALU.add)
            tt(p1[q, :], mag, cos, ALU.mult)
            ts(p1[q, :], p1[q, :], 1.0, None, ALU.subtract, ALU.bypass)
            tt(p2[q, :], mag, sin, ALU.mult)
            pool.wait_ge(rden_done, 1)
            tt(p3[q, :], p1[q, :], a_re[q, :], ALU.mult)
            tt(p5[q, :], p2[q, :], a_im[q, :], ALU.mult)
            tt(p3[q, :], p3[q, :], p5[q, :], ALU.add)
            tt(f_re, p3[q, :], p6[q, :], ALU.mult)
            tt(p3[q, :], p2[q, :], a_re[q, :], ALU.mult)
            tt(p5[q, :], p1[q, :], a_im[q, :], ALU.mult)
            tt(p3[q, :], p3[q, :], p5[q, :], ALU.subtract)
            nc.gpsimd.tensor_tensor(f_im, p3[q, :], p6[q, :], ALU.mult).then_inc(par_done, 1)

            pool.wait_ge(par_ready, 1)
            mag, cos, sin, f_re, f_im = (par[:, i, :] for i in range(5))
            tt(ab_re[:, :], mag, cos, ALU.mult)
            tt(ab_im[:, :], mag, sin, ALU.mult)
            tt(mag2[:, :], mag, mag, ALU.mult)
            tt(pw_t[:, 0, :], cos, cos, ALU.mult)
            tt(pw_t[:, 1, :], sin, sin, ALU.mult)
            tt(pw_re[:, :], pw_t[:, 0, :], pw_t[:, 1, :], ALU.subtract)
            tt(pw_t[:, 0, :], cos, sin, ALU.mult)
            ts(pw_im[:, :], pw_t[:, 0, :], 2.0, None, ALU.mult, ALU.bypass)
            cos_s, sin_s = (t[:, :, :].rearrange("p q (m s) -> p (q m) s", s=FRAME) for t in (cos_t, sin_t))

            def square():
                tt(pw_t[:, 0, :], pw_re[:, :], pw_re[:, :], ALU.mult)
                tt(pw_t[:, 1, :], pw_im[:, :], pw_im[:, :], ALU.mult)
                tt(pw_im[:, :], pw_im[:, :], pw_re[:, :], ALU.mult)
                ts(pw_im[:, :], pw_im[:, :], 2.0, None, ALU.mult, ALU.bypass)
                tt(pw_re[:, :], pw_t[:, 0, :], pw_t[:, 1, :], ALU.subtract)

            link(nc.gpsimd.memset(cos_s[:, :, 0:1], 1.0))
            link(nc.gpsimd.memset(sin_s[:, :, 0:1], 0.0))
            link(nc.gpsimd.tensor_copy(cos_s[:, :, 1:2], pw_re[:, :].unsqueeze(2)))
            link(nc.gpsimd.tensor_copy(sin_s[:, :, 1:2], pw_im[:, :].unsqueeze(2)))
            n = 2
            while n < FRAME:
                square()
                for k0 in range(0, n, GROUP_W):
                    k1 = min(n, k0 + GROUP_W)
                    wr = pw_re[:, :].unsqueeze(2).to_broadcast([P, PAIRS, k1 - k0])
                    wi = pw_im[:, :].unsqueeze(2).to_broadcast([P, PAIRS, k1 - k0])
                    t1, t2 = tmp1[:, :, 0:k1 - k0], tmp2[:, :, 0:k1 - k0]
                    tt(t1, cos_s[:, :, k0:k1], wr, ALU.mult)
                    tt(t2, sin_s[:, :, k0:k1], wi, ALU.mult)
                    tt(cos_s[:, :, n + k0:n + k1], t1, t2, ALU.subtract)
                    tt(t1, cos_s[:, :, k0:k1], wi, ALU.mult)
                    tt(t2, sin_s[:, :, k0:k1], wr, ALU.mult)
                    tt(sin_s[:, :, n + k0:n + k1], t1, t2, ALU.add)
                n *= 2
            square()
            tt(turn_re[:, :], pw_re[:, :], mag2[:, :], ALU.mult)
            tt(turn_im[:, :], pw_im[:, :], mag2[:, :], ALU.mult)
            tt(pw_t[:, 0, :], ab_re[:, :], f_re, ALU.mult)
            tt(pw_t[:, 1, :], ab_im[:, :], f_im, ALU.mult)
            tt(af_re[:, :], pw_t[:, 0, :], pw_t[:, 1, :], ALU.subtract)
            tt(pw_t[:, 0, :], ab_re[:, :], f_im, ALU.mult)
            tt(pw_t[:, 1, :], ab_im[:, :], f_re, ALU.mult)
            tt(af_im[:, :], pw_t[:, 0, :], pw_t[:, 1, :], ALU.add)
            pool.wait_ge(bc_landed, 32)
            for i, (fr, fi) in enumerate(((f_re, f_im), (af_re[:, :], af_im[:, :]))):
                fr, fi = (f.unsqueeze(2).to_broadcast([P, PAIRS, GROUP_W]) for f in (fr, fi))
                for dst, x, y, op in ((bb[i][0], b_re, b_im, ALU.subtract), (bb[i][1], b_im, b_re, ALU.add)):
                    tt(tmp1[:, :, :], x[:, :, :], fr, ALU.mult)
                    tt(tmp2[:, :, :], y[:, :, :], fi, ALU.mult)
                    if dst is bb[1][1]:
                        pool.wait_ge(decayed, HEADS)
                    link(nc.gpsimd.memset(dst[:, :, :], 0.0))
                    for g in range(2):
                        h = slice(STATES * g, STATES * (g + 1))
                        ins = nc.gpsimd.tensor_tensor(dst[h, :, GROUP_W * g:GROUP_W * (g + 1)], tmp1[h, :, :], tmp2[h, :, :], op)
                        if dst is bb[1][1] and g == 1:
                            ins.then_inc(setup_done, 1)
                        else:
                            link(ins)
            pool.dma_start(router[:, :, :], A["moe_router"][0].rearrange("(k p) e -> p k e", p=P)).then_inc(moe_landed, 16)

            pool.wait_ge(setup_done, 1)
            pool.wait_ge(used, S5_U0)
            for dst, name in zip(c_in, ("s5_c_re", "s5_c_im")):
                pool.dma_start(dst[:, :, :], A[name][0].rearrange("(t g) n p -> (g n) t p", g=8)).then_inc(cin_landed, 16)
            pool.wait_ge(cin_landed, 32)
            for dst, src, sign in ((cc[0], c_in[0], 1.0), (cc[1], c_in[1], -1.0)):
                for g, col in ((0, C_EVEN), (1, C_ODD)):
                    nc.gpsimd.tensor_scalar(dst[:, :, STATES * g:STATES * (g + 1)], src[:, :, :], cst[:, col:col + 1], sign,
                                            ALU.mult, ALU.mult).then_inc(c_padded, 1)
            pool.wait_ge(bt_done, 2)
            nc.gpsimd.memset(direct[:, :, :], 0.0).then_inc(zero_ready, 1)
            pool.wait_ge(c_padded, 4)
            pool.wait_ge(ct_copied, 2)
            for half in range(2):
                k = slice(half * KT // 2, (half + 1) * KT // 2)
                m = slice(half * PAIRS // 2, (half + 1) * PAIRS // 2)
                ar, ai = (a[:, m].unsqueeze(2).to_broadcast([P, PAIRS // 2, 32]) for a in (ab_re, ab_im))

                def pairs(t):
                    return t[:, k, :].rearrange("p k (i n) -> p (k i) n", i=4)
                t1, t2 = (t[:, :, :].rearrange("p m n -> p (m n)").rearrange("p (m n) -> p m n", n=32) for t in (tmp1, tmp2))
                for dst, x, y, op in ((ct[1][0], ct[0][0], ct[0][1], ALU.add), (ct[1][1], ct[0][1], ct[0][0], ALU.subtract)):
                    tt(t1, pairs(x), ar, ALU.mult)
                    tt(t2, pairs(y), ai, ALU.mult)
                    nc.gpsimd.tensor_tensor(pairs(dst), t1, t2, op).then_inc(ct1_ready, 1)
                    pool.wait_ge(ct1_ready, 2 * half + (1 if dst is ct[1][0] else 2))
            pool.wait_ge(used, S5_U0 + S5_IN_UNITS)
            for qt in range(QUARTERS):
                def frames(t):
                    return t.rearrange("p h (m s) -> p h m s", s=FRAME)
                sin_q = sin_t[:, qt, :].rearrange("p (m s) -> p m s", s=FRAME).unsqueeze(1).to_broadcast(
                    [P, FRAMES, QPAIRS, FRAME])
                pool.wait_ge(scans_done, qt + 1)
                nc.gpsimd.tensor_tensor(frames(turned[:, :, :]), frames(scan[:, 0]), sin_q, ALU.mult).then_inc(turned_ready, 1)
                if qt < QUARTERS - 1:
                    pool.wait_ge(turned_ready, qt + 1)
                    pool.wait_ge(im_part_ready, qt + 1)
                    x_im = frames(states[qt % 2][:, 1])
                    nc.gpsimd.tensor_tensor(x_im, x_im, frames(turned[:, :, :]), ALU.add).then_inc(st_im_ready, 1)
                    pool.wait_ge(st_im_ready, qt + 1)
            pool.wait_ge(st_im_ready, QUARTERS)
            pool.dma_start(gain_row[:, :], A["norm_ffn"][1:2, :].to_broadcast([P, D])).then_inc(moe_landed, 16)
            pool.wait_ge(hn_hi_ready, 1)
            nc.gpsimd.tensor_tensor(hn_lo[:, :, :], hn[:, :, :], hn_hi[:, :, :].bitcast(F32), ALU.subtract).then_inc(hn_lo_ready, 1)
            pool.wait_ge(lo_ready, SPARE_U0 + SPARE)
            pool.dma_start(final_gain[:, :], A["norm_final"].unsqueeze(0).to_broadcast([P, D])).then_inc(fin_landed, 16)

        @block.scalar
        def _(act):
            n_self = [0]

            def link(ins):
                n_self[0] += 1
                ins.then_inc(act_self, 1)
                act.wait_ge(act_self, n_self[0])

            def copy(o, i):
                return nc.scalar.activation(o, i, ACT.Copy)

            act.dma_start(cst[:, 0:C_FIRST], consts[:, 0:C_FIRST]).then_inc(c_landed, 16)
            act.dma_start(cst[:, C_FIRST:C_COLS], consts[:, C_FIRST:C_COLS]).then_inc(c2_landed, 16)

            def load_sqrt():
                nc.scalar.activation(unused[:, 0:1], unused[:, 1:2], ACT.Sqrt)

            def split_hi(n, e=None):
                if is_spare(n, e):
                    act.wait_ge(spare_landed[n - SPARE_U0], 16)
                else:
                    r = ring_number(n, e)
                    act.wait_ge(landed[r % RAW], count(16 * (r // RAW + 1), e, 16 * (FFN_UNITS // RAW)))
                if n >= SPLIT:
                    act.wait_ge(used, count(n - SPLIT + 1, e, FFN_UNITS))
                copy(w_hi[:, n % SPLIT, :], raw_unit(n, e)).then_inc(hi_ready, 1)

            def norm_rows(i):
                if i == 0:
                    act.wait_ge(unused_set, 1)
                    load_sqrt()
                    act.wait_ge(c_landed, 16)
                    act.wait_ge(x_landed[0], 16)
                else:
                    load_sqrt()
                if i:
                    act.wait_ge(resid_ready, i)
                nc.scalar.activation(hn[:, 0, :], resid[:, 0, :], ACT.Square, accum_out=ssq[:, 0:1]).then_inc(ssq0_done, 1)
                act.wait_ge(ssq0_done, i + 1)
                act.wait_ge(ssq1_done, i + 1)
                if i == 0:
                    act.wait_ge(x_landed[1], 16)
                nc.scalar.activation(std[:, :], ssq[:, :], ACT.Sqrt, scale=1.0 / D, bias=eps).then_inc(std_done, 1)
                if i < 3:
                    act.wait_ge(rstd_done, i + 1)
                    nc.scalar.activation(hn[:, 1, :], resid[:, 1, :], ACT.Copy, scale=rstd[:, 1:2]).then_inc(hn1_ready, 1)

            def norm_split(i):
                gain = (gains[:, 0:KT], gains[:, 2 * KT:3 * KT], gains[:, KT:2 * KT])[i]
                act.wait_ge(gains_ready, 1)
                for bank in range(KT // 2):
                    act.wait_ge(xt_done, KT // 2 * i + bank + 1)
                    for j in range(2):
                        kt = 2 * bank + j
                        ins = nc.scalar.activation(xt_hi[:, kt, :], PS[:, bank, j * SEQ:(j + 1) * SEQ], ACT.Copy,
                                                   scale=gain[:, kt:kt + 1])
                    ins.then_inc(xhi_ready, 1)

            def ffn(u0, s0, tts, e=None, each=None):
                silu_at = {ffn_first(s) + 4: s for s in range(STEPS)}
                evac_at = {7 if s == 0 else 41 if s == STEPS - 1 else 6 * s + 6: s for s in range(STEPS)}
                for i in range(FFN_UNITS):
                    if i in silu_at:
                        s = s0 + silu_at[i]
                        act.wait_ge(used, count(u0 + ffn_first(silu_at[i]) + 2, e, FFN_UNITS))
                        if s:
                            act.wait_ge(mult_done, count(s, e, STEPS))
                        nc.scalar.activation(gated[:, 0:tts, :], PS[:, 0:tts, :], ACT.Silu).then_inc(silu_done, 1)
                    if i in evac_at:
                        s = s0 + evac_at[i]
                        act.wait_ge(act_t_done, count(s + 1, e, STEPS))
                        copy(ht_hi[evac_at[i] % 2][:, 0:tts, :, :],
                             PS[:, tts:2 * tts, :].rearrange("p t (f c) -> p t f c", f=FT)).then_inc(act_hi, 1)
                    if each:
                        each(i)
                    if i < AHEAD:
                        continue
                    split_hi(u0 + i, e)

            norm_rows(0)
            split_hi(0)
            act.wait_ge(gains_t, 1)
            copy(gains[:, :], PS[:, 7, 0:7 * KT]).then_inc(gains_ready, 1)
            norm_split(0)
            split_hi(1)
            act.wait_ge(a_landed, 48)
            q = slice(0, PAIRS)
            nc.scalar.activation(dt[q, :], log_step[q, :], ACT.Exp).then_inc(dt_done, 1)

            def evac_yt(h):
                act.wait_ge(yt_done, h + 1)
                for ft in range(FT):
                    ins = nc.scalar.activation(ht_hi[0][:, :, ft, :], PS[:, 2:4, ft * P:(ft + 1) * P], ACT.Copy,
                                               scale=g_gn[:, h * FT + ft:h * FT + ft + 1])
                ins.then_inc(yt_hi, 1)

            for h in range(HEADS):
                f0 = ret_first(h)
                last = RET_UNITS if h == HEADS - 1 else ret_first(h + 1)
                for n in range(f0, last):
                    if n == 3:
                        act.wait_ge(ar_done, 1)
                        nc.scalar.activation(par_in[q, 0, :], p1[q, :], ACT.Exp).then_inc(mag_done, 1)
                        act.wait_ge(angle_done, 1)
                        nc.scalar.activation(par_in[q, 1, :], p2[q, :], ACT.Sin, scale=0.5).then_inc(sin_done, 1)
                        nc.scalar.activation(par_in[q, 2, :], p2[q, :], ACT.Sin).then_inc(sin_done, 1)
                    if h and n == f0 + 1:
                        act.wait_ge(bn_done, h)
                        nc.scalar.activation(hstd[:, :], bn_a[:, :, 1], ACT.Sqrt, bias=eps).then_inc(hstd_done, 1)
                    if h and n == f0 + 3:
                        evac_yt(h - 1)
                    if n == f0 + 4:
                        act.wait_ge(used, f0 + 2)
                        copy(qk_t[:, :, :, :], PS[:, 0:2, :].rearrange("p a (b c) -> p a b c", b=2)).then_inc(qk_copied, 1)
                    if h and n == f0:
                        act.wait_ge(used, ret_first(h - 1) + 6)
                        if h > 1:
                            act.wait_ge(y_normed, h - 1)
                        nc.scalar.activation(gated[:, :, :], PS[:, 0:2, :], ACT.Silu).then_inc(g_silu, 1)
                    if h == 1 and n == f0 + 2:
                        act.wait_ge(par_t, 1)
                        copy(par[:, :, :], PS[:, 4, 0:5 * PAIRS].rearrange("p (a m) -> p a m", a=5)).then_inc(par_ready, 1)
                    if h == HEADS - 1 and n == f0 + 8:
                        act.wait_ge(used, f0 + 6)
                        act.wait_ge(y_normed, h)
                        nc.scalar.activation(gated[:, :, :], PS[:, 0:2, :], ACT.Silu).then_inc(g_silu, 1)
                    if h == HEADS - 1 and n == f0 + 9:
                        act.wait_ge(bn_done, HEADS)
                        nc.scalar.activation(hstd[:, :], bn_a[:, :, 1], ACT.Sqrt, bias=eps).then_inc(hstd_done, 1)
                    if n >= 2:
                        split_hi(n)
            evac_yt(HEADS - 1)

            for i in range(2):
                split_hi(FFN_U0 + i)
            norm_rows(1)
            norm_split(1)
            split_hi(FFN_U0 + 2)
            act.wait_ge(setup_done, 1)
            ffn(FFN_U0, 0, TT)

            for i in range(2):
                split_hi(S5_U0 + i)
            norm_rows(2)
            norm_split(2)
            def evac_turned(tables, copied):
                for j, t in enumerate(tables):
                    copy(t[:, :, :], PS[:, 4 + 2 * j:6 + 2 * j, :].rearrange("p a (b c) -> p (a b) c", c=P)).then_inc(copied, 1)

            for i in range(STEP):
                act.wait_ge(bt_done, i + 1)
                evac_turned(bt[i], bt_copied)
            def copy_u(c):
                act.wait_ge(used, S5_U0 + c + 1)
                copy(u_t[:, 2 * c:2 * c + 2, :], PS[:, U_BANK[c], :].rearrange("p (a b) -> p a b", a=2)).then_inc(u_copied, 1)

            def spread_u(q):
                act.wait_ge(u_copied, q + 1)
                if q:
                    act.wait_ge(bu_done, q)
                for i in range(4):
                    r = slice(32 * i, 32 * i + 32)
                    copy(spread[r, :, :, i, :],
                         u_t[r, QKT * q:QKT * q + QKT, :].rearrange("p k (c s) -> p k s c", s=STEP)).then_inc(spread_ready, 1)

            def magnitudes(q):
                c = slice(QPAIRS * q, QPAIRS * (q + 1))
                copy(mag_t[:, q, :, 1:FRAME], mag2[:, c].unsqueeze(2).to_broadcast([P, QPAIRS, FRAME - 1])).then_inc(mag_ready, 1)
                copy(mag_t[:, q, :, 0:1], cst[:, C_ZERO:C_ZERO + 1].unsqueeze(1).to_broadcast([P, QPAIRS, 1])).then_inc(mag_ready, 1)

            split_hi(S5_U0 + 2)
            copy_u(0)
            act.wait_ge(ct_done, 1)
            evac_turned(ct[0], ct_copied)
            copy_u(1)
            act.wait_ge(spread_zero, 1)
            spread_u(0)
            split_hi(S5_U0 + 3)
            copy_u(2)
            magnitudes(0)
            spread_u(1)
            copy_u(3)
            act.wait_ge(zero_ready, 1)
            act.wait_ge(direct_done, 1)
            for i in range(4):
                r = slice(32 * i, 32 * i + 32)
                copy(direct[r, :, r], PS[r, 7, 0:KT * 32].rearrange("p (k n) -> p k n", k=KT)).then_inc(direct_ready, 1)
            for q in range(1, QUARTERS):
                magnitudes(q)
            for q in range(QUARTERS):
                if q == QUARTERS - 1:
                    act.wait_ge(st_im_ready, QUARTERS)
                    split_hi(S5_U0 + 4)
                    split_hi(S5_U0 + 5)
                if q + 2 < QUARTERS:
                    spread_u(q + 2)
                k = slice(2 * q, 2 * q + 2)
                act.wait_ge(sy_added, q + 1)
                nc.scalar.activation(gelu_t[:, k, :], y_t[:, k, :], ACT.Gelu_apprx_tanh).then_inc(gelu_done, 1)
                act.wait_ge(gelu_done, q + 1)
                copy(xt_hi[:, k, :], gelu_t[:, k, :]).then_inc(xhi_ready, 1)
            act.wait_ge(sy_done, QUARTERS)
            split_hi(S5_U0 + 6)
            for n in range(7, S5_IN_UNITS + S5_OUT_UNITS):
                if n == 11:
                    act.wait_ge(used, S5_U0 + 8)
                    nc.scalar.activation(glu_gate[:, :, :], PS[:, 2:4, :], ACT.Sigmoid).then_inc(glu_sig, 1)
                split_hi(S5_U0 + n)
            for i in range(2):
                split_hi(MOE_U0 + i)
            act.wait_ge(used, MOE_U0)
            act.wait_ge(glu_read, 1)
            nc.scalar.activation(glu_gate[:, :, :], PS[:, 6:8, :], ACT.Sigmoid).then_inc(glu_sig, 1)

            norm_rows(3)
            split_hi(MOE_U0 + 2)
            act.wait_ge(hnt_done, 1)
            copy(hn_t[:, 0:4, :], PS[:, 0:2, :].rearrange("p a (b c) -> p (a b) c", c=SEQ)).then_inc(hnt_copied, 1)
            act.wait_ge(logits_done, 1)
            copy(hn_hi[:, :, :], hn[:, :, :]).then_inc(hn_hi_ready, 1)
            act.wait_ge(top_done, 1)
            for t in range(TT):
                nc.scalar.activation(r_exp[:, t, :], logit[:, t, :], ACT.Exp, bias=neg_top[:, t:t + 1]).then_inc(exp_done, 1)

            def gather_hi(g):
                act.wait_ge(gathered, g)
                copy(xg_hi[:, :, :], PS[:, 2:4, :].rearrange("p a (b c) -> p (a b) c", c=SLOTS)).then_inc(xg_hi_ready, 1)

            def experts(p):
                u0 = MOE_U0 + p * EXPERTS * FFN_UNITS
                gather_hi(9 * p + 1)
                if p:
                    for i in range(AHEAD):
                        split_hi(u0 + i)

                def expert(e, last):
                    def each(i):
                        if i == 2:
                            act.wait_ge(used, count(u0, e, FFN_UNITS))
                            copy(y_rows[:, 0:512], PS[:, 4, :]).then_inc(y0_copied, 1)
                        if i == 19:
                            act.wait_ge(put_t_done, count(8 * p + 1, e, 1))
                            copy(put_g[:, :, :], PS[:, 6, 0:2 * P].rearrange("p (a b) -> p a b", a=2)).then_inc(put_ready, 1)
                    ffn(u0, STEPS * (1 + EXPERTS * p), 1, e, each)
                    gather_hi(count(9 * p + 2, e, 1))
                    if not last:
                        for i in range(AHEAD):
                            split_hi(u0 + FFN_UNITS + i, e)

                expert(0, False)
                with act.Fori(1, EXPERTS - 1) as e:
                    expert(e, False)
                expert(EXPERTS - 1, True)
                act.wait_ge(used, u0 + EXPERTS * FFN_UNITS)
                copy(y_rows[:, 0:512], PS[:, 4, :]).then_inc(y0_copied, 1)

            experts(0)
            act.wait_ge(keys_done, 1)
            flag = act.value_load(over[0:1, 0:1], min_val=0, max_val=1)
            with act.If(flag > 0):
                experts(1)
            norm_rows(4)

        @block.vector
        def _(dve):
            n_self = [0]

            def link(ins):
                n_self[0] += 1
                ins.then_inc(dve_self, 1)
                dve.wait_ge(dve_self, n_self[0])

            def tt(o, a, b, op):
                return nc.vector.tensor_tensor(o, a, b, op)

            def split_lo(n, e=None):
                dve.wait_ge(hi_ready, count(n + 1, e, FFN_UNITS))
                tt(w_lo[:, n % SPLIT, :], raw_unit(n, e), w_hi[:, n % SPLIT, :].bitcast(F32),
                   ALU.subtract).then_inc(lo_ready, 1)

            def norm_rows(i):
                if i == 0:
                    dve.wait_ge(x_landed[1], 16)
                else:
                    dve.wait_ge(resid_ready, i)
                nc.vector.scalar_tensor_tensor(out=hn[:, 1, :], in0=resid[:, 1, :], scalar=1.0, in1=resid[:, 1, :],
                                               op0=ALU.mult, op1=ALU.mult, accum_out=ssq[:, 1:2]).then_inc(ssq1_done, 1)
                dve.wait_ge(std_done, i + 1)
                nc.vector.reciprocal(rstd[:, :], std[:, :]).then_inc(rstd_done, 1)
                dve.wait_ge(rstd_done, i + 1)
                if i < 3:
                    nc.vector.tensor_scalar(hn[:, 0, :], resid[:, 0, :], rstd[:, 0:1], None, ALU.mult).then_inc(hn0_ready, 1)

            def norm_split(i):
                gain = (gains[:, 0:KT], gains[:, 2 * KT:3 * KT], gains[:, KT:2 * KT])[i]
                dve.wait_ge(gains_ready, 1)
                for bank in range(KT // 2):
                    dve.wait_ge(xhi_ready, KT // 2 * i + bank + 1)
                    for j in range(2):
                        kt = 2 * bank + j
                        ins = nc.vector.scalar_tensor_tensor(
                            out=xt_lo[:, kt, :], in0=PS[:, bank, j * SEQ:(j + 1) * SEQ], scalar=gain[:, kt:kt + 1],
                            in1=xt_hi[:, kt, :].bitcast(F32), op0=ALU.mult, op1=ALU.subtract)
                    ins.then_inc(xlo_ready, 1)

            def ffn(u0, s0, tts, e=None, each=None):
                mult_at = {ffn_first(s) + 6: s for s in range(STEPS)}
                evac_at = {7 if s == 0 else 41 if s == STEPS - 1 else 6 * s + 6: s for s in range(STEPS)}
                for i in range(FFN_UNITS):
                    if i in mult_at:
                        s = s0 + mult_at[i]
                        dve.wait_ge(silu_done, count(s + 1, e, STEPS))
                        dve.wait_ge(used, count(u0 + ffn_first(mult_at[i]) + 4, e, FFN_UNITS))
                        if s:
                            dve.wait_ge(act_t_done, count(s, e, STEPS))
                        tt(act_rows[:, 0:tts, :], gated[:, 0:tts, :], PS[:, tts:2 * tts, :], ALU.mult).then_inc(mult_done, 1)
                    if i in evac_at:
                        s = s0 + evac_at[i]
                        dve.wait_ge(act_hi, count(s + 1, e, STEPS))
                        b = evac_at[i] % 2
                        for t in range(tts):
                            ins = tt(ht_lo[b][:, t, :, :], PS[:, tts + t, :].rearrange("p (f c) -> p f c", f=FT),
                                     ht_hi[b][:, t, :, :].bitcast(F32), ALU.subtract)
                        ins.then_inc(act_lo, 1)
                    if each:
                        each(i)
                    if i < AHEAD:
                        continue
                    split_lo(u0 + i, e)

            def add_out():
                for t in range(TT):
                    ins = tt(resid[:, t, :], resid[:, t, :], PS[:, 4 + 2 * t:6 + 2 * t, :].rearrange("p a b -> p (a b)"), ALU.add)
                ins.then_inc(resid_ready, 1)

            nc.vector.memset(unused[:, :], 1.0).then_inc(unused_set, 1)
            norm_rows(0)
            split_lo(0)
            norm_split(0)
            split_lo(1)

            def decay(h):
                dve.wait_ge(scores_done, h + 1)
                if h == 0:
                    dve.wait_ge(c2_landed, 16)
                c = C_DECAY + h * SEQ
                tt(scores[:, 0:SEQ], PS[:, 2, 0:SEQ], cst[:, c:c + SEQ], ALU.mult)
                tt(scores[:, SEQ:SEQ + P], PS[:, 2, SEQ:SEQ + P], cst[:, c:c + P], ALU.mult).then_inc(decayed, 1)

            def group_norm(h):
                dve.wait_ge(y_done, h + 1)
                for t in range(TT):
                    link(nc.vector.bn_stats(bn_s[:, t, :], PS[:, 3 - t, :]))
                for t in range(TT):
                    ins = nc.vector.bn_aggr(bn_a[:, t, :], bn_s[:, t, :])
                ins.then_inc(bn_done, 1)
                dve.wait_ge(hstd_done, h + 1)
                link(nc.vector.reciprocal(hrstd[:, :], hstd[:, :]))
                for t in range(TT):
                    link(nc.vector.tensor_scalar(act_rows[:, t, :], PS[:, 3 - t, :], bn_a[:, t, 0:1], hrstd[:, t:t + 1],
                                                 ALU.subtract, ALU.mult))
                dve.wait_ge(g_silu, h + 1)
                tt(act_rows[:, :, :], act_rows[:, :, :], gated[:, :, :], ALU.mult).then_inc(y_normed, 1)

            def evac_yt(h):
                dve.wait_ge(yt_hi, h + 1)
                for ft in range(FT):
                    ins = nc.vector.scalar_tensor_tensor(
                        out=ht_lo[0][:, :, ft, :], in0=PS[:, 2:4, ft * P:(ft + 1) * P], scalar=g_gn[:, h * FT + ft:h * FT + ft + 1],
                        in1=ht_hi[0][:, :, ft, :].bitcast(F32), op0=ALU.mult, op1=ALU.subtract)
                ins.then_inc(yt_lo, 1)

            for h in range(HEADS):
                f0 = ret_first(h)
                last = RET_UNITS if h == HEADS - 1 else ret_first(h + 1)
                for n in range(f0, last):
                    if n == 3:
                        dve.wait_ge(den_done, 1)
                        nc.vector.reciprocal(p6[0:PAIRS, :], p4[0:PAIRS, :]).then_inc(rden_done, 1)
                    if h and n == f0:
                        decay(h - 1)
                    if h and n == f0 + 1:
                        group_norm(h - 1)
                    if h and n == f0 + 3:
                        evac_yt(h - 1)
                    if n == f0 + 6 and h:
                        dve.wait_ge(used, f0 + 4)
                        nc.vector.tensor_copy(v_rows[:, :, :], PS[:, 2:4, :]).then_inc(v_copied, 1)
                    if h == HEADS - 1 and n == f0 + 8:
                        decay(h)
                    if h == HEADS - 1 and n == f0 + 9:
                        group_norm(h)
                    if n >= 2:
                        split_lo(n)
                if h == 0:
                    dve.wait_ge(used, f0 + 4)
                    nc.vector.tensor_copy(v_rows[:, :, :], PS[:, 2:4, :]).then_inc(v_copied, 1)
            evac_yt(HEADS - 1)

            for i in range(2):
                split_lo(FFN_U0 + i)
            dve.wait_ge(used, FFN_U0)
            add_out()
            norm_rows(1)
            norm_split(1)
            split_lo(FFN_U0 + 2)
            ffn(FFN_U0, 0, TT)

            for i in range(2):
                split_lo(S5_U0 + i)
            dve.wait_ge(used, S5_U0)
            add_out()
            norm_rows(2)
            norm_split(2)
            split_lo(S5_U0 + 2)
            dve.wait_ge(used, S5_U0 + 2)
            nc.vector.memset(spread[:, :, :, :], 0.0).then_inc(spread_zero, 1)
            split_lo(S5_U0 + 3)

            def add_y(q):
                dve.wait_ge(sy_done, q + 1)
                for j in range(2):
                    k = 2 * q + j
                    ins = nc.vector.scalar_tensor_tensor(out=y_t[:, k, :], in0=u_t[:, k, :], scalar=d_skip[:, k:k + 1],
                                                         in1=PS[:, 4 + q, j * SEQ:(j + 1) * SEQ], op0=ALU.mult, op1=ALU.add)
                ins.then_inc(sy_added, 1)

            def gelu_lo(q):
                k = slice(2 * q, 2 * q + 2)
                dve.wait_ge(xhi_ready, 3 * (KT // 2) + q + 1)
                tt(xt_lo[:, k, :], gelu_t[:, k, :], xt_hi[:, k, :].bitcast(F32), ALU.subtract).then_inc(xlo_ready, 1)

            def by_frame(t):
                return t.rearrange("p h (m s) -> p h m s", s=FRAME)

            def table(t, q):
                return t[:, q, :].rearrange("p (m s) -> p m s", s=FRAME).unsqueeze(1).to_broadcast([P, FRAMES, QPAIRS, FRAME])

            re, im, tmp = by_frame(scan[:, 0]), by_frame(scan[:, 1]), by_frame(scan_tmp[:, :, :])
            bu_re, bu_im = (PS[:, 2 * j:2 * j + 2, :].rearrange("p a (m h s) -> p h (a m) s", h=FRAMES, s=FRAME)
                            for j in range(2))
            dve.wait_ge(used, S5_U0 + 2)
            for q in range(QUARTERS):
                cos, sin = table(cos_t, q), table(sin_t, q)
                dve.wait_ge(bu_done, q + 1)
                tt(re, bu_re, cos, ALU.mult)
                link(tt(im, bu_im, sin, ALU.mult))
                link(tt(re, re, im, ALU.add))
                tt(im, bu_im, cos, ALU.mult)
                tt(tmp, bu_re, sin, ALU.mult).then_inc(bu_read, 1)
                dve.wait_ge(bu_read, q + 1)
                link(tt(im, im, tmp, ALU.subtract))
                dve.wait_ge(mag_ready, 2 * q + 2)
                for f in range(FRAMES):
                    first = scan[:, :, f, :].rearrange("p j (m s) -> p j m s", s=FRAME)[:, :, :, 0]
                    if f:
                        last = scan[:, :, f - 1, :].rearrange("p j (m s) -> p j m s", s=FRAME)[:, :, :, FRAME - 1]
                        for j, turn in enumerate((turn_re, turn_im)):
                            ins = tt(car[:, j], last, turn[:, q * QPAIRS:(q + 1) * QPAIRS].unsqueeze(1).to_broadcast(
                                [P, 2, QPAIRS]), ALU.mult)
                        link(ins)
                        link(tt(first, first, car[:, 0], ALU.add))
                        tt(first[:, 0], first[:, 0], car[:, 1, 1], ALU.subtract)
                        link(tt(first[:, 1], first[:, 1], car[:, 1, 0], ALU.add))
                    for j in range(2):
                        ins = nc.vector.tensor_tensor_scan(scan[:, j, f, :], mag_t[:, q, :, :].rearrange("p m s -> p (m s)"), scan[:, j, f, :], 0.0,
                                                           ALU.mult, ALU.add)
                    if f < FRAMES - 1:
                        link(ins)
                ins.then_inc(scans_done, 1)
                dve.wait_ge(scans_done, q + 1)
                if q == 0:
                    dve.wait_ge(used, S5_U0 + 3)
                if q == 1:
                    dve.wait_ge(used, S5_U0 + 4)
                if q >= 2:
                    dve.wait_ge(sy_done, q - 1)
                x_re, x_im = (by_frame(states[q % 2][:, j]) for j in range(2))
                tt(x_re, re, cos, ALU.mult)
                link(tt(tmp, im, sin, ALU.mult))
                tt(x_re, x_re, tmp, ALU.subtract).then_inc(st_re_ready, 1)
                tt(x_im, im, cos, ALU.mult).then_inc(im_part_ready, 1)
                dve.wait_ge(turned_ready, q + 1)
                dve.wait_ge(im_part_ready, q + 1)
                if q == QUARTERS - 1:
                    tt(x_im, x_im, by_frame(turned[:, :, :]), ALU.add).then_inc(st_im_ready, 1)
                if q:
                    add_y(q - 1)
            gelu_lo(0)
            gelu_lo(1)
            dve.wait_ge(st_im_ready, QUARTERS)
            split_lo(S5_U0 + 4)
            split_lo(S5_U0 + 5)
            add_y(QUARTERS - 1)
            gelu_lo(2)
            gelu_lo(3)
            split_lo(S5_U0 + 6)

            def glu(dh):
                dve.wait_ge(glu_sig, dh + 1)
                link(tt(glu_out[:, :, :], glu_gate[:, :, :], PS[:, 4 * dh:4 * dh + 2, :], ALU.mult))
                return tt(resid[:, :, dh * 512:dh * 512 + 512], resid[:, :, dh * 512:dh * 512 + 512],
                          glu_out[:, :, :], ALU.add)

            for n in range(7, S5_IN_UNITS + S5_OUT_UNITS):
                if n == 11:
                    glu(0).then_inc(glu_read, 1)
                split_lo(S5_U0 + n)
            for i in range(2):
                split_lo(MOE_U0 + i)
            dve.wait_ge(glu_read, 1)
            glu(1).then_inc(resid_ready, 1)

            norm_rows(3)
            dve.wait_ge(moe_landed, 32)
            dve.wait_ge(ssq0_done, 4)
            for t, ready in enumerate((hn0_ready, hn1_ready)):
                nc.vector.scalar_tensor_tensor(out=hn[:, t, :], in0=resid[:, t, :], scalar=rstd[:, t:t + 1], in1=gain_row[:, :],
                                               op0=ALU.mult, op1=ALU.mult).then_inc(ready, 1)
            split_lo(MOE_U0 + 2)
            dve.wait_ge(hnt_done, 2)
            nc.vector.tensor_copy(hn_t[:, 4:8, :], PS[:, 2:4, :].rearrange("p a (b c) -> p (a b) c", c=SEQ)).then_inc(hnt_copied, 1)
            nc.vector.memset(PS[:, 4, :], 0.0)
            nc.vector.memset(PS[:, 5, :], 0.0)
            nc.vector.memset(put_g[:, :, :], 0.0).then_inc(put_ready, 1)
            dve.wait_ge(logits_done, 1)
            link(nc.vector.tensor_copy(logit[:, :, :], PS[:, 6, 0:TT * EXPERTS].rearrange("p (t e) -> p t e", t=TT)))
            for t in range(TT):
                link(nc.vector.max(top[:, t, :], logit[:, t, :]))
            nc.vector.tensor_scalar(neg_top[:, :], top[:, :, 0], -1.0, None, ALU.mult).then_inc(top_done, 1)
            for t in range(TT):
                second = top[:, t, 1:2]
                nc.vector.tensor_scalar(r_gt[:, t, :], logit[:, t, :], second, None, ALU.is_gt)
                link(nc.vector.tensor_scalar(r_eq[:, t, :], logit[:, t, :], second, None, ALU.is_equal))
                nc.vector.tensor_tensor_scan(r_cum[:, t, :], ones[:, 0:EXPERTS], r_eq[:, t, :], 0.0, ALU.mult, ALU.add)
            link(nc.vector.tensor_reduce(r_n[:, :], r_gt[:, :, :], AX_X, ALU.add))
            link(nc.vector.tensor_scalar(r_n[:, :], r_n[:, :], -1.0, 2.0, ALU.mult, ALU.add))
            for t in range(TT):
                link(nc.vector.tensor_scalar(r_cum[:, t, :], r_cum[:, t, :], r_n[:, t:t + 1], None, ALU.is_le))
            link(tt(r_eq[:, :, :], r_eq[:, :, :], r_cum[:, :, :], ALU.mult))
            tt(chosen[:, :, :], r_gt[:, :, :], r_eq[:, :, :], ALU.add).then_inc(chosen_done, 1)
            dve.wait_ge(chosen_done, 1)
            dve.wait_ge(exp_done, TT)
            link(tt(r_exp[:, :, :], r_exp[:, :, :], chosen[:, :, :], ALU.mult))
            link(nc.vector.tensor_reduce(r_n[:, :], r_exp[:, :, :], AX_X, ALU.add))
            link(nc.vector.reciprocal(r_n[:, :], r_n[:, :]))
            for t in range(TT):
                link(nc.vector.tensor_scalar(gate_w[:, t, :], r_exp[:, t, :], r_n[:, t:t + 1], None, ALU.mult))
            dve.wait_ge(rank_done, 1)
            link(nc.vector.tensor_scalar(r_cum[:, :, :], PS[:, 6, 32:32 + TT * EXPERTS].rearrange("p (t e) -> p t e", t=TT),
                                         1.0, None, ALU.add))
            for b in range(2):
                link(nc.vector.memset(key[b][:, :, :], -1.0))
            link(tt(r_cum[:, :, :], r_cum[:, :, :], chosen[:, :, :], ALU.mult))
            link(nc.vector.tensor_scalar(key[0][:, :, 0:EXPERTS], r_cum[:, :, :], 1.0, None, ALU.subtract))
            link(nc.vector.tensor_scalar(key[1][:, :, 0:EXPERTS], r_cum[:, :, :], 1.0 + SLOTS, None, ALU.subtract))
            link(nc.vector.tensor_reduce(most[:, :], PS[:, 6, 64:64 + EXPERTS], AX_X, ALU.max))
            link(nc.vector.tensor_scalar(most[:, :], most[:, :], float(SLOTS), None, ALU.is_gt))
            nc.vector.tensor_copy(over[:, :], most[:, :]).then_inc(keys_done, 1)
            dve.wait_ge(keys_done, 1)

            def column(e):
                return slice(e, e + 1) if isinstance(e, int) else bass.ds(e, 1)

            def make_pick(b, col):
                for t in range(TT):
                    ins = nc.vector.tensor_scalar(pick[:, t, :], iota, key[b][:, t, col], None, ALU.is_equal)
                ins.then_inc(pick_ready, 1)

            def gather_lo(g):
                dve.wait_ge(xg_hi_ready, g)
                tt(xg_lo[:, :, :], PS[:, 2:4, :].rearrange("p a (b c) -> p (a b) c", c=SLOTS), xg_hi[:, :, :].bitcast(F32),
                   ALU.subtract).then_inc(xg_lo_ready, 1)

            def add_scattered(n):
                dve.wait_ge(scattered, n)
                tt(resid[:, 0, :], resid[:, 0, :], PS[:, 2:4, :].rearrange("p a b -> p (a b)"), ALU.add)
                tt(resid[:, 1, :], resid[:, 1, :], PS[:, 6:8, :].rearrange("p a b -> p (a b)"), ALU.add).then_inc(scatter_added, 1)

            def experts(p):
                u0 = MOE_U0 + p * EXPERTS * FFN_UNITS
                if p:
                    nc.vector.memset(put_g[:, :, :], 0.0).then_inc(put_ready, 1)
                make_pick(p, slice(0, 1))
                gather_lo(9 * p + 1)
                if p:
                    for i in range(AHEAD):
                        split_lo(u0 + i)

                def expert(e, last):
                    def each(i):
                        if i == 2:
                            dve.wait_ge(used, count(u0, e, FFN_UNITS))
                            nc.vector.tensor_copy(y_rows[:, 512:1024], PS[:, 5, :]).then_inc(y1_copied, 1)
                            make_pick(p, column(e + 1))
                        if i == 8:
                            add_scattered(count(9 * p + 1, e, 1))
                        if i == 10:
                            for t in range(TT):
                                ins = nc.vector.tensor_scalar(pick_g[:, t, :], iota, key[p][:, t, column(e)],
                                                              gate_w[:, t, column(e)], ALU.is_equal, ALU.mult)
                            ins.then_inc(pick_g_ready, 1)
                    ffn(u0, STEPS * (1 + EXPERTS * p), 1, e, each)
                    gather_lo(count(9 * p + 2, e, 1))
                    if not last:
                        for i in range(AHEAD):
                            split_lo(u0 + FFN_UNITS + i, e)

                expert(0, False)
                with dve.Fori(1, EXPERTS - 1) as e:
                    expert(e, False)
                expert(EXPERTS - 1, True)
                dve.wait_ge(used, u0 + EXPERTS * FFN_UNITS)
                nc.vector.tensor_copy(y_rows[:, 512:1024], PS[:, 5, :]).then_inc(y1_copied, 1)
                add_scattered(9 * p + 9)
                dve.wait_ge(scatter_added, 9 * p + 9)

            experts(0)
            flag = dve.value_load(over[0:1, 0:1], min_val=0, max_val=1)
            with dve.If(flag > 0):
                experts(1)
            nc.vector.memset(ssq[:, :], 0.0).then_inc(resid_ready, 1)
            norm_rows(4)
            dve.wait_ge(ssq0_done, 5)
            dve.wait_ge(fin_landed, 16)
            for t in range(TT):
                nc.vector.scalar_tensor_tensor(out=hn[:, t, :], in0=resid[:, t, :], scalar=rstd[:, t:t + 1],
                                               in1=final_gain[:, :], op0=ALU.mult, op1=ALU.mult).then_inc(out_ready, 1)

        @block.tensor
        def _(pe):
            def mm(o, l, r, start, stop):
                return nc.tensor.matmul(o, l, r, start=start, stop=stop)

            def split_ready(n, e=None):
                pe.wait_ge(lo_ready, count(n + 1, e, FFN_UNITS))

            def product3(o, l_hi, l_lo, r_hi, r_lo, start, stop):
                mm(o, l_hi, r_hi, start, False)
                mm(o, l_hi, r_lo, False, False)
                return mm(o, l_lo, r_hi, False, stop)

            def rows_unit(n, half, banks, x_hi, x_lo, e=None, norm_i=None):
                split_ready(n, e)
                hi = w_hi[:, n % SPLIT, :].rearrange("p (k n) -> p k n", k=4)
                lo = w_lo[:, n % SPLIT, :].rearrange("p (k n) -> p k n", k=4)
                for k in range(4):
                    kt = 4 * half + k
                    x_ready(norm_i, kt)
                    for t, bank in enumerate(banks):
                        cols = slice(t * P, (t + 1) * P)
                        ins = product3(PS[:, bank, :], x_hi[:, kt, cols], x_lo[:, kt, cols], hi[:, k, :], lo[:, k, :],
                                       kt == 0, kt == KT - 1)
                ins.then_inc(used, 1)

            def cols_unit(n, bank, norm_i=None):
                split_ready(n)
                hi = w_hi[:, n % SPLIT, :].rearrange("p (k n) -> p k n", k=KT)
                lo = w_lo[:, n % SPLIT, :].rearrange("p (k n) -> p k n", k=KT)
                for j in range(2):
                    o = PS[:, bank, j * SEQ:(j + 1) * SEQ]
                    for kt in range(KT):
                        if j == 0:
                            x_ready(norm_i, kt)
                        c = slice(j * P, (j + 1) * P)
                        mm(o, hi[:, kt, c], xt_hi[:, kt, :], kt == 0, False)
                        mm(o, hi[:, kt, c], xt_lo[:, kt, :], False, False)
                        ins = mm(o, lo[:, kt, c], xt_hi[:, kt, :], False, kt == KT - 1)
                ins.then_inc(used, 1)

            def out_unit(n, half, tts, a_hi, a_lo, first, last, e=None):
                split_ready(n, e)
                hi = w_hi[:, n % SPLIT, :].rearrange("p (k n) -> p k n", k=2)
                lo = w_lo[:, n % SPLIT, :].rearrange("p (k n) -> p k n", k=2)
                for k in range(2):
                    ft = 2 * half + k
                    for t in range(tts):
                        for dh in range(2):
                            c = slice(dh * 512, dh * 512 + 512)
                            ins = product3(PS[:, out_bank(t, dh), :], a_hi[:, t, ft, :], a_lo[:, t, ft, :],
                                           hi[:, k, c], lo[:, k, c], first and ft == 0, last and ft == FT - 1)
                ins.then_inc(used, 1)

            def transposes(i):
                pe.wait_ge(hn0_ready, i + 1)
                pe.wait_ge(hn1_ready, i + 1)
                for kt in range(KT):
                    for t in range(TT):
                        c = kt % 2 * SEQ + t * P
                        ins = nc.tensor.transpose(PS[:, kt // 2, c:c + P], hn[:, t, kt * P:(kt + 1) * P], ident)
                    yield kt, ins

            def norm(i):
                for kt, ins in transposes(i):
                    if kt % 2:
                        ins.then_inc(xt_done, 1)

            def x_ready(i, kt):
                if i is not None and kt % 2 == 0:
                    pe.wait_ge(xlo_ready, KT // 2 * i + max(2, kt // 2 + 1))

            def turn_rows(banks):
                for t, bank in enumerate(banks):
                    for ft in range(FT):
                        ins = nc.tensor.transpose(PS[:, bank, ft * P:(ft + 1) * P],
                                                  act_rows[:, t, ft * P:(ft + 1) * P], ident)
                return ins

            def ffn(u0, s0, tts, x_hi, x_lo, e=None, after_up0=None, each=None, before_last=None):
                def turn(s):
                    pe.wait_ge(mult_done, count(s0 + s + 1, e, STEPS))
                    turn_rows(up_banks(tts)).then_inc(act_t_done, 1)

                def down(s, half, i):
                    if half == 0:
                        pe.wait_ge(act_lo, count(s0 + s + 1, e, STEPS))
                    out_unit(u0 + i, half, tts, ht_hi[s % 2], ht_lo[s % 2], s == 0, s == STEPS - 1, e)

                for s in range(STEPS):
                    f0 = ffn_first(s)
                    if s0 + s:
                        pe.wait_ge(silu_done, count(s0 + s, e, STEPS))
                    for half in range(2):
                        rows_unit(u0 + f0 + half, half, gate_banks(tts), x_hi, x_lo, e,
                                  1 if u0 == FFN_U0 and s == 0 else None)
                    if s0 + s:
                        pe.wait_ge(act_lo, count(s0 + s, e, STEPS))
                    for half in range(2):
                        rows_unit(u0 + f0 + 2 + half, half, up_banks(tts), x_hi, x_lo, e)
                    if s == 0:
                        if after_up0:
                            after_up0()
                        turn(0)
                        continue
                    down(s - 1, 0, f0 + 4)
                    turn(s)
                    if each:
                        each(s)
                    down(s - 1, 1, f0 + 5)
                if before_last:
                    before_last()
                down(STEPS - 1, 0, FFN_UNITS - 2)
                down(STEPS - 1, 1, FFN_UNITS - 1)

            pe.wait_ge(c_landed, 16)
            norm(0)
            pe.wait_ge(g_landed, 64)
            nc.tensor.transpose(PS[:, 7, 0:7 * KT], gain_rows[0:7 * KT, :],
                                cst[0:7 * KT, C_IDENT:C_IDENT + 7 * KT]).then_inc(gains_t, 1)

            def turn_y(h):
                pe.wait_ge(y_normed, h + 1)
                turn_rows([2, 3]).then_inc(yt_done, 1)

            def head_out(h, half, n):
                if half == 0:
                    pe.wait_ge(yt_lo, h + 1)
                    pe.wait_ge(par_ready, 1)
                out_unit(n, half, TT, ht_hi[0], ht_lo[0], h == 0, h == HEADS - 1)

            for h in range(HEADS):
                f0 = ret_first(h)
                if h:
                    pe.wait_ge(g_silu, h)
                cols_unit(f0, 0, 0 if h == 0 else None)
                if h:
                    turn_y(h - 1)
                cols_unit(f0 + 1, 1)
                if h:
                    pe.wait_ge(yt_lo, h)
                for half in range(2):
                    rows_unit(f0 + 2 + half, half, (2, 3), xt_hi, xt_lo)
                pe.wait_ge(qk_copied, h + 1)
                for half in range(2):
                    rows_unit(f0 + 4 + half, half, (0, 1), xt_hi, xt_lo)
                pe.wait_ge(v_copied, h + 1)
                for dt_i in range(2):
                    mm(PS[:, 2, 0:SEQ], qk_t[:, 1, dt_i, 0:P], qk_t[:, 0, dt_i, :], dt_i == 0, dt_i == 1)
                for dt_i in range(2):
                    ins = mm(PS[:, 2, SEQ:SEQ + P], qk_t[:, 1, dt_i, P:SEQ], qk_t[:, 0, dt_i, P:SEQ], dt_i == 0, dt_i == 1)
                ins.then_inc(scores_done, 1)
                if h:
                    head_out(h - 1, 0, f0 + 6)
                pe.wait_ge(decayed, h + 1)
                mm(PS[:, 3, :], scores[:, 0:P], v_rows[:, 0, :], True, True)
                mm(PS[:, 2, :], scores[:, P:SEQ], v_rows[:, 0, :], True, False)
                mm(PS[:, 2, :], scores[:, SEQ:SEQ + P], v_rows[:, 1, :], False, True).then_inc(y_done, 1)
                if h:
                    head_out(h - 1, 1, f0 + 7)
                if h == 0:
                    pe.wait_ge(par_done, 1)
                    for i in range(5):
                        ins = nc.tensor.transpose(PS[:, 4, i * PAIRS:(i + 1) * PAIRS], par_in[0:PAIRS, i, :],
                                                  cst[0:PAIRS, C_IDENT:C_IDENT + PAIRS])
                    ins.then_inc(par_t, 1)
            turn_y(HEADS - 1)
            for half in range(2):
                head_out(HEADS - 1, half, RET_UNITS - 2 + half)

            norm(1)
            ffn(FFN_U0, 0, TT, xt_hi, xt_lo)

            norm(2)
            pe.wait_ge(setup_done, 1)
            def turn_b(i):
                for j, src in enumerate(bb[i]):
                    for k in range(KT):
                        ins = nc.tensor.transpose(PS[:, 4 + 2 * j + k // 4, k % 4 * P:(k % 4 + 1) * P],
                                                  src[:, 4 * k:4 * k + 4, :].rearrange("p a b -> p (a b)"), ident)
                ins.then_inc(bt_done, 1)

            turn_b(0)
            cols_unit(S5_U0, 0, 2)
            pe.wait_ge(bt_copied, 2)
            turn_b(1)
            cols_unit(S5_U0 + 1, 1)
            pe.wait_ge(bt_copied, 4)
            pe.wait_ge(c_padded, 4)
            for j, src in enumerate(cc):
                for k in range(KT):
                    ins = nc.tensor.transpose(PS[:, 4 + 2 * j + k // 4, k % 4 * P:(k % 4 + 1) * P], src[:, k, :], ident)
            ins.then_inc(ct_done, 1)
            cols_unit(S5_U0 + 2, U_BANK[2])

            def rows32(m):
                return slice(32 * (m % 4), 32 * (m % 4) + 32)

            def s5_in(q):
                pe.wait_ge(spread_ready, 4 * q + 4)
                for j in range(2):
                    for a in range(QKT):
                        k = QKT * q + a
                        if q == 0 and 2 * j + a in U_BANK:
                            pe.wait_ge(u_copied, U_BANK.index(2 * j + a) + 1)
                        o = PS[:, 2 * j + a, :].rearrange("p (i c) -> p i c", i=4)
                        mm(o, bt[0][j][:, k, :], spread[:, a, 0, :, :], True, False)
                        ins = mm(o[:, :, 1:KEPT], bt[1][j][:, k, :], spread[:, a, 1, :, 0:KEPT - 1], False, True)
                ins.then_inc(bu_done, 1)

            s5_in(0)
            pe.wait_ge(ct_copied, 2)
            cols_unit(S5_U0 + 3, U_BANK[3])
            pe.wait_ge(ct_copied, 2)
            for m in range(PAIRS):
                r = rows32(m)
                o = PS[r, 7, m // 4 * 32:m // 4 * 32 + 32]
                mm(o, bb[0][0][:, m, :], ct[0][0][:, m // 4, r], True, False)
                ins = mm(o, bb[0][1][:, m, :], ct[0][1][:, m // 4, r], False, True)
            ins.then_inc(direct_done, 1)
            for q in range(QUARTERS):
                if q + 1 < QUARTERS:
                    pe.wait_ge(bu_read, q + 1)
                    s5_in(q + 1)
                if q == 0:
                    pe.wait_ge(u_copied, S5_IN_UNITS)
                    pe.wait_ge(direct_ready, 4)
                    pe.wait_ge(ct1_ready, 4)
                y = PS[:, 4 + q, :].rearrange("p (k s two) -> p k two s", k=2, two=STEP)
                pe.wait_ge(st_re_ready, q + 1)
                pe.wait_ge(st_im_ready, q + 1)
                for m in range(q * QPAIRS, (q + 1) * QPAIRS):
                    r, k = rows32(m), m // 4
                    for i in range(STEP):
                        o = y[r, k % 2, i, :]
                        if i:
                            mm(o, direct[:, k, r], u_t[:, k, 1::2], True, False)
                        for j in range(2):
                            x = states[q % 2][:, j, :, m % QPAIRS * FRAME:(m % QPAIRS + 1) * FRAME]
                            ins = mm(o.rearrange("p (h s) -> p h s", h=FRAMES), ct[i][j][:, k, r], x, i == 0 and j == 0, j == 1)
                ins.then_inc(sy_done, 1)
            n = S5_U0 + S5_IN_UNITS
            for dh in range(2):
                for part in range(2):
                    for half in range(2):
                        pe.wait_ge(xlo_ready, 3 * (KT // 2) + 2 * half + 2)
                        rows_unit(n, half, (4 * dh + 2 * part, 4 * dh + 2 * part + 1), xt_hi, xt_lo)
                        n += 1

            for kt, ins in transposes(3):
                if kt % 4 == 3:
                    ins.then_inc(hnt_done, 1)
            pe.wait_ge(hnt_copied, 2)
            pe.wait_ge(moe_landed, 32)
            for t in range(TT):
                for kt in range(KT):
                    ins = mm(PS[:, 6, t * EXPERTS:(t + 1) * EXPERTS], hn_t[:, kt, t * P:(t + 1) * P], router[:, kt, :],
                             kt == 0, kt == KT - 1)
            ins.then_inc(logits_done, 1)
            pe.wait_ge(chosen_done, 1)
            mm(PS[:, 6, 32:32 + EXPERTS], tri, chosen[:, 0, :], True, True)
            mm(PS[:, 6, 40:40 + EXPERTS], ones, chosen[:, 0, :], True, False)
            mm(PS[:, 6, 40:40 + EXPERTS], tri, chosen[:, 1, :], False, True)
            mm(PS[:, 6, 64:64 + EXPERTS], ones, chosen[:, 0, :], True, False)
            mm(PS[:, 6, 64:64 + EXPERTS], ones, chosen[:, 1, :], False, True).then_inc(rank_done, 1)

            def gather(n):
                pe.wait_ge(pick_ready, n)
                pe.wait_ge(hn_lo_ready, 1)
                for kt in range(KT):
                    for t in range(TT):
                        o = PS[:, 2 + kt // 4, kt % 4 * P:(kt % 4 + 1) * P]
                        mm(o, hn_hi[:, t, kt * P:(kt + 1) * P], pick[:, t, :], t == 0, False)
                        ins = mm(o, hn_lo[:, t, kt * P:(kt + 1) * P], pick[:, t, :], False, t == TT - 1)
                ins.then_inc(gathered, 1)

            def scatter(n):
                pe.wait_ge(y0_copied, n)
                pe.wait_ge(y1_copied, n)
                pe.wait_ge(put_ready, n)
                for t in range(TT):
                    for dh in range(2):
                        ins = mm(PS[:, 2 + 4 * t + dh, :], put_g[:, t, :], y_rows[:, dh * 512:dh * 512 + 512], True, True)
                ins.then_inc(scattered, 1)

            def experts(p):
                u0 = MOE_U0 + p * EXPERTS * FFN_UNITS
                gather(9 * p + 1)

                def expert(e):
                    pe.wait_ge(xg_lo_ready, count(9 * p + 1, e, 1))

                    def after_up0():
                        scatter(count(9 * p + 1, e, 1))

                    def each(s):
                        if s == 2:
                            pe.wait_ge(pick_g_ready, count(8 * p + 1, e, 1))
                            pe.wait_ge(scatter_added, count(9 * p + 1, e, 1))
                            for t in range(TT):
                                ins = nc.tensor.transpose(PS[:, 6, t * P:(t + 1) * P], pick_g[:, t, :], ident)
                            ins.then_inc(put_t_done, 1)

                    def before_last():
                        gather(count(9 * p + 2, e, 1))

                    ffn(u0, STEPS * (1 + EXPERTS * p), 1, xg_hi, xg_lo, e, after_up0, each, before_last)

                expert(0)
                with pe.Fori(1, EXPERTS - 1) as e:
                    expert(e)
                expert(EXPERTS - 1)
                pe.wait_ge(xg_lo_ready, 9 * p + 9)
                scatter(9 * p + 9)
                pe.wait_ge(scatter_added, 9 * p + 9)

            experts(0)
            pe.wait_ge(keys_done, 1)
            flag = pe.value_load(over[0:1, 0:1], min_val=0, max_val=1)
            with pe.If(flag > 0):
                experts(1)


_INS = ["x", "norm_mix", "norm_ffn", "norm_final", "ret_w_in", "ret_gn", "ret_w_out", "s5_w_in", "s5_a_re", "s5_a_im",
        "s5_log_step", "s5_b_re", "s5_b_im", "s5_c_re", "s5_c_im", "s5_d", "s5_w_out", "ffn_w_gate", "ffn_w_up",
        "ffn_w_down", "moe_router", "moe_w_gate", "moe_w_up", "moe_w_down"]


def kernel(**inputs):
    import concourse.bacc as bacc
    from concourse.bass_utils import run_bass_kernel_spmd

    nc = bacc.Bacc("TRN2", target_bir_lowering=False, num_devices=1)
    arrays, aps = {}, {}
    for name in _INS:
        a = np.ascontiguousarray(inputs[name])
        arrays[f"in_{name}"] = a
        aps[name] = nc.dram_tensor(f"in_{name}", a.shape, F32, kind="ExternalInput").ap()
    arrays["in_constants"] = constants()
    consts = nc.dram_tensor("in_constants", (P, C_COLS), F32, kind="ExternalInput").ap()
    out = nc.dram_tensor("out", (1, SEQ, D), F32, kind="ExternalOutput").ap()
    trunk(nc, aps, consts, out)
    r = run_bass_kernel_spmd(nc, [arrays], core_ids=[0])
    return r.results[0]["out"]
```
